# Optimizing a Trainium2 kernel written in Bass

```python
import math
import jax, jax.numpy as jnp
from jax import lax
import numpy as np

D_MODEL = 1024
BATCH = 1
SEQ = 256
DEPTH = 2
DEC_BATCH = 8
DEC_SEQ = 1
PAST_LEN = 1024
PAGE_SIZE = 128

HEAD_DIM = 64
MOBA_HEADS = 8
NSA_HEADS = 8
NSA_KV_HEADS = 2
NSA_GROUP = NSA_HEADS // NSA_KV_HEADS
ATTN_HEADS = MOBA_HEADS + NSA_HEADS
MOBA_BLOCK = 256
MOBA_TOPK = 3
CMP_BLOCK = 32
CMP_HIDDEN = 2 * HEAD_DIM
SEL_BLOCK = 64
SEL_TOPK = 16
WINDOW = 512
WIN_QBLOCK = 128
Q_CHUNK = 16
NUM_BUCKETS = 32
MAX_DISTANCE = 128
S5_GROUP_CH = 16
S5_GROUPS = D_MODEL // S5_GROUP_CH
S5_STATE = 64
DT_MIN = 0.001
DT_MAX = 0.1
D_FF = 4 * D_MODEL
N_ATTN_LAYERS = (DEPTH + 1) // 2
N_SSM_LAYERS = DEPTH // 2
MOBA_W = MOBA_HEADS * HEAD_DIM
NSA_Q_W = NSA_HEADS * HEAD_DIM
NSA_KV_W = NSA_KV_HEADS * HEAD_DIM
IN_COLS = 3 * MOBA_W + NSA_Q_W + 6 * NSA_KV_W + 3 * NSA_HEADS
SCALE = HEAD_DIM ** -0.5
EPS = 1e-6

kernel_name = "moba_nsa_s5_hybrid_step"

def rms_norm(x, g):
    xf = x.astype(jnp.float32)
    y = xf * lax.rsqrt(jnp.mean(xf * xf, axis=-1, keepdims=True) + EPS)
    return (y * g.astype(jnp.float32)).astype(x.dtype)

def adaln(c, w, b):
    m = (jax.nn.silu(c) @ w + b)[:, None, :]
    return jnp.split(m, 3, axis=-1)

def modulate(x, g, shift, scale):
    return rms_norm(x, g) * (1 + scale) + shift

def rel_bucket(dist):
    n = jnp.maximum(dist, 0)
    max_exact = NUM_BUCKETS // 2
    nf = jnp.maximum(n, 1).astype(jnp.float32)
    large = max_exact + (jnp.log(nf / max_exact) / math.log(MAX_DISTANCE / max_exact)
                         * (NUM_BUCKETS - max_exact)).astype(jnp.int32)
    large = jnp.minimum(large, NUM_BUCKETS - 1)
    return jnp.where(n < max_exact, n, large)

def masked_softmax(logits, mask):
    lf = jnp.where(mask, logits.astype(jnp.float32), -jnp.inf)
    m = jnp.max(lf, axis=-1, keepdims=True)
    m = jnp.where(jnp.isfinite(m), m, 0.0)
    p = jnp.exp(lf - m)
    return p / jnp.maximum(jnp.sum(p, axis=-1, keepdims=True), 1e-30)

def map_query_chunks(fn, q_pos, *xs):
    t = q_pos.shape[0]
    c = min(Q_CHUNK, t)
    n = -(-t // c)
    pad = n * c - t
    pos = jnp.pad(q_pos, (0, pad), mode="edge").reshape(n, c)

    def split(x):
        x = jnp.pad(x, [(0, 0), (0, pad)] + [(0, 0)] * (x.ndim - 2))
        return jnp.moveaxis(x.reshape((x.shape[0], n, c) + x.shape[2:]), 1, 0)

    out = lax.map(lambda a: fn(*a), (pos,) + tuple(split(x) for x in xs))
    out = jnp.moveaxis(out, 0, 1)
    return out.reshape((out.shape[0], n * c) + out.shape[3:])[:, :t]

def attn_project(h, w_in, qk_g):
    b, t = h.shape[:2]
    z = h @ w_in
    sizes = [MOBA_W, MOBA_W, MOBA_W, NSA_Q_W] + [NSA_KV_W] * 6
    mq, mk, mv, nq, kc, vc, ks, vs, kw, vw, gl = jnp.split(z, np.cumsum(sizes).tolist(), axis=-1)
    hd = lambda a, nh: a.reshape(b, t, nh, HEAD_DIM)
    mq = rms_norm(hd(mq, MOBA_HEADS), qk_g[0])
    mk = rms_norm(hd(mk, MOBA_HEADS), qk_g[1])
    mv = hd(mv, MOBA_HEADS)
    nq = rms_norm(hd(nq, NSA_HEADS), qk_g[2])
    kc, vc = hd(kc, NSA_KV_HEADS), hd(vc, NSA_KV_HEADS)
    ks, vs = rms_norm(hd(ks, NSA_KV_HEADS), qk_g[4]), hd(vs, NSA_KV_HEADS)
    kw, vw = rms_norm(hd(kw, NSA_KV_HEADS), qk_g[5]), hd(vw, NSA_KV_HEADS)
    gates = jax.nn.sigmoid(gl.astype(jnp.float32)).astype(h.dtype).reshape(b, t, NSA_HEADS, 3)
    return mq, mk, mv, nq, kc, vc, ks, vs, kw, vw, gates

def moba_attention(q, k, v, q_pos, bias_h):
    b, L = k.shape[:2]
    nb = -(-L // MOBA_BLOCK)
    pad = ((0, 0), (0, nb * MOBA_BLOCK - L), (0, 0), (0, 0))
    kb = jnp.pad(k, pad).reshape(b, nb, MOBA_BLOCK, MOBA_HEADS, HEAD_DIM)
    vb = jnp.pad(v, pad).reshape(b, nb, MOBA_BLOCK, MOBA_HEADS, HEAD_DIM)
    k_mean = jnp.mean(kb.astype(jnp.float32), axis=2).astype(k.dtype)
    n_top = min(MOBA_TOPK, nb)
    bi = jnp.arange(b)[:, None, None, None]
    hi = jnp.arange(MOBA_HEADS)[None, :, None, None]
    offs = jnp.arange(MOBA_BLOCK, dtype=jnp.int32)

    def chunk(pc, qc):
        own = pc // MOBA_BLOCK
        gate = jnp.einsum("bqhd,bnhd->bhqn", qc, k_mean).astype(jnp.float32)
        past = jnp.arange(nb)[None, :] < own[:, None]
        gate = jnp.where(past, gate, -jnp.inf)
        top_v, top_i = lax.top_k(gate, n_top)
        own_b = jnp.broadcast_to(own[None, None, :, None], top_i.shape[:3] + (1,)).astype(top_i.dtype)
        blocks = jnp.concatenate([top_i, own_b], axis=-1)
        blk_ok = jnp.concatenate([jnp.isfinite(top_v), jnp.ones(own_b.shape, bool)], axis=-1)
        kg = kb[bi, blocks, :, hi]
        vg = vb[bi, blocks, :, hi]
        dist = pc[None, None, :, None, None] - (blocks[..., None] * MOBA_BLOCK + offs)
        mask = blk_ok[..., None] & (dist >= 0)
        bias = bias_h[hi[..., None], rel_bucket(dist)]
        logits = jnp.einsum("bqhd,bhqjsd->bhqjs", qc, kg).astype(jnp.float32) * SCALE + bias
        shp = logits.shape[:3] + (-1,)
        p = masked_softmax(logits.reshape(shp), mask.reshape(shp))
        return jnp.einsum("bhqm,bhqmd->bqhd", p.astype(v.dtype), vg.reshape(shp + (HEAD_DIM,)))

    return map_query_chunks(chunk, q_pos, q)

def nsa_compress(x, pos_emb, w1, w2):
    b, L = x.shape[:2]
    nc = L // CMP_BLOCK
    blk = x[:, :nc * CMP_BLOCK].reshape(b, nc, CMP_BLOCK, NSA_KV_HEADS, HEAD_DIM) + pos_emb[:, None, :]
    flat = blk.transpose(0, 1, 3, 2, 4).reshape(b, nc, NSA_KV_HEADS, CMP_BLOCK * HEAD_DIM)
    return jax.nn.gelu(flat @ w1) @ w2

def nsa_cmp_sel(q, kc, vc, ks, vs, q_pos, cmp_pos, cmp_w1, cmp_w2, g_kc, bias_h):
    b, tq = q.shape[:2]
    L = ks.shape[1]
    qg = q.reshape(b, tq, NSA_KV_HEADS, NSA_GROUP, HEAD_DIM)
    k_cmp = rms_norm(nsa_compress(kc, cmp_pos[0], cmp_w1[0], cmp_w2[0]), g_kc)
    v_cmp = nsa_compress(vc, cmp_pos[1], cmp_w1[1], cmp_w2[1])
    nc = k_cmp.shape[1]
    dist_c = q_pos[:, None] - ((jnp.arange(nc, dtype=jnp.int32) + 1) * CMP_BLOCK - 1)[None, :]
    bias_c = bias_h[:, rel_bucket(dist_c)].reshape(NSA_KV_HEADS, NSA_GROUP, tq, nc)
    logits_c = jnp.einsum("bqkgd,bnkd->bkgqn", qg, k_cmp).astype(jnp.float32) * SCALE + bias_c
    p_cmp = masked_softmax(logits_c, dist_c >= 0)
    o_cmp = jnp.einsum("bkgqn,bnkd->bqkgd", p_cmp.astype(vc.dtype), v_cmp).reshape(b, tq, NSA_HEADS, HEAD_DIM)
    ns = -(-L // SEL_BLOCK)
    ratio = SEL_BLOCK // CMP_BLOCK
    imp = jnp.pad(jnp.sum(p_cmp, axis=2), ((0, 0), (0, 0), (0, 0), (0, ns * ratio - nc)))
    imp = imp.reshape(b, NSA_KV_HEADS, tq, ns, ratio).sum(-1).transpose(0, 2, 1, 3)
    pad = ((0, 0), (0, ns * SEL_BLOCK - L), (0, 0), (0, 0))
    ksb = jnp.pad(ks, pad).reshape(b, ns, SEL_BLOCK, NSA_KV_HEADS, HEAD_DIM)
    vsb = jnp.pad(vs, pad).reshape(b, ns, SEL_BLOCK, NSA_KV_HEADS, HEAD_DIM)
    n_top = min(SEL_TOPK, ns)
    bi = jnp.arange(b)[:, None, None, None]
    ki = jnp.arange(NSA_KV_HEADS)[None, :, None, None]
    bias_g = bias_h.reshape(NSA_KV_HEADS, NSA_GROUP, NUM_BUCKETS)
    ki6 = jnp.arange(NSA_KV_HEADS)[None, :, None, None, None, None]
    gi6 = jnp.arange(NSA_GROUP)[None, None, :, None, None, None]
    offs = jnp.arange(SEL_BLOCK, dtype=jnp.int32)

    def chunk(pc, qc, ic):
        own = pc // SEL_BLOCK
        past = jnp.arange(ns)[None, :] < own[:, None]
        score = jnp.where(past[None, :, None, :], ic, -jnp.inf).transpose(0, 2, 1, 3)
        top_v, top_i = lax.top_k(score, n_top)
        own_b = jnp.broadcast_to(own[None, None, :, None], top_i.shape[:3] + (1,)).astype(top_i.dtype)
        blocks = jnp.concatenate([top_i, own_b], axis=-1)
        blk_ok = jnp.concatenate([jnp.isfinite(top_v), jnp.ones(own_b.shape, bool)], axis=-1)
        kg = ksb[bi, blocks, :, ki]
        vg = vsb[bi, blocks, :, ki]
        dist = pc[None, None, :, None, None] - (blocks[..., None] * SEL_BLOCK + offs)
        mask = (blk_ok[..., None] & (dist >= 0))[:, :, None]
        bias = bias_g[ki6, gi6, rel_bucket(dist)[:, :, None]]
        logits = jnp.einsum("bqkgd,bkqjsd->bkgqjs", qc, kg).astype(jnp.float32) * SCALE + bias
        p = masked_softmax(logits.reshape(logits.shape[:4] + (-1,)), mask.reshape(mask.shape[:4] + (-1,)))
        return jnp.einsum("bkgqm,bkqmd->bqkgd", p.astype(vs.dtype), vg.reshape(vg.shape[:3] + (-1, HEAD_DIM)))

    o_sel = map_query_chunks(chunk, q_pos, qg, imp).reshape(b, tq, NSA_HEADS, HEAD_DIM)
    return o_cmp, o_sel

def window_attend(q, k, v, q_pos, k_pos, bias_h):
    n, tq, tk = q.shape[1], q.shape[2], k.shape[2]
    dist = q_pos[:, :, None] - k_pos[:, None, :]
    mask = (dist >= 0) & (dist <= WINDOW) & (k_pos[:, None, :] >= 0)
    bias = bias_h[:, rel_bucket(dist)].reshape(NSA_KV_HEADS, NSA_GROUP, n, tq, tk)
    logits = jnp.einsum("bnqkgd,bntkd->bkgnqt", q, k).astype(jnp.float32) * SCALE + bias
    p = masked_softmax(logits, mask)
    return jnp.einsum("bkgnqt,bntkd->bnqkgd", p.astype(v.dtype), v)

def window_prompt(q, k, v, bias_h):
    b, s = q.shape[:2]
    nqb = s // WIN_QBLOCK
    idx = jnp.arange(nqb, dtype=jnp.int32)[:, None] * WIN_QBLOCK + jnp.arange(WINDOW + WIN_QBLOCK, dtype=jnp.int32)[None, :]
    pad = ((0, 0), (WINDOW, 0), (0, 0), (0, 0))
    kb = jnp.pad(k, pad)[:, idx]
    vb = jnp.pad(v, pad)[:, idx]
    qb = q.reshape(b, nqb, WIN_QBLOCK, NSA_KV_HEADS, NSA_GROUP, HEAD_DIM)
    q_pos = jnp.arange(s, dtype=jnp.int32).reshape(nqb, WIN_QBLOCK)
    out = window_attend(qb, kb, vb, q_pos, idx - WINDOW, bias_h)
    return out.reshape(b, s, NSA_HEADS, HEAD_DIM)

def attn_core(mq, nq, gates, mk, mv, kc, vc, ks, vs, o_win, q_pos, cmp_pos, cmp_w1, cmp_w2, g_kc, bias_moba, bias_nsa):
    o_moba = moba_attention(mq, mk, mv, q_pos, bias_moba)
    o_cmp, o_sel = nsa_cmp_sel(nq, kc, vc, ks, vs, q_pos, cmp_pos, cmp_w1, cmp_w2, g_kc, bias_nsa)
    o_nsa = gates[..., 0:1] * o_cmp + gates[..., 1:2] * o_sel + gates[..., 2:3] * o_win
    b, t = mq.shape[:2]
    return jnp.concatenate([o_moba, o_nsa], axis=2).reshape(b, t, ATTN_HEADS * HEAD_DIM)

def _complex_affine_combine(e1, e2):
    a1r, a1i, b1r, b1i = e1
    a2r, a2i, b2r, b2i = e2
    return (a2r * a1r - a2i * a1i, a2r * a1i + a2i * a1r,
            a2r * b1r - a2i * b1i + b2r, a2r * b1i + a2i * b1r + b2i)

def s5_mixer(u, h0, a_re, a_im, log_dt, b_re, b_im, c_re, c_im, d_skip, w_glu):
    f32 = jnp.float32
    bsz, t, d = u.shape
    a_re, a_im = a_re.astype(f32), a_im.astype(f32)
    dt = jnp.exp(log_dt.astype(f32))[:, None]
    decay = jnp.exp(dt * a_re)
    ab_re, ab_im = decay * jnp.cos(dt * a_im), decay * jnp.sin(dt * a_im)
    den = a_re * a_re + a_im * a_im
    f_re = ((ab_re - 1) * a_re + ab_im * a_im) / den
    f_im = (ab_im * a_re - (ab_re - 1) * a_im) / den
    br, bim = b_re.astype(f32), b_im.astype(f32)
    bb_re = f_re[..., None] * br - f_im[..., None] * bim
    bb_im = f_re[..., None] * bim + f_im[..., None] * br
    uf = u.astype(f32)
    ug = uf.reshape(bsz, t, S5_GROUPS, S5_GROUP_CH)
    bu_re = jnp.einsum("btgc,gnc->tbgn", ug, bb_re)
    bu_im = jnp.einsum("btgc,gnc->tbgn", ug, bb_im)
    h_re, h_im = h0[:, 0].astype(f32), h0[:, 1].astype(f32)
    bu_re = bu_re.at[0].add(ab_re * h_re - ab_im * h_im)
    bu_im = bu_im.at[0].add(ab_re * h_im + ab_im * h_re)
    a_seq_re = jnp.broadcast_to(ab_re, (t, 1) + ab_re.shape)
    a_seq_im = jnp.broadcast_to(ab_im, (t, 1) + ab_im.shape)
    _, _, x_re, x_im = lax.associative_scan(_complex_affine_combine, (a_seq_re, a_seq_im, bu_re, bu_im), axis=0)
    y = (jnp.einsum("tbgn,gcn->btgc", x_re, c_re.astype(f32))
         - jnp.einsum("tbgn,gcn->btgc", x_im, c_im.astype(f32)))
    y = y.reshape(bsz, t, d) + d_skip.astype(f32) * uf
    z = jax.nn.gelu(y) @ w_glu.astype(f32)
    out = z[..., :d] * jax.nn.sigmoid(z[..., d:])
    new_state = jnp.stack([x_re[-1], x_im[-1]], axis=1)
    return out.astype(u.dtype), new_state.astype(h0.dtype)

def mlp_sublayer(x, c, g, ada_w, ada_b, w1, w2):
    shift, scale, gate = adaln(c, ada_w, ada_b)
    h = modulate(x, g, shift, scale)
    return x + gate * (jnp.square(jax.nn.relu(h @ w1)) @ w2)

def setup_inputs(seed: int = 0) -> dict:
    key = jax.random.key(seed)
    keys = list(jax.random.split(key, 48))

    def normal(shape, scale=1.0):
        r = jax.random.normal(keys.pop(), shape, jnp.float32)
        return r if scale == 1.0 else scale * r

    def gain(shape):
        return 1.0 + normal(shape, 0.02)

    d = D_MODEL
    na, nsl = N_ATTN_LAYERS, N_SSM_LAYERS
    n_pages = PAST_LEN // PAGE_SIZE
    n_pool = (DEC_BATCH * n_pages * 5) // 4
    w_eff = min(WINDOW, PAST_LEN)
    page_table = jax.random.permutation(keys.pop(), n_pool)[: DEC_BATCH * n_pages].reshape(DEC_BATCH, n_pages).astype(jnp.int32)
    a_im0 = math.pi * jnp.arange(S5_STATE, dtype=jnp.float32)
    return {
        "x_prompt": normal((BATCH, SEQ, d)),
        "x_sample": normal((DEC_BATCH, DEC_SEQ, d)),
        "cache_moba_kv": normal((na, n_pool, PAGE_SIZE, 2, MOBA_HEADS, HEAD_DIM)),
        "cache_nsa_kv": normal((na, n_pool, PAGE_SIZE, 4, NSA_KV_HEADS, HEAD_DIM)),
        "state_nsa_win": normal((na, DEC_BATCH, w_eff, 2, NSA_KV_HEADS, HEAD_DIM)),
        "state_s5": normal((nsl, DEC_BATCH, 2, S5_GROUPS, S5_STATE), 0.5),
        "page_table": page_table,
        "c_prompt": normal((BATCH, d)),
        "c_sample": normal((DEC_BATCH, d)),
        "rel_bias": normal((NUM_BUCKETS, ATTN_HEADS), 0.2),
        "attn_norm_g": gain((na, d)),
        "attn_ada_w": normal((na, d, 3 * d), 0.5 * d ** -0.5),
        "attn_ada_b": normal((na, 3 * d), 0.02),
        "attn_w_in": normal((na, d, IN_COLS), d ** -0.5),
        "attn_qk_g": gain((na, 6, HEAD_DIM)),
        "nsa_cmp_pos": normal((na, 2, CMP_BLOCK, HEAD_DIM), 0.1),
        "nsa_cmp_w1": normal((na, 2, CMP_BLOCK * HEAD_DIM, CMP_HIDDEN), (CMP_BLOCK * HEAD_DIM) ** -0.5),
        "nsa_cmp_w2": normal((na, 2, CMP_HIDDEN, HEAD_DIM), CMP_HIDDEN ** -0.5),
        "attn_w_out": normal((na, ATTN_HEADS * HEAD_DIM, d), (ATTN_HEADS * HEAD_DIM) ** -0.5),
        "ssm_norm_g": gain((nsl, d)),
        "ssm_ada_w": normal((nsl, d, 3 * d), 0.5 * d ** -0.5),
        "ssm_ada_b": normal((nsl, 3 * d), 0.02),
        "s5_a_re": -0.5 + normal((nsl, S5_GROUPS, S5_STATE), 0.01),
        "s5_a_im": a_im0 + normal((nsl, S5_GROUPS, S5_STATE), 0.01),
        "s5_log_dt": jax.random.uniform(keys.pop(), (nsl, S5_GROUPS), jnp.float32, math.log(DT_MIN), math.log(DT_MAX)),
        "s5_b_re": normal((nsl, S5_GROUPS, S5_STATE, S5_GROUP_CH), (2 * S5_GROUP_CH) ** -0.5),
        "s5_b_im": normal((nsl, S5_GROUPS, S5_STATE, S5_GROUP_CH), (2 * S5_GROUP_CH) ** -0.5),
        "s5_c_re": normal((nsl, S5_GROUPS, S5_GROUP_CH, S5_STATE), S5_STATE ** -0.5),
        "s5_c_im": normal((nsl, S5_GROUPS, S5_GROUP_CH, S5_STATE), S5_STATE ** -0.5),
        "s5_d": normal((nsl, d)),
        "s5_w_glu": normal((nsl, d, 2 * d), d ** -0.5),
        "mlp_norm_g": gain((DEPTH, d)),
        "mlp_ada_w": normal((DEPTH, d, 3 * d), 0.5 * d ** -0.5),
        "mlp_ada_b": normal((DEPTH, 3 * d), 0.02),
        "mlp_w1": normal((DEPTH, d, D_FF), d ** -0.5),
        "mlp_w2": normal((DEPTH, D_FF, d), D_FF ** -0.5),
    }

def reference(x_prompt, x_sample, cache_moba_kv, cache_nsa_kv, state_nsa_win, state_s5, page_table,
              c_prompt, c_sample, rel_bias, attn_norm_g, attn_ada_w, attn_ada_b, attn_w_in, attn_qk_g,
              nsa_cmp_pos, nsa_cmp_w1, nsa_cmp_w2, attn_w_out, ssm_norm_g, ssm_ada_w, ssm_ada_b,
              s5_a_re, s5_a_im, s5_log_dt, s5_b_re, s5_b_im, s5_c_re, s5_c_im, s5_d, s5_w_glu,
              mlp_norm_g, mlp_ada_w, mlp_ada_b, mlp_w1, mlp_w2):
    bias_t = rel_bias.T
    bias_moba, bias_nsa = bias_t[:MOBA_HEADS], bias_t[MOBA_HEADS:]
    bp, seq = x_prompt.shape[:2]
    bs, dec_seq = x_sample.shape[:2]
    pos_p = jnp.arange(seq, dtype=jnp.int32)
    pos_s = PAST_LEN + jnp.arange(dec_seq, dtype=jnp.int32)
    xp, xs = x_prompt, x_sample
    moba_p, moba_s, nsa_p, nsa_s, win_p, win_s, s5_p, s5_s = [], [], [], [], [], [], [], []
    cat = lambda a, b: jnp.concatenate([a, b], axis=1)
    for layer in range(DEPTH):
        if layer % 2 == 0:
            ia = layer // 2
            cmp_args = (nsa_cmp_pos[ia], nsa_cmp_w1[ia], nsa_cmp_w2[ia], attn_qk_g[ia, 3], bias_moba, bias_nsa)
            shift, scale, gate = adaln(c_prompt, attn_ada_w[ia], attn_ada_b[ia])
            h = modulate(xp, attn_norm_g[ia], shift, scale)
            mq, mk, mv, nq, kc, vc, ks, vs, kw, vw, gt = attn_project(h, attn_w_in[ia], attn_qk_g[ia])
            o_win = window_prompt(nq, kw, vw, bias_nsa)
            o = attn_core(mq, nq, gt, mk, mv, kc, vc, ks, vs, o_win, pos_p, *cmp_args)
            xp = xp + gate * (o @ attn_w_out[ia])
            moba_p.append(jnp.stack([mk, mv], axis=2).reshape(bp, seq // PAGE_SIZE, PAGE_SIZE, 2, MOBA_HEADS, HEAD_DIM))
            nsa_p.append(jnp.stack([kc, vc, ks, vs], axis=2).reshape(bp, seq // PAGE_SIZE, PAGE_SIZE, 4, NSA_KV_HEADS, HEAD_DIM))
            win_p.append(jnp.stack([kw, vw], axis=2)[:, seq - min(WINDOW, seq):])
            shift, scale, gate = adaln(c_sample, attn_ada_w[ia], attn_ada_b[ia])
            h = modulate(xs, attn_norm_g[ia], shift, scale)
            mq, mk, mv, nq, kc, vc, ks, vs, kw, vw, gt = attn_project(h, attn_w_in[ia], attn_qk_g[ia])
            past_m = cache_moba_kv[ia, page_table].reshape(bs, -1, 2, MOBA_HEADS, HEAD_DIM)
            past_n = cache_nsa_kv[ia, page_table].reshape(bs, -1, 4, NSA_KV_HEADS, HEAD_DIM)
            win = state_nsa_win[ia]
            w_eff = win.shape[1]
            kw_all, vw_all = cat(win[:, :, 0], kw), cat(win[:, :, 1], vw)
            kpos_w = (PAST_LEN - w_eff + jnp.arange(w_eff + dec_seq, dtype=jnp.int32))[None]
            o_win = window_attend(nq.reshape(bs, 1, dec_seq, NSA_KV_HEADS, NSA_GROUP, HEAD_DIM),
                                  kw_all[:, None], vw_all[:, None], pos_s[None], kpos_w,
                                  bias_nsa).reshape(bs, dec_seq, NSA_HEADS, HEAD_DIM)
            o = attn_core(mq, nq, gt, cat(past_m[:, :, 0], mk), cat(past_m[:, :, 1], mv),
                          cat(past_n[:, :, 0], kc), cat(past_n[:, :, 1], vc),
                          cat(past_n[:, :, 2], ks), cat(past_n[:, :, 3], vs), o_win, pos_s, *cmp_args)
            xs = xs + gate * (o @ attn_w_out[ia])
            moba_s.append(jnp.stack([mk, mv], axis=2))
            nsa_s.append(jnp.stack([kc, vc, ks, vs], axis=2))
            win_s.append(jnp.stack([kw_all, vw_all], axis=2)[:, dec_seq:])
        else:
            isx = layer // 2
            s5_args = (s5_a_re[isx], s5_a_im[isx], s5_log_dt[isx], s5_b_re[isx], s5_b_im[isx],
                       s5_c_re[isx], s5_c_im[isx], s5_d[isx], s5_w_glu[isx])
            shift, scale, gate = adaln(c_prompt, ssm_ada_w[isx], ssm_ada_b[isx])
            h = modulate(xp, ssm_norm_g[isx], shift, scale)
            y, st = s5_mixer(h, jnp.zeros((bp, 2, S5_GROUPS, S5_STATE), h.dtype), *s5_args)
            xp = xp + gate * y
            s5_p.append(st)
            shift, scale, gate = adaln(c_sample, ssm_ada_w[isx], ssm_ada_b[isx])
            h = modulate(xs, ssm_norm_g[isx], shift, scale)
            y, st = s5_mixer(h, state_s5[isx], *s5_args)
            xs = xs + gate * y
            s5_s.append(st)
        xp = mlp_sublayer(xp, c_prompt, mlp_norm_g[layer], mlp_ada_w[layer], mlp_ada_b[layer], mlp_w1[layer], mlp_w2[layer])
        xs = mlp_sublayer(xs, c_sample, mlp_norm_g[layer], mlp_ada_w[layer], mlp_ada_b[layer], mlp_w1[layer], mlp_w2[layer])
    return (xp, xs, jnp.stack(moba_p), jnp.stack(moba_s), jnp.stack(nsa_p), jnp.stack(nsa_s),
            jnp.stack(win_p), jnp.stack(win_s), jnp.stack(s5_p), jnp.stack(s5_s))


_drawn_inputs = setup_inputs


def setup_inputs(seed=0):
    import zlib

    import numpy as np

    out = dict(_drawn_inputs(seed))
    spreads = {}
    factors = {'cache_moba_kv': 4.613,
     'cache_nsa_kv': 2.98,
     'rel_bias': 4.775,
     'attn_norm_g': 2.881,
     'attn_qk_g': 4.481,
     'nsa_cmp_pos': 7.307,
     'ssm_norm_g': 3.201,
     's5_a_re': 13.462,
     'mlp_norm_g': 4.543,
     'ssm_ada_b': 2.762,
     's5_c_re': 6.915,
     's5_c_im': 6.799}
    for name, (base, spread) in spreads.items():
        noise = np.random.default_rng([zlib.crc32(name.encode()), seed]).standard_normal(out[name].shape)
        drawn = base * np.exp(spread * noise) if base else spread * noise
        out[name] = __import__('jax').numpy.asarray(drawn.astype(out[name].dtype))
    for name, factor in factors.items():
        out[name] = (out[name] * factor).astype(out[name].dtype)
    return out
```

```python
from contextlib import ExitStack

import concourse.bass as bass
from concourse import mybir

F32 = mybir.dt.float32
I32 = mybir.dt.int32
ALU = mybir.AluOpType
ACT = mybir.ActivationFunctionType
AX = mybir.AxisListType.X
DS = bass.DynSlice

P = 128
D = 1024
KC = D // P
TP, TS = 256, 8
T = TP + TS
PAST, PAGE = 1024, 128
PAGES = PAST // PAGE
POOL = 80
HD = 64
MOBA_H, NSA_H, KVH, GRP = 8, 8, 2, 4
IN_COLS = 2840
MQ, MK, MV, NQ, KCMP, VCMP, KSEL, VSEL, KWIN, VWIN, GATE = 0, 512, 1024, 1536, 2048, 2176, 2304, 2432, 2560, 2688, 2816
SCALE = HD ** -0.5
EPS = 1e-6
NEG = -1e30
FF = 4 * D
NBUCKET = 32
CMP = 32
SEG = 128
NT = 32
ARENA = 28670
SMALL, S5_LOADS = 15, 12
OH_TZ, OH_PG, OH_CS, OH_OWN, OH_CP, OH_ALL = 0, 384, 1408, 1536, 1544, 3592
C_ID, C_MB, C_G, C_DM, C_AM, C_NI, C_MC, C_OM, C_GT, C_ALL = 0, 128, 130, 138, 146, 150, 154, 162, 226, 290
TWO_PI_A, TWO_PI_B, TWO_PI_C = 6.28125, 0.0019350051879882812, 3.019916050561733e-07
ROUND = 12582912.0


def at(ap, *dims):
    return bass.AP(tensor=ap.tensor, offset=ap.offset, ap=[list(ap.ap[0])] + [list(d) for d in dims])


SLOTS = 4
SEQ = dict(ada0=0, cmp=6, w_in=8, cmp_p=14, ada1=16, ada2=22, ada3=28, w_out=34, w1_0=36, w2_0=44, glu=52, w1_1=56, w2_1=64)


def panel_full(seq):
    return sum(32 if SEQ["glu"] <= n < SEQ["glu"] + 4 else 16 for n in range(seq % SLOTS, seq + 1, SLOTS))


KVS = 8
KV_CMP, KV_MK, KV_MV, KV_SK, KV_WK, KV_SV, KV_WV, KV_END = 0, 32, 96, 160, 176, 184, 200, 208


def kv_full_value(seq):
    total = 0
    for n in range(seq % KVS, seq + 1, KVS):
        total += 32 if n < KV_MK else 64 if KV_SK <= n < KV_WK or KV_SV <= n < KV_WV else 16
    return total


class Signals:

    def __init__(self, sem):
        self.small_loaded = sem("small_loaded")
        self.x_loaded = sem("x_loaded")
        self.pt_loaded = sem("pt_loaded")
        self.s5_rows_loaded = sem("s5_rows_loaded")
        self.s5_loaded = sem("s5_loaded")
        self.ones_made = sem("ones_made")
        self.tz_stored = sem("tz_stored")
        self.bias_back = sem("bias_back")
        self.mm_done = sem("mm_done")
        self.small_tr = sem("small_tr")
        self.small_ev = sem("small_ev")
        self.bias_mm = sem("bias_mm")
        self.bias_ev = sem("bias_ev")
        self.csil_ready = sem("csil_ready")
        self.c_tr = sem("c_tr")
        self.c_ev = sem("c_ev")
        self.x_tr = sem("x_tr")
        self.x_ev = sem("x_ev")
        self.sq_ready = sem("sq_ready")
        self.ssq_ready = sem("ssq_ready")
        self.rt_ready = sem("rt_ready")
        self.h_mul = sem("h_mul")
        self.h_ready = sem("h_ready")
        self.hs_ready = sem("hs_ready")
        self.mods_ready = sem("mods_ready")
        self.x_ready = sem("x_ready")
        self.z_ev = sem("z_ev")
        self.zs_ss = sem("zs_ss")
        self.zs_std = sem("zs_std")
        self.zs_normed = sem("zs_normed")
        self.z_ss = sem("z_ss")
        self.z_std = sem("z_std")
        self.z_normed = sem("z_normed")
        self.gates_ready = sem("gates_ready")
        self.z_stored = sem("z_stored")
        self.q_bc = sem("q_bc")
        self.q_bc_ev = sem("q_bc_ev")
        self.qk_tr = sem("qk_tr")
        self.qk_ev = sem("qk_ev")
        self.scored = sem("scored")
        self.moba_scored = sem("moba_scored")
        self.zdup_ready = sem("zdup_ready")
        self.cmp_tr = sem("cmp_tr")
        self.cmp_ev = sem("cmp_ev")
        self.gelu_ev = sem("gelu_ev")
        self.pb_mm = sem("pb_mm")
        self.pb_ev = sem("pb_ev")
        self.cmp2_mm = sem("cmp2_mm")
        self.kc_ss = sem("kc_ss")
        self.kc_std = sem("kc_std")
        self.kdup_ready = sem("kdup_ready")
        self.kcp_tr = sem("kcp_tr")
        self.kcp_ev = sem("kcp_ev")
        self.gate_sum = sem("gate_sum")
        self.mx_in = sem("mx_in")
        self.mx_tr = sem("mx_tr")
        self.mx_diag = sem("mx_diag")
        self.mx_bc = sem("mx_bc")
        self.log_ready = sem("log_ready")
        self.p_exp = sem("p_exp")
        self.p_ready = sem("p_ready")
        self.l_done = sem("l_done")
        self.pv_done = sem("pv_done")
        self.osum_ready = sem("osum_ready")
        self.osum_mm = sem("osum_mm")
        self.oTs_ready = sem("oTs_ready")
        self.cp_mm = sem("cp_mm")
        self.cp_log = sem("cp_log")
        self.cp_exp = sem("cp_exp")
        self.cp_ready = sem("cp_ready")
        self.cp_tr = sem("cp_tr")
        self.cp_tev = sem("cp_tev")
        self.pr_s = sem("pr_s")
        self.pr_log = sem("pr_log")
        self.pr_exp = sem("pr_exp")
        self.pr_p = sem("pr_p")
        self.pr_tr = sem("pr_tr")
        self.pr_tev = sem("pr_tev")
        self.pr_pv = sem("pr_pv")
        self.pr_oev = sem("pr_oev")
        self.relu_ev = sem("relu_ev")
        self.act_ready = sem("act_ready")
        self.out_free = sem("out_free")
        self.sig_ready = sem("sig_ready")
        self.dve_step = sem("dve_step")
        self.act_step = sem("act_step")
        self.s5_rows_made = sem("s5_rows_made")
        self.s5_rows_tr = sem("s5_rows_tr")
        self.s5_rows_ev = sem("s5_rows_ev")
        self.s5_dt = sem("s5_dt")
        self.s5_ang = sem("s5_ang")
        self.s5_sin = sem("s5_sin")
        self.s5_bd = sem("s5_bd")
        self.s5_b_tr = sem("s5_b_tr")
        self.s5_b_ev = sem("s5_b_ev")
        self.s5_c_tr = sem("s5_c_tr")
        self.s5_c_ev = sem("s5_c_ev")
        self.s5_tables = sem("s5_tables")
        self.u_mm = sem("u_mm")
        self.u_free = sem("u_free")
        self.zc_ready = sem("zc_ready")
        self.zp_done = sem("zp_done")
        self.y_mm = sem("y_mm")
        self.y_ev = sem("y_ev")
        self.gelu_ready = sem("gelu_ready")
        self.us_mm = sem("us_mm")
        self.xs_ready = sem("xs_ready")
        self.ys_mm = sem("ys_mm")
        self.fin_ready = sem("fin_ready")
        self.fin_tr = sem("fin_tr")
        self.fin_ev = sem("fin_ev")
        self.y_tr = sem("y_tr")
        self.y_out_ev = sem("y_out_ev")
        self.y_stored = sem("y_stored")
        self.r_ready = sem("r_ready")
        self.ada_row = sem("ada_row")
        self.ada_tr = sem("ada_tr")
        self.c_loaded = sem("c_loaded")
        self.win_stored = sem("win_stored")
        self.cmp_mm = sem("cmp_mm")
        self.cw_made = sem("cw_made")


def program(nc, I, O):
    scratch = nc.dram_tensor("toeplitz_rows", [16, 384], F32).ap()
    with ExitStack() as ctx:
        def sb(name, shape, dt=F32):
            return ctx.enter_context(nc.sbuf_tensor("sb_" + name, shape, dt))

        def sem(name):
            return ctx.enter_context(nc.semaphore(name))

        xT = sb("xT", [P, KC, T])
        hT = sb("hT", [P, KC, T])
        sq = sb("sq", [P, KC, T])
        ring = sb("ring", [P, SLOTS, 4096])
        ones = sb("ones", [P, P])
        cst = sb("cst", [P, C_ALL])
        mods = sb("mods", [P, 4, 24, 9])
        vT = sb("vT", [P, 136])
        cT = sb("cT", [P, KC, 9])
        ident = cst[:, C_ID:C_ID + 128]
        arena = sb("arena", [P, ARENA])
        pt = sb("pt", [1, 64], I32)

        used = [0]

        def take(n, rows=P):
            a = arena[0:rows, used[0]:used[0] + n]
            used[0] += n
            return a

        z = take(2 * IN_COLS).rearrange("p (t c) -> p t c", t=2)
        zs = take(IN_COLS, TS)
        kv = take(KVS * 512).rearrange("p (s c) -> p s c", s=KVS)
        pbuf = take(2304)
        qb = take(8 * 512).rearrange("p (b c) -> p b c", b=8)
        bias = take(8 * 256).rearrange("p (h k) -> p h k", h=8)
        kvc = take(512)
        qkT = take(2048)
        qkg = take(384).rearrange("p (i d) -> p i d", i=6)
        spt = take(1536)
        biasP, biasC, biasO, biasCP = take(128), take(8), take(16, 8), take(128)
        s_win, own = take(256), take(192, 8)
        m1, mx, diag, lsum, lrec = take(64), take(1, 64), take(64, 64), take(64), take(1, 64)
        gcol, gtmp = take(3, 64), take(24, 64)
        ss, sss, gates, gates_s = take(56), take(28, 8), take(48), take(24, 8)
        posT, pbias, w2c = take(32), take(2), take(128)
        kvp, kpd, kcTp, s_cs, s_cp = take(256, 8), take(256, 8), take(16), take(64), take(128)
        nmin, lrow, wrow = take(8), take(8), take(8)
        ssc, cw, m16, l16, s4 = take(8), take(16), take(16), take(16), take(256, 8)
        pcT = take(512, 8)
        assert used[0] <= ARENA, used[0]
        onehot = arena[0:33, 0:OH_ALL]
        xrow = [qb[:, 0:2, :].rearrange("p b c -> p (b c)"), qb[:, 2:4, :].rearrange("p b c -> p (b c)"),
                qb[0:TS, 4:6, :].rearrange("p b c -> p (b c)")]
        rel = qb[0:33, 6, 0:16]
        crow, csil = pbuf[0:9, 0:1024], pbuf[0:9, 1024:2048]
        vecA, vecB = pbuf[0:120, 2048:2176], pbuf[0:16, 2176:2304]
        posrow, tz = qkT[0:32, 0:128], qkT[0:16, 128:512]
        sqf = sq[:, :, :].rearrange("p k t -> p (k t)")
        prod, s_raw, s_log = sqf[:, 0:1024], sqf[:, 1024:1536], sqf[:, 1536:2048]
        hg = spt[:, 0:1056]
        pairs = arena[:, 0:8192]
        p_pairs = pbuf[:, 0:512]
        sp_, pT = spt[:, 0:768], spt[:, 768:1536]
        sps, pTs = (sp_, z[:, 0, 0:768]), (pT, z[:, 1, 0:768])
        otmp, oacc, obr = z[0:64, 1, 768:896], z[0:64, 0, MV:MV + 512], z[0:64, 1, MV:MV + 512]
        zdup = spt[:, 0:1024].rearrange("p (t s h c) -> p t s h c", t=2, s=2, h=2)
        used[0] = 0
        actT = take(32 * T).rearrange("p (f t) -> p f t", f=32)
        cosT = take(NT * SEG).rearrange("p (q t) -> p q t", q=NT)
        sinT = take(NT * SEG).rearrange("p (q t) -> p q t", q=NT)
        BT = take(2048).rearrange("p (k r n) -> p k r n", k=8, r=2)
        CT = take(3072).rearrange("p (i k c) -> p i k c", i=3, k=8)
        h0 = take(512).rearrange("p (b r q) -> p b r q", b=8, r=2)
        xs5 = take(512).rearrange("p (b r q) -> p b r q", b=8, r=2)
        st = take(24 * 32).rearrange("p (i q) -> p i q", i=24)
        tail5 = take(ARENA - used[0])
        yT = actT[:, 0:8, :]
        braw = tail5[:, 0:1024].rearrange("p (r q c) -> p r q c", r=2, q=NT)
        bbar = tail5[:, 1024:2048].rearrange("p (r q c) -> p r q c", r=2, q=NT)
        bdia = tail5[:, 2048:4096].rearrange("p (r q j c) -> p r q j c", r=2, q=NT, j=2)
        s5row = tail5[0:32, 4096:4480].rearrange("p (i c) -> p i c", i=3)
        hrow = tail5[:, 4480:4992].rearrange("p (a c) -> p a c", a=4)
        s5dt = tail5[0:32, 4992:4994]
        craw = CT.rearrange("p i k c -> p (i k c)")[:, 0:2048].rearrange("p (r k j n) -> p r k j n", r=2, k=8, j=2)
        dbl = tail5[:, 0:4096].rearrange("p (i q t) -> p i q t", i=2, q=NT)
        t1, t2, zin = tail5[:, 0:512], tail5[:, 512:1024], tail5[:, 1024:1536]
        zcur = tail5[:, 1536:2560].rearrange("p (i c) -> p i c", i=2)
        pc5 = tail5[:, 2560:3584].rearrange("p (i c) -> p i c", i=2)
        ps5 = tail5[:, 3584:4608].rearrange("p (i c) -> p i c", i=2)
        zlast, zinit, xlast = tail5[:, 4608:4672], tail5[:, 4672:4736], tail5[:, 4736:4800]
        t5s = tail5[:, 4800:5056]
        finrow = arena[:, 3200:3840].rearrange("p (i c) -> p i c", i=5)
        yrow = arena[:, 8448:8448 + 3072].rearrange("p (t c) -> p t c", t=3)
        sig = arena[:, 2112:2112 + 2 * T].rearrange("p (i t) -> p i t", i=2)
        glu = arena[:, 2640:2640 + 2 * T].rearrange("p (i t) -> p i t", i=2)

        psum = ctx.enter_context(nc.psum_tensor("psum", [P, 8, 512], F32))
        bank = [psum[:, i, :] for i in range(8)]

        N = Signals(sem)
        ring_full = [sem(f"ring_full{i}") for i in range(SLOTS)]
        kv_full = [sem(f"kv_full{i}") for i in range(KVS)]
        kv_odd = [sem(f"kv_odd{i}") for i in range(KVS)]
        kv_free = [sem(f"kv_free{i}") for i in range(KVS)]

        block = ctx.enter_context(nc.Block())

        def cmp_piece(page, u, g, e):
            return (kv[64 * g:64 * g + 64, u, :].rearrange("p (x e d) -> p x e d", x=4, e=2)[:, :, e],
                    I["cache_nsa_kv"][0].rearrange("n (q e) a h d -> n q e (a h d)", e=2)[page, :, e, 0:256].rearrange(
                        "n q (x d) -> (n q) x d", d=HD))

        @block.sync
        def _(sp):
            sp.dma_start(pt[:], I["page_table"].rearrange("b (o p) -> o (b p)", o=1)).then_inc(N.pt_loaded, 16)
            sp.dma_start(crow[0:1, :], I["c_prompt"]).then_inc(N.c_loaded, 16)
            sp.dma_start(crow[1:9, :], I["c_sample"]).then_inc(N.c_loaded, 16)
            small = [
                (cst[:], I["c_cst"]), (onehot, I["c_onehot"]), (rel[0:32, :], I["rel_bias"]), (rel[32:33, :], I["c_one"]),
                (vecA[0:24, :], I["attn_ada_b"].rearrange("a (r c) -> (a r) c", c=P)),
                (vecA[24:48, :], I["mlp_ada_b"][0].rearrange("(r c) -> r c", c=P)),
                (vecA[48:72, :], I["ssm_ada_b"].rearrange("a (r c) -> (a r) c", c=P)),
                (vecA[72:96, :], I["mlp_ada_b"][1].rearrange("(r c) -> r c", c=P)),
                (vecA[96:104, :], I["attn_norm_g"].rearrange("a (r c) -> (a r) c", c=P)),
                (vecA[104:112, :], I["ssm_norm_g"].rearrange("a (r c) -> (a r) c", c=P)),
                (vecA[112:120, :], I["s5_d"].rearrange("a (r c) -> (a r) c", c=P)),
                (vecB, I["mlp_norm_g"].rearrange("a (r c) -> (a r) c", c=P)),
                (posrow, I["nsa_cmp_pos"][0].rearrange("a (i e) d -> (a i) (e d)", e=2)),
                (w2c.rearrange("p (a d) -> p a d", a=2), I["nsa_cmp_w2"][0].rearrange("a h d -> h a d")),
                (qkg, I["attn_qk_g"][0].partition_broadcast(P)),
            ]
            assert len(small) == SMALL
            for dst, src in small:
                sp.dma_start(dst, src).then_inc(N.small_loaded, 16)
            for t in range(2):
                sp.dma_start(xrow[t], I["x_prompt"][0, t * P:(t + 1) * P, :]).then_inc(N.x_loaded, 16)
            sp.dma_start(xrow[2], I["x_sample"].rearrange("b t d -> (b t) d")).then_inc(N.x_loaded, 16)
            sp.wait_ge(N.bias_ev, 1)
            sp.dma_start(scratch, tz).then_inc(N.tz_stored, 16)
            sp.wait_ge(N.tz_stored, 16)
            toeplitz = [bass.AP(tensor=scratch.tensor, offset=h0_ * 384, ap=[[1, P], [384, 8], [1, 256]])
                        for h0_ in (0, 8)]
            sp.dma_start(bias, toeplitz[0]).then_inc(N.bias_back, 16)
            sp.wait_ge(N.pt_loaded, 16)
            moba = I["cache_moba_kv"][0].rearrange("n p a h d -> n p (a h d)")
            nsa = I["cache_nsa_kv"][0].rearrange("n p a h d -> n p (a h d)")

            def page(i):
                return DS(sp.value_load(pt[0:1, DS(i, 1)], min_val=0, max_val=POOL - 1), 1)

            def moba_units(first, col):
                with sp.Fori(0, TS) as b:
                    for pg in range(PAGES):
                        sp.wait_ge(kv_free[pg], b + first // KVS + 1)
                        sp.dma_start(kv[:, pg, :], moba[page(b * 8 + pg), :, col:col + 512].rearrange("n p c -> (n p) c")
                                     ).then_inc(kv_full[pg], 16)

            def nsa_units(first, col):
                with sp.Fori(0, 2) as r:
                    for u in range(KVS):
                        sp.wait_ge(kv_free[u], r + first // KVS + 1)
                        for g in range(4):
                            sp.dma_start(kv[:, u, g * P:(g + 1) * P],
                                         nsa[page(r * 32 + u * 4 + g), :, col:col + P].rearrange("n p c -> (n p) c")
                                         ).then_inc(kv_full[u], 16)

            def window_units(first, which):
                for b in range(TS):
                    sp.wait_ge(kv_free[b], first // KVS + 1)
                    sp.dma_start(kv[:, b, :].rearrange("p (t c) -> p t c", t=4),
                                 I["state_nsa_win"][0, b, :, which].rearrange("(t p) k d -> p t (k d)", p=P)
                                 ).then_inc(kv_full[b], 16)

            with sp.Fori(0, 4) as r:
                for u in range(KVS):
                    sp.wait_ge(kv_free[u], r + 1)
                    for g in range(2):
                        sp.dma_start(*cmp_piece(page(r * 16 + u * 2 + g), u, g, 0)).then_inc(kv_full[u], 16)
            moba_units(KV_MK, 0)
            moba_units(KV_MV, 512)
            sp.wait_ge(N.pr_log, 4)
            sp.dma_start(bias, toeplitz[1]).then_inc(N.bias_back, 16)
            nsa_units(KV_SK, 256)
            window_units(KV_WK, 0)
            nsa_units(KV_SV, 384)
            window_units(KV_WV, 1)
            sp.wait_ge(N.x_ready, 1)
            sp.wait_ge(N.z_stored, 16 * 6)
            loads = [
                (s5row[:, 0, :], I["s5_a_re"][0].rearrange("(q j) n -> q (j n)", j=2)),
                (s5row[:, 1, :], I["s5_a_im"][0].rearrange("(q j) n -> q (j n)", j=2)),
                (s5dt, I["s5_log_dt"][0].rearrange("(q j) -> q j", j=2)),
                (hrow, I["state_s5"][0].rearrange("(a b) r (q j) n -> (b r q) a (j n)", b=2, j=2)),
            ]
            for i, name in enumerate(("s5_b_re", "s5_b_im")):
                for j in range(2):
                    loads.append((braw[64 * j:64 * j + 64, i], I[name][0].rearrange("(q j) n c -> j n q c", j=2)[j]))
            for i, name in enumerate(("s5_c_re", "s5_c_im")):
                for j in range(2):
                    loads.append((craw[:, i, :, j], I[name][0].rearrange("(k g) c n -> (g c) k n", g=8)))
            assert len(loads) == S5_LOADS
            for n, (dst, src) in enumerate(loads):
                sp.dma_start(dst, src).then_inc(N.s5_rows_loaded if n < 4 else N.s5_loaded, 16)
            sp.dma_start(O["win_sample"][0, :, 0:511].rearrange("b t a k d -> b (t a k d)"),
                         I["state_nsa_win"][0, :, 1:512].rearrange("b t a k d -> b (t a k d)")).then_inc(N.win_stored, 16)
            sp.wait_ge(N.fin_ev, 2)
            sp.dma_start(O["s5_prompt"][0, 0].rearrange("r (q j) n -> (r q) (j n)", j=2), finrow[0:64, 0, :]).then_inc(N.y_stored, 16)
            sp.dma_start(O["s5_sample"][0].rearrange("(a b) r (q j) n -> (b r q) a (j n)", b=2, j=2), finrow[:, 1:5, :]).then_inc(N.y_stored, 16)
            for t in range(3):
                sp.wait_ge(N.y_out_ev, 2 * (t + 1))
                dst = O["y_prompt"][0, t * P:(t + 1) * P, :] if t < 2 else O["y_sample"].rearrange("b t d -> (b t) d")
                sp.dma_start(dst, yrow[0:P if t < 2 else TS, t, :]).then_inc(N.y_stored, 16)
            sp.wait_ge(N.win_stored, 16)
            sp.wait_ge(N.y_stored, 16 * 5)

        @block.gpsimd
        def _(pool):
            nc.gpsimd.memset(ones[:], 1.0).then_inc(N.ones_made, 1)

            def room(seq):
                if seq >= SLOTS:
                    pool.wait_ge(N.mm_done, 4 * (seq - SLOTS + 1))

            def load(seq, src, dst=None):
                room(seq)
                s = seq % SLOTS
                pool.dma_start(ring[:, s, :].rearrange("p (k c) -> p k c", k=KC) if dst is None else dst, src
                               ).then_inc(ring_full[s], 16)

            def by_rows(w):
                return w.rearrange("(k p) c -> p k c", p=P)

            def load_ada(seq, w, first=0, end=6):
                for i in range(first, end):
                    load(seq + i, by_rows(w)[:, :, 512 * i:512 * i + 512])

            pool.wait_ge(N.x_loaded, 48)
            def load_cmp(seq):
                for kind in range(2):
                    load(seq + kind, I["nsa_cmp_w1"][0, kind].rearrange("(i p) h -> p i h", p=P),
                         ring[:, (seq + kind) % SLOTS, 0:2048].rearrange("p (i h) -> p i h", i=CMP // 2))

            def cmp_pages(r):
                for u in range(KVS):
                    pool.wait_ge(kv_free[u], r + 1)
                    for g in range(2):
                        n = pool.value_load(pt[0:1, DS(r * 16 + u * 2 + g, 1)], min_val=0, max_val=POOL - 1)
                        pool.dma_start(*cmp_piece(DS(n, 1), u, g, 1)).then_inc(kv_odd[u], 16)

            load_ada(SEQ["ada0"], I["attn_ada_w"][0], 0, 4)
            pool.wait_ge(N.pt_loaded, 16)
            cmp_pages(0)
            load_ada(SEQ["ada0"], I["attn_ada_w"][0], 4, 6)
            load_cmp(SEQ["cmp"])
            with pool.Fori(1, 4) as r:
                cmp_pages(r)
            for i in range(6):
                w = min(512, IN_COLS - 512 * i)
                s = (SEQ["w_in"] + i) % SLOTS
                load(SEQ["w_in"] + i, by_rows(I["attn_w_in"][0])[:, :, 512 * i:512 * i + w],
                     ring[:, s, 0:KC * w].rearrange("p (k c) -> p k c", k=KC))
            load_cmp(SEQ["cmp_p"])
            load_ada(SEQ["ada1"], I["mlp_ada_w"][0])
            load_ada(SEQ["ada2"], I["ssm_ada_w"][0])
            load_ada(SEQ["ada3"], I["mlp_ada_w"][1])
            for i in range(2):
                load(SEQ["w_out"] + i, by_rows(I["attn_w_out"][0])[:, :, 512 * i:512 * i + 512])

            def load_mlp(layer):
                base = SEQ["w1_%d" % layer]
                w1 = by_rows(I["mlp_w1"][layer])
                with pool.Fori(0, 2) as it:
                    for j in range(4):
                        pool.wait_ge(N.mm_done, it * 16 + 4 * (base + j - SLOTS + 1))
                        pool.dma_start(ring[:, (base + j) % SLOTS, :].rearrange("p (k c) -> p k c", k=KC),
                                       w1[:, :, DS(it * 2048 + j * 512, 512)]).then_inc(ring_full[(base + j) % SLOTS], 16)
                base = SEQ["w2_%d" % layer]
                w2 = I["mlp_w2"][layer].rearrange("(f p) c -> p f c", p=P)
                with pool.Fori(0, 2) as it:
                    for j in range(4):
                        pool.wait_ge(N.mm_done, it * 16 + 4 * (base + j - SLOTS + 1))
                        pool.dma_start(ring[:, (base + j) % SLOTS, :].rearrange("p (f c) -> p f c", f=16),
                                       w2[:, 16 * (j % 2):16 * (j % 2) + 16, DS(it * 512 + (j // 2) * 256, 256)]
                                       ).then_inc(ring_full[(base + j) % SLOTS], 16)

            load_mlp(0)
            for i in range(4):
                seq = SEQ["glu"] + i
                room(seq)
                for half in range(2):
                    pool.dma_start(ring[:, seq % SLOTS, :].rearrange("p (k z c) -> p k z c", k=KC, z=2)[:, :, half, :],
                                   by_rows(I["s5_w_glu"][0])[:, :, half * D + 256 * i:half * D + 256 * i + 256]
                                   ).then_inc(ring_full[seq % SLOTS], 16)
            for n in range(2 * 16):
                seg, i = divmod(n, 16)
                pool.wait_ge(N.zc_ready, n + 1)
                if n >= 2:
                    pool.wait_ge(N.y_mm, n - 1)
                zc = zcur[:, n % 2]
                c2 = at(cosT[:, 2 * i:2 * i + 2, :], (SEG, 2), (0, 2), (1, SEG))
                s2 = at(sinT[:, 2 * i:2 * i + 2, :], (SEG, 2), (0, 2), (1, SEG))
                zc3 = zc.rearrange("p (q r t) -> p q r t", q=2, r=2)
                nc.gpsimd.tensor_tensor(pc5[:, n % 2].rearrange("p (q r t) -> p q r t", q=2, r=2), zc3, c2, ALU.mult).then_inc(N.zp_done, 1)
                nc.gpsimd.tensor_tensor(ps5[:, n % 2].rearrange("p (q r t) -> p q r t", q=2, r=2), zc3, s2, ALU.mult).then_inc(N.zp_done, 1)
            load_mlp(1)

        def ada_row(i):
            return hT[0:9, 4 + 2 * (i % 2):6 + 2 * (i % 2), 0:TP]

        GROUPS = ((0, 16, 0), (NQ, 8, 16), (KSEL, 2, 24), (KWIN, 2, 26))
        GAINS = ((MQ, 8, 0), (MK, 8, 1), (NQ, 8, 2), (KSEL, 2, 4), (KWIN, 2, 5))
        ADA_SEQ = (SEQ["ada0"], SEQ["ada1"], SEQ["ada2"], SEQ["ada3"])
        GAIN_AT = (96, 120, 104, 128)

        @block.tensor
        def _(pe):
            mm = nc.tensor.matmul

            def tr(out, in_, rows=P):
                return nc.tensor.transpose(out, in_, ident[0:rows, 0:rows])

            pe.wait_ge(N.small_loaded, 16 * SMALL)
            tr(bank[1][:, 0:120], vecA, 120)
            tr(bank[1][:, 120:136], vecB, 16)
            tr(bank[1][:, 136:168], posrow, 32).then_inc(N.small_tr, 1)
            pe.wait_ge(N.csil_ready, 1)
            for k in range(KC):
                last = tr(bank[0][:, 9 * k:9 * k + 9], csil[:, P * k:P * k + P], 9)
            last.then_inc(N.c_tr, 1)
            pe.wait_ge(N.x_loaded, 48)
            for k in range(KC):
                if k >= 2:
                    pe.wait_ge(N.x_ev, k - 1)
                for t in range(3):
                    rows = P if t < 2 else TS
                    last = tr(bank[2 + k % 2][:, P * t:P * t + rows], xrow[t][:, P * k:P * k + P], rows)
                last.then_inc(N.x_tr, 1)

            def ada(n, mm_banks, dst):
                def turn_back(i):
                    pe.wait_ge(N.ada_row, 6 * n + i + 1)
                    for ch in range(4):
                        last = tr(dst[:, (4 * i + ch) * 9:(4 * i + ch) * 9 + 9], ada_row(i)[:, ch // 2, P * (ch % 2):P * (ch % 2) + P], 9)
                    last.then_inc(N.ada_tr, 1)

                for i in range(6):
                    seq = ADA_SEQ[n] + i
                    pe.wait_ge(ring_full[seq % SLOTS], panel_full(seq))
                    if i >= 2:
                        pe.wait_ge(N.ada_row, 6 * n + i - 1)
                    for k in range(KC):
                        last = mm(mm_banks[i % 2][0:9, 0:512], cT[:, k, :], ring[:, seq % SLOTS, 512 * k:512 * k + 512],
                                  start=(k == 0), stop=(k == KC - 1))
                    last.then_inc(N.mm_done, 4)
                    if i:
                        turn_back(i - 1)
                turn_back(5)

            def sum_squares(n):
                for half in range(2):
                    pe.wait_ge(N.sq_ready, 2 * n + half + 1)
                    for k in range(4 * half, 4 * half + 4):
                        last = mm(bank[6][:, 0:T], ones[:], sq[:, k, :], start=(k == 0), stop=(k == KC - 1))
                last.then_inc(N.ssq_ready, 1)

            def normed(n):
                pe.wait_ge(N.h_ready, 8 * (n + 1))
                pe.wait_ge(N.hs_ready, n + 1)

            pe.wait_ge(N.c_ev, 1)
            pe.wait_ge(N.small_ev, 1)
            ada(0, bank[0:2], bank[7])
            pe.wait_ge(N.ones_made, 1)
            sum_squares(0)
            mm(bank[4][0:16, 0:384], rel, onehot[:, OH_TZ:OH_TZ + 384], start=True, stop=True)
            for pg in range(PAGES):
                mm(bank[5][:, 16 * pg:16 * pg + 16], onehot[:, OH_PG + P * pg:OH_PG + P * pg + P], rel, start=True, stop=True)
            mm(bank[5][:, 128:136], onehot[:, OH_CS:OH_CS + P], rel[:, 8:16], start=True, stop=True)
            mm(bank[5][0:8, 136:152], onehot[:, OH_OWN:OH_OWN + 8], rel, start=True, stop=True)
            for tn in range(16):
                last = mm(bank[5][:, 152 + 8 * tn:160 + 8 * tn], onehot[:, OH_CP + P * tn:OH_CP + P * tn + P], rel[:, 8:16],
                          start=True, stop=True)
            last.then_inc(N.bias_mm, 1)

            pe.wait_ge(N.bias_ev, 1)
            w1k = []
            for kind in range(2):
                seq = SEQ["cmp"] + kind
                pe.wait_ge(ring_full[seq % SLOTS], panel_full(seq))
                w1k.append(ring[:, seq % SLOTS, 0:2048].rearrange("p (i h) -> p i h", i=CMP // 2))
                for i in range(CMP // 2):
                    last = mm(bank[4][:, kind:kind + 1], w1k[kind][:, i, :], posT[:, 16 * kind + i:16 * kind + i + 1],
                              start=(i == 0), stop=(i == CMP // 2 - 1))
            last.then_inc(N.pb_mm, 1)
            for half in range(2):
                for u in range(2 * KVS):
                    seq = 2 * KVS * half + u
                    pe.wait_ge(kv_full[seq % KVS], kv_full_value(seq))
                    pe.wait_ge(kv_odd[seq % KVS], 32 * (seq // KVS + 1))
                    if seq >= 2:
                        pe.wait_ge(N.cmp_ev, seq - 1)
                    for x in range(4):
                        last = tr(bank[2 + seq % 2][:, P * x:P * x + P], kv[:, seq % KVS, P * x:P * x + P])
                        if x == 0 and u:
                            last.then_inc(kv_free[(seq - 1) % KVS], 1)
                    last.then_inc(N.cmp_tr, 1)
                pe.wait_ge(N.cmp_ev, 2 * KVS * (half + 1))
                if half:
                    pe.wait_ge(N.gelu_ev, 1)
                for kind in range(2):
                    for i in range(CMP // 2):
                        last = mm(bank[kind][:, 0:256], w1k[kind][:, i, :], at(pairs[:, 4096 * kind + i:], (2048, 2), (16, 128)),
                                  start=(i == 0), stop=(i == CMP // 2 - 1))
                        if kind == 0 and i == 0:
                            last.then_inc(kv_free[seq % KVS], 1)
                if half:
                    last.then_inc(N.mm_done, 8)
                else:
                    last.then_inc(N.cmp_mm, 1)

            normed(0)
            pe.wait_ge(N.gelu_ev, 2)
            pe.wait_ge(N.small_ev, 1)
            for p in range(6):
                seq = SEQ["w_in"] + p
                w = min(512, IN_COLS - 512 * p)
                pe.wait_ge(ring_full[seq % SLOTS], panel_full(seq))
                for t in range(3):
                    if p >= 2:
                        pe.wait_ge(N.z_ev, 3 * (p - 2) + t + 1)
                    rows = P if t < 2 else TS
                    for k in range(KC):
                        last = mm(bank[3 * (p % 2) + t][0:rows, 0:w], hT[:, k, P * t:P * t + rows],
                                  ring[:, seq % SLOTS, w * k:w * k + w], start=(k == 0), stop=(k == KC - 1))
                    last.then_inc(N.mm_done, 2 if t == 2 else 1)

            def spread_q(col, n0):
                for b in range(TS):
                    if b >= 2 or n0:
                        pe.wait_ge(N.q_bc_ev, n0 + b - 1)
                    mm(bank[b % 2][:, 0:512], ident[0:TS, b:b + 1].to_broadcast([TS, P]), zs[:, col:col + 512],
                       start=True, stop=True).then_inc(N.q_bc, 1)

            pe.wait_ge(N.z_ev, 18)
            pe.wait_ge(N.zs_normed, 1)
            spread_q(MQ, 0)
            pe.wait_ge(N.gates_ready, 1)
            mm(bank[6][0:64, 0:24], cst[0:8, C_GT:C_GT + 64], gates_s, start=True, stop=True).then_inc(N.small_tr, 1)

            def turn(groups, n0):
                for g, pieces in enumerate(groups):
                    if n0 + g >= 2:
                        pe.wait_ge(N.qk_ev, n0 + g - 1)
                    for i, piece in enumerate(pieces):
                        last = tr(bank[2 + g % 2][:, P * i:P * i + P], piece)
                    last.then_inc(N.qk_tr, 1)

            def chunks_of(col, pair):
                return [z[:, t, col + P * c:col + P * c + P] for c in (2 * pair, 2 * pair + 1) for t in range(2)]

            pe.wait_ge(N.z_normed, 1)
            turn([chunks_of(MQ, 0), chunks_of(MQ, 1), chunks_of(MK, 0), chunks_of(MK, 1)], 0)
            pe.wait_ge(N.mods_ready, 1)
            pe.wait_ge(N.qk_ev, 4)
            for kind in range(2):
                for h in range(KVH):
                    for t in range(2):
                        for e in range(2):
                            c = 256 * kind + P * h + 64 * t
                            last = mm(bank[2][64 * e:64 * e + 64, c:c + 64],
                                      z[:, t, KCMP + P * kind + 64 * h:KCMP + P * kind + 64 * h + 64], at(ident[:, e:], (2, 64)),
                                      start=True, stop=True)
            last.then_inc(N.cmp_tr, 1)
            pe.wait_ge(N.cmp_ev, 4 * KVS + 1)
            for kind in range(2):
                seq = SEQ["cmp_p"] + kind
                pe.wait_ge(ring_full[seq % SLOTS], panel_full(seq))
                w1 = ring[:, seq % SLOTS, 0:2048].rearrange("p (i h) -> p i h", i=CMP // 2)
                for i in range(CMP // 2):
                    last = mm(bank[4][:, 16 * kind:16 * kind + 16], w1[:, i, :], at(p_pairs[:, 256 * kind + i:], (P, 2), (16, 8)),
                              start=(i == 0), stop=(i == CMP // 2 - 1))
                last.then_inc(N.mm_done, 4)
            pe.wait_ge(N.gelu_ev, 3)
            for kind in range(2):
                for half in range(2):
                    for h in range(KVH):
                        c = ((kind * 2 + half) * 2 + h) * 64
                        last = mm(bank[5][:, c:c + 64], hg[:, (kind * 2 + h) * 256 + P * half:(kind * 2 + h) * 256 + P * half + P],
                                  w2c[:, 64 * kind:64 * kind + 64], start=True, stop=True)
            for kind in range(2):
                for h in range(KVH):
                    c = 64 + (kind * 2 + h) * 64
                    last = mm(bank[4][0:8, c:c + 64], hg[:, 1024 + (kind * 2 + h) * 8:1032 + (kind * 2 + h) * 8],
                              w2c[:, 64 * kind:64 * kind + 64], start=True, stop=True)
            last.then_inc(N.cmp2_mm, 1)
            pe.wait_ge(N.q_bc_ev, 8)
            ada(1, bank[0:2], bank[7])
            pe.wait_ge(N.small_ev, 2)
            ada(2, bank[0:2], bank[6])

            pe.wait_ge(N.kdup_ready, 1)
            for h in range(KVH):
                last = tr(bank[4][:, 384 + 8 * h:392 + 8 * h], kpd[:, P * h:P * h + P], 8)
            last.then_inc(N.kcp_tr, 1)

            pe.wait_ge(N.moba_scored, 1)
            mm(bank[0][:, 0:512], ones[:], s_raw, start=True, stop=True).then_inc(N.gate_sum, 1)

            def softmax_sums(br, last_dim, mine):
                pe.wait_ge(N.mx_in, br + 1)
                last = tr(bank[2][0:64, 0:P], last_dim)
                if mine is not None:
                    last = tr(bank[2][0:64, P:P + 8], mine, 8)
                last.then_inc(N.mx_tr, 1)
                pe.wait_ge(N.mx_diag, br + 1)
                mm(bank[3][:, 0:64], ones[0:64, :], diag, start=True, stop=True).then_inc(N.mx_bc, 1)
                pe.wait_ge(N.p_ready, br + 1)
                last = mm(bank[4][0:64, 0:1], s_cs if br == 1 else lsum, ones[:, 0:1], start=True, stop=mine is None)
                if mine is not None:
                    last = mm(bank[4][0:64, 0:1], mine, ones[0:8, 0:1], start=False, stop=True)
                last.then_inc(N.l_done, 1)

            def pair_scores(i):
                if i:
                    pe.wait_ge(N.pr_log, i)
                for pr in range(2):
                    if i < 4:
                        r = slice(64 * pr, 64 * pr + 64)
                        q = qkT[r, TP * i:TP * i + TP]
                        k = qkT[r, 1024 + TP * i:1024 + TP * i + TP]
                    else:
                        h = i - 4
                        r = slice(64 * (h % 2), 64 * (h % 2) + 64)
                        q = qkT[r, TP * (h // 2):TP * (h // 2) + TP]
                        k = qkT[r, 1024 + 512 * pr + TP * (h // 4):1024 + 512 * pr + TP * (h // 4) + TP]
                    mm(bank[pr][:, 0:P], q[:, 0:P], k[:, 0:P], start=True, stop=True)
                    last = mm(bank[pr][:, P:P + TP], q[:, P:TP], k, start=True, stop=True)
                last.then_inc(N.pr_s, 1)

            def pair_rest(i):
                pe.wait_ge(N.pr_p, i + 1)
                if i:
                    pe.wait_ge(N.pr_tev, i)
                for pr in range(2):
                    for j in range(3):
                        last = tr(bank[2 + pr][:, P * j:P * j + P], sps[i % 2][:, 384 * pr + P * j:384 * pr + P * j + P])
                last.then_inc(N.pr_tr, 1)
                chunk = i if i < 4 else 4 + (i - 4) // 2
                ob = bank[6 + chunk % 2]
                if chunk >= 2 and (i < 4 or i % 2 == 0):
                    pe.wait_ge(N.pr_oev, chunk - 1)
                h = i - 4
                if i >= 4:
                    if i > 4:
                        pe.wait_ge(N.cp_tev, h)
                    for t in range(2):
                        c = (((h % 2) * 2 + t) * 4 + h // 2) * 8
                        last = tr(bank[4][0:8, TP + P * t:TP + P * t + P], s_cp[:, c:c + 8])
                    last.then_inc(N.cp_tr, 1)
                    rows = slice(64 * (h % 2), 64 * (h % 2) + 64)
                    pe.wait_ge(N.cp_tev, h + 1)
                    mm(ob[rows, 0:TP], kvp[:, P + 64 * (h // 4):P + 64 * (h // 4) + 64], pcT[:, TP * (h % 2):TP * (h % 2) + TP],
                       start=True, stop=False)
                pe.wait_ge(N.pr_tev, i + 1)
                for pr in range(2):
                    if i < 4:
                        rows, v = slice(64 * pr, 64 * pr + 64), MV + 64 * (2 * i + pr)
                        first, final = True, True
                    else:
                        v = (VSEL, VWIN)[pr] + 64 * (h // 4)
                        first, final = False, pr == 1
                    pTp = pTs[i % 2][:, 384 * pr:384 * pr + 384]
                    mm(ob[rows, 0:TP], z[:, 0, v:v + 64], pTp[:, 0:TP], start=first, stop=False)
                    last = mm(ob[rows, P:TP], z[:, 1, v:v + 64], pTp[:, TP:384], start=False, stop=final)
                last.then_inc(N.pr_pv, 1)

            def pair_step(i, first, end):
                if i < end:
                    pair_scores(i)
                if i > first:
                    pair_rest(i - 1)

            def p_of(half, b4, pg):
                return pbuf[:, 1024 * half + 256 * b4 + 32 * pg:1024 * half + 256 * b4 + 32 * pg + 32]

            own_m, own_s, own_w = own[:, 0:64], own[:, 64:128], own[:, 128:192]
            pe.wait_ge(N.kcp_ev, 1)
            softmax_sums(0, m1, own_m)
            spread_q(NQ, 8)
            pe.wait_ge(N.q_bc_ev, 16)
            for half in range(2):
                mm(bank[half][:, 0:512], s4[:, P * half:P * half + P], zs[:, NQ:NQ + 512], start=True, stop=True).then_inc(N.q_bc, 1)
            for b in range(TS):
                for pg in range(PAGES):
                    seq = KV_MV + 8 * b + pg
                    pe.wait_ge(kv_full[seq % KVS], kv_full_value(seq))
                    mm(bank[5][32 * (b // 4):32 * (b // 4) + 32, 0:512], p_of(b // 4, b % 4, pg), kv[:, seq % KVS, :],
                       start=(b % 4 == 0 and pg == 0), stop=False).then_inc(kv_free[seq % KVS], 1)
                if b == 0:
                    pe.wait_ge(N.cw_made, 1)
                    pe.wait_ge(N.mods_ready, 3)
                    pe.wait_ge(N.bias_back, 16)
                if b < 5:
                    pair_step(b, 0, 4)
            for half in range(2):
                last = mm(bank[5][32 * half:32 * half + 32, 0:512], own_m[:, 32 * half:32 * half + 32], zs[:, MV:MV + 512],
                          start=False, stop=True)
            last.then_inc(N.pv_done, 1)
            pe.wait_ge(N.osum_ready, 1)
            for c in range(4):
                last = mm(bank[2][:, 8 * c:8 * c + 8], oacc[:, P * c:P * c + P], cst[0:64, C_G:C_G + 8], start=True, stop=True)
            last.then_inc(N.osum_mm, 1)
            pe.wait_ge(N.zdup_ready, 1)
            pe.wait_ge(N.oTs_ready, 1)
            turn([chunks_of(NQ, 0), chunks_of(NQ, 1)] +
                 [[zdup[:, t, src, h] for h in range(KVH) for t in range(2)] for src in range(2)], 4)
            pe.wait_ge(N.qk_ev, 8)
            for h in range(NSA_H):
                r = slice(64 * (h % 2), 64 * (h % 2) + 64)
                for t in range(2):
                    last = mm(bank[h % 2][:, (t * 4 + h // 2) * 8:(t * 4 + h // 2) * 8 + 8],
                              qkT[r, TP * (h // 2) + P * t:TP * (h // 2) + P * t + P], kcTp[r, 8 * (h // 4):8 * (h // 4) + 8],
                              start=True, stop=True)
            last.then_inc(N.cp_mm, 1)
            pe.wait_ge(N.pr_oev, 4)
            ada(3, bank[2:4], bank[7])

            softmax_sums(1, s_cs, None)
            for half in range(2):
                last = mm(bank[5][32 * half:32 * half + 32, 0:P], s_cs[:, 32 * half:32 * half + 32],
                          kvc[:, 256 + P * half:256 + P * half + P], start=True, stop=True)
            last.then_inc(N.pv_done, 1)

            def pages_pv(br, mine, vcol, units, tiles):
                softmax_sums(br, m1, mine)
                for u in range(units[1] - units[0]):
                    seq = units[0] + u
                    pe.wait_ge(kv_full[seq % KVS], kv_full_value(seq))
                    for g in range(4):
                        b, pg = divmod(4 * u + g, tiles)
                        last = mm(bank[5][32 * (b // 4):32 * (b // 4) + 32, 0:P], p_of(b // 4, b % 4, pg),
                                  kv[:, seq % KVS, P * g:P * g + P], start=(b % 4 == 0 and pg == 0), stop=False)
                    last.then_inc(kv_free[seq % KVS], 1)
                    if br == 2 and u % 2:
                        if u == 1:
                            pe.wait_ge(N.cp_ready, 1)
                            pe.wait_ge(N.mods_ready, 4)
                            pe.wait_ge(N.bias_back, 32)
                        pair_step(4 + u // 2, 4, 12)
                if br == 2:
                    pair_step(12, 4, 12)
                for half in range(2):
                    last = mm(bank[5][32 * half:32 * half + 32, 0:P], mine[:, 32 * half:32 * half + 32],
                              zs[:, vcol:vcol + P], start=False, stop=True)
                last.then_inc(N.pv_done, 1)

            pages_pv(2, own_s, VSEL, (KV_SV, KV_WV), 8)
            pages_pv(3, own_w, VWIN, (KV_WV, KV_END), 4)
            pe.wait_ge(N.osum_ready, 2)
            for c in range(4):
                last = mm(bank[2][:, 8 * c:8 * c + 8], oacc[:, P * c:P * c + P], cst[0:64, C_G:C_G + 8], start=True, stop=True)
            last.then_inc(N.osum_mm, 1)

            pe.wait_ge(N.pr_oev, 8)
            pe.wait_ge(N.oTs_ready, 2)
            for i in range(2):
                seq = SEQ["w_out"] + i
                pe.wait_ge(ring_full[seq % SLOTS], panel_full(seq))
                for ch in range(4):
                    if i:
                        pe.wait_ge(N.out_free, ch + 1)
                    for k in range(KC):
                        last = mm(bank[ch][:, 0:T], ring[:, seq % SLOTS, 512 * k + P * ch:512 * k + P * ch + P], hT[:, k, :],
                                  start=(k == 0), stop=(k == KC - 1))
                    last.then_inc(N.mm_done, 1)

            def mlp(layer, outs_before, between):
                base = SEQ["w1_%d" % layer]
                normed(1 + 2 * layer)
                pe.wait_ge(N.out_free, outs_before)
                with pe.Fori(0, 2) as it:
                    for j in range(4):
                        s = (base + j) % SLOTS
                        pe.wait_ge(ring_full[s], it * 16 + panel_full(base + j))
                        for ch in range(4):
                            pe.wait_ge(N.relu_ev, it * 16 + 36 * layer + 4 * j + ch + 1)
                            for k in range(KC):
                                last = mm(bank[ch][:, 0:T], ring[:, s, 512 * k + P * ch:512 * k + P * ch + P], hT[:, k, :],
                                          start=(k == 0), stop=(k == KC - 1))
                            last.then_inc(N.mm_done, 1)
                pe.wait_ge(N.relu_ev, 36 * (layer + 1))
                between()
                base = SEQ["w2_%d" % layer]
                pe.wait_ge(N.act_ready, 8 * (layer + 1))
                with pe.Fori(0, 2) as it:
                    for j in range(4):
                        s = (base + j) % SLOTS
                        pe.wait_ge(ring_full[s], it * 16 + panel_full(base + j))
                        if j % 2 == 0:
                            pe.wait_ge(N.out_free, it * 4 + outs_before)
                        for c in range(2):
                            for f in range(16):
                                last = mm(bank[j // 2 * 2 + c][:, 0:T], ring[:, s, 256 * f + P * c:256 * f + P * c + P],
                                          actT[:, 16 * (j % 2) + f, :], start=(j % 2 == 0 and f == 0), stop=(j % 2 == 1 and f == 15))
                            last.then_inc(N.mm_done, 2)

            sum_squares(1)
            pe.wait_ge(N.s5_rows_made, 1)
            pe.wait_ge(N.s5_rows_loaded, 64)
            pe.wait_ge(N.out_free, 8)
            for i in range(3):
                tr(bank[0][:, 32 * i:32 * i + 32], s5row[:, i, :], 32)
            for a in range(4):
                last = tr(bank[1][:, P * a:P * a + P], hrow[:, a, :])
            last.then_inc(N.s5_rows_tr, 1)
            pe.wait_ge(N.s5_rows_ev, 1)

            def s5_turns():
                pe.wait_ge(N.s5_bd, 1)
                for r in range(2):
                    for k in range(8):
                        last = tr(bank[2 * r + k // 4][:, P * (k % 4):P * (k % 4) + P],
                                  bdia[:, r].rearrange("p q j c -> p (q j c)")[:, P * k:P * k + P])
                last.then_inc(N.s5_b_tr, 1)
                for r in range(2):
                    for k in range(8):
                        last = tr(bank[4 + 2 * r + k // 4][:, P * (k % 4):P * (k % 4) + P],
                                  craw[:, r, k].rearrange("p j n -> p (j n)"))
                last.then_inc(N.s5_c_tr, 1)
                pe.wait_ge(N.s5_b_ev, 1)
                pe.wait_ge(N.s5_c_ev, 1)

            mlp(0, 8, s5_turns)
            sum_squares(2)

            normed(2)
            pe.wait_ge(N.out_free, 16)

            def rows_of(q):
                return slice(32 * (q % 4), 32 * (q % 4) + 32)

            for q in range(NT):
                for r in range(2):
                    c = (q // 4) * 16 + 8 * r
                    last = mm(bank[4 + q % 4][:, c:c + 8], BT[rows_of(q), q // 4, r, :], hT[rows_of(q), q // 4, TP:T],
                              start=True, stop=True)
            last.then_inc(N.us_mm, 1)

            def c_of(i, q):
                return CT[:, i, q // 4, 32 * (q % 4):32 * (q % 4) + 32]

            def unit_out(n):
                seg, i = divmod(n, 16)
                k = i // 2
                g = 8 * seg + k
                pe.wait_ge(N.zp_done, 2 * (n + 1))
                if g >= 2 and i % 2 == 0:
                    pe.wait_ge(N.y_ev, g)
                c3 = pc5[:, n % 2].rearrange("p (q r t) -> p q r t", q=2, r=2)
                s3 = ps5[:, n % 2].rearrange("p (q r t) -> p q r t", q=2, r=2)
                for e in range(2):
                    q = 2 * i + e
                    out = bank[4 + g % 2][rows_of(q), 0:SEG]
                    mm(out, c_of(0, q), c3[:, e, 0], start=True, stop=False)
                    mm(out, c_of(1, q), s3[:, e, 1], start=False, stop=False)
                    mm(out, c_of(2, q), s3[:, e, 0], start=False, stop=False)
                    last = mm(out, c_of(2, q), c3[:, e, 1], start=False, stop=True)
                last.then_inc(N.y_mm, 1)

            def unit_in(n):
                seg, i = divmod(n, 16)
                if n >= 2:
                    pe.wait_ge(N.u_free, n - 1)
                for e in range(2):
                    q = 2 * i + e
                    for r in range(2):
                        last = mm(bank[2 * (n % 2) + e][:, SEG * r:SEG * r + SEG], BT[rows_of(q), q // 4, r, :],
                                  hT[rows_of(q), q // 4, SEG * seg:SEG * seg + SEG], start=True, stop=True)
                last.then_inc(N.u_mm, 1)

            unit_in(0)
            pe.wait_ge(N.xs_ready, 1)
            for q in range(NT):
                out = bank[6][rows_of(q), 8 * (q // 4):8 * (q // 4) + 8]
                mm(out, c_of(0, q), xs5[:, :, 0, q], start=True, stop=False)
                last = mm(out, c_of(2, q), xs5[:, :, 1, q], start=False, stop=True)
            last.then_inc(N.ys_mm, 1)
            for a in range(4):
                last = tr(bank[7][:, P * a:P * a + P], xs5[:, 2 * a:2 * a + 2].rearrange("p b r q -> p (b r q)"))
            last.then_inc(N.fin_tr, 1)
            for n in range(1, 33):
                if n < 32:
                    unit_in(n)
                unit_out(n - 1)
            pe.wait_ge(N.fin_ready, 1)
            pe.wait_ge(N.gelu_ready, 17)
            tr(bank[6][0:64, 0:P], xlast).then_inc(N.fin_tr, 1)

            pe.wait_ge(N.fin_ev, 2)
            pe.wait_ge(N.u_free, 32)
            for j in range(4):
                seq = SEQ["glu"] + j
                pe.wait_ge(ring_full[seq % SLOTS], panel_full(seq))
                for c in range(2):
                    if 2 * j + c >= 4:
                        pe.wait_ge(N.out_free, 16 + 2 * j + c - 3)
                    for zi in range(2):
                        b = 4 * (j % 2) + 2 * c + zi
                        for k in range(KC):
                            last = mm(bank[b][:, 0:T], ring[:, seq % SLOTS, 512 * k + 256 * zi + P * c:512 * k + 256 * zi + P * c + P],
                                      yT[:, k, :], start=(k == 0), stop=(k == KC - 1))
                        last.then_inc(N.mm_done, 1)
            pe.wait_ge(N.out_free, 24)
            sum_squares(3)
            mlp(1, 24, lambda: None)

            pe.wait_ge(N.x_ready, 4)
            for t in range(3):
                rows = P if t < 2 else TS
                for half in range(2):
                    for k in range(4):
                        last = tr(bank[2 * t + half][0:rows, P * k:P * k + P], xT[:, 4 * half + k, P * t:P * t + rows])
                    last.then_inc(N.y_tr, 1)

        @block.scalar
        def _(act):
            step = [0]

            def then(ins):
                step[0] += 1
                ins.then_inc(N.act_step, 1)
                act.wait_ge(N.act_step, step[0])

            f = nc.scalar.activation
            act.wait_ge(N.c_loaded, 32)
            f(csil, crow, ACT.Silu).then_inc(N.csil_ready, 1)
            for k in range(KC):
                act.wait_ge(N.x_tr, k + 1)
                nc.scalar.copy(xT[:, k, :], bank[2 + k % 2][:, 0:T]).then_inc(N.x_ev, 1)

            def norm(n):
                act.wait_ge(N.x_ev, 8)
                if n:
                    act.wait_ge(N.x_ready, n)
                for half in range(2):
                    k = slice(4 * half, 4 * half + 4)
                    f(sq[:, k, :], xT[:, k, :], ACT.Square).then_inc(N.sq_ready, 1)
                act.wait_ge(N.r_ready, 2 * n + 1)
                f(sq[:, 0, :], sq[:, 0, :], ACT.Sqrt).then_inc(N.rt_ready, 1)
                for k in range(KC):
                    act.wait_ge(N.h_mul, 8 * n + k + 1)
                    f(hT[:, k, 0:TP], hT[:, k, 0:TP], ACT.Identity, bias=mods[:, n, k, 0:1]).then_inc(N.h_ready, 1)

            def ada_evac(n, banks):
                for i in range(6):
                    act.wait_ge(N.mm_done, 4 * (ADA_SEQ[n] + i + 1))
                    if 6 * n + i >= 2:
                        act.wait_ge(N.ada_tr, 6 * n + i - 1)
                    nc.scalar.copy(ada_row(i), banks[i % 2][0:9, 0:512].rearrange("p (k c) -> p k c", k=2)).then_inc(N.ada_row, 1)

            ada_evac(0, bank[0:2])
            norm(0)
            act.wait_ge(N.pb_mm, 1)
            nc.scalar.copy(pbias, bank[4][:, 0:2]).then_inc(N.pb_ev, 1)
            for half in range(2):
                for u in range(2 * KVS):
                    n = 2 * KVS * half + u
                    act.wait_ge(N.cmp_tr, n + 1)
                    nc.scalar.copy(at(pairs[:, P * u:], (2048, 4), (1, P)), bank[2 + n % 2][:, 0:512].rearrange("p (x c) -> p x c", x=4)
                                   ).then_inc(N.cmp_ev, 1)
                if half:
                    act.wait_ge(N.mm_done, 4 * (SEQ["cmp"] + 2))
                else:
                    act.wait_ge(N.cmp_mm, 1)
                act.wait_ge(N.pb_ev, 1)
                for kind in range(2):
                    last = f(at(hg[:, 512 * kind + P * half:], (256, 2), (1, P)), bank[kind][:, 0:256].rearrange("p (h c) -> p h c", h=2),
                             ACT.Gelu_apprx_tanh, bias=pbias[:, kind:kind + 1])
                last.then_inc(N.gelu_ev, 1)
            for p in range(6):
                w = min(512, IN_COLS - 512 * p)
                for t in range(3):
                    act.wait_ge(N.mm_done, 4 * (SEQ["w_in"] + p) + (t + 1 if t < 2 else 4))
                    dst = z[:, t, 512 * p:512 * p + w] if t < 2 else zs[:, 512 * p:512 * p + w]
                    nc.scalar.copy(dst, bank[3 * (p % 2) + t][0:P if t < 2 else TS, 0:w]).then_inc(N.z_ev, 1)
            act.wait_ge(N.zs_ss, 1)
            f(sss, sss, ACT.Sqrt).then_inc(N.zs_std, 1)
            act.wait_ge(N.z_ev, 18)
            act.wait_ge(N.z_ss, 1)
            f(ss, ss, ACT.Sqrt).then_inc(N.z_std, 1)
            f(gates_s, zs[:, GATE:GATE + 24], ACT.Sigmoid).then_inc(N.gates_ready, 1)
            f(gates.rearrange("p (t c) -> p t c", t=2), z[:, :, GATE:GATE + 24], ACT.Sigmoid).then_inc(N.gates_ready, 1)

            def spread_evac(n0):
                for b in range(TS):
                    act.wait_ge(N.q_bc, n0 + b + 1)
                    nc.scalar.copy(qb[:, b, :], bank[b % 2][:, 0:512]).then_inc(N.q_bc_ev, 1)

            def turn_evac(n0):
                for g in range(4):
                    act.wait_ge(N.qk_tr, n0 + g + 1)
                    nc.scalar.copy(qkT[:, 512 * g:512 * g + 512], bank[2 + g % 2][:, 0:512]).then_inc(N.qk_ev, 1)

            spread_evac(0)
            act.wait_ge(N.tz_stored, 16)
            turn_evac(0)
            act.wait_ge(N.zs_normed, 1)
            act.dma_start(O["moba_sample"], zs[:, MK:MK + 1024]).then_inc(N.z_stored, 16)
            act.dma_start(O["nsa_sample"], zs[:, KCMP:KCMP + 512]).then_inc(N.z_stored, 16)
            act.dma_start(O["win_sample"][0, :, 511].rearrange("b a k d -> b (a k d)"), zs[:, KWIN:KWIN + 256]).then_inc(N.z_stored, 16)
            act.wait_ge(N.z_normed, 1)
            act.dma_start(O["moba_prompt"].rearrange("(t p) c -> p t c", p=P), z[:, :, MK:MK + 1024]).then_inc(N.z_stored, 16)
            act.dma_start(O["nsa_prompt"].rearrange("(t p) c -> p t c", p=P), z[:, :, KCMP:KCMP + 512]).then_inc(N.z_stored, 16)
            act.dma_start(O["win_prompt"].rearrange("(t p) c -> p t c", p=P), z[:, :, KWIN:KWIN + 256]).then_inc(N.z_stored, 16)

            act.wait_ge(N.cmp_tr, 4 * KVS + 1)
            nc.scalar.copy(p_pairs, bank[2][:, 0:512]).then_inc(N.cmp_ev, 1)
            act.wait_ge(N.mm_done, 4 * (SEQ["cmp_p"] + 2))
            for kind in range(2):
                last = f(hg[:, 1024 + 16 * kind:1040 + 16 * kind], bank[4][:, 16 * kind:16 * kind + 16], ACT.Gelu_apprx_tanh,
                         bias=pbias[:, kind:kind + 1])
            last.then_inc(N.gelu_ev, 1)
            ada_evac(1, bank[0:2])
            ada_evac(2, bank[0:2])
            act.wait_ge(N.kc_ss, 1)
            f(ssc[:, 0:4], ssc[:, 0:4], ACT.Sqrt)
            f(ssc[0:8, 4:6], ssc[0:8, 4:6], ACT.Sqrt).then_inc(N.kc_std, 1)

            def pair_exp(i):
                act.wait_ge(N.pr_log, i + 1)
                buf = sps[i % 2]
                for pr in range(2):
                    for t, (a, b) in enumerate(((0, P), (P, 384))):
                        j = 4 * (i % 2) + 2 * pr + t
                        last = f(buf[:, 384 * pr + a:384 * pr + b], buf[:, 384 * pr + a:384 * pr + b], ACT.Exp,
                                 bias=nmin[:, j:j + 1], scale=-1.0, accum_out=lrow[:, j:j + 1])
                last.then_inc(N.pr_exp, 1)

            def pair_evac(i):
                act.wait_ge(N.pr_tr, i + 1)
                if i >= 2:
                    act.wait_ge(N.pr_pv, i - 1)
                nc.scalar.copy(pTs[i % 2].rearrange("p (a c) -> p a c", a=2), psum[:, 2:4, 0:384]).then_inc(N.pr_tev, 1)
                if i >= 4:
                    act.wait_ge(N.cp_tr, i - 3)
                    c = TP * (i % 2)
                    nc.scalar.copy(pcT[:, c:c + TP], bank[4][0:8, TP:2 * TP]).then_inc(N.cp_tev, 1)
                chunk = i if i < 4 else 4 + (i - 4) // 2
                if i < 4 or i % 2:
                    act.wait_ge(N.pr_pv, i + 1)
                    nc.scalar.copy(hT[:, chunk, 0:TP], bank[6 + chunk % 2][:, 0:TP]).then_inc(N.pr_oev, 1)

            def pair_steps(first, end):
                for i in range(first, end + 1):
                    if i < end:
                        pair_exp(i)
                    if i > first:
                        pair_evac(i - 1)

            def exp_pages(br, tiles, mine):
                act.wait_ge(N.log_ready, br + 1)
                for half in range(2):
                    f(at(pbuf[:, 1024 * half:], (264, 4), (32, tiles), (1, 8)),
                      at(s_log[:, 32 * tiles * half:], (8 * tiles, 4), (8, tiles), (1, 8)), ACT.Exp)
                f(mine, mine, ACT.Exp).then_inc(N.p_exp, 1)

            exp_pages(0, 8, own[:, 0:64])
            spread_evac(8)
            act.wait_ge(N.z_stored, 16 * 6)
            pair_steps(0, 4)
            turn_evac(4)
            act.wait_ge(N.cp_log, 1)
            f(s_cp, s_cp, ACT.Exp).then_inc(N.cp_exp, 1)
            ada_evac(3, bank[2:4])
            act.wait_ge(N.log_ready, 2)
            f(s_cs, s_cs, ACT.Exp).then_inc(N.p_exp, 1)
            exp_pages(2, 8, own[:, 64:128])
            pair_steps(4, 12)
            exp_pages(3, 4, own[:, 128:192])

            def relu(layer):
                act.wait_ge(N.x_ready, 1 + 2 * layer)
                if layer:
                    act.wait_ge(N.y_stored, 32)
                act.sem_inc(N.relu_ev, 4)
                act.wait_ge(N.z_stored, 16 * 6)
                base = SEQ["w1_%d" % layer]
                with act.Fori(0, 2) as it:
                    for m in range(16):
                        act.wait_ge(N.mm_done, it * 16 + 4 * base + m + 1)
                        f(actT[:, DS(it * 16 + m, 1), :], psum[:, m % 4:m % 4 + 1, 0:T], ACT.Relu).then_inc(N.relu_ev, 1)

            norm(1)
            act.wait_ge(N.s5_rows_ev, 1)
            f(st[:, 3, :], st[:, 2, :], ACT.Exp).then_inc(N.s5_dt, 1)
            act.wait_ge(N.s5_ang, 1)
            f(st[:, 8, :], st[:, 4, :], ACT.Exp)
            f(st[:, 9, :], st[:, 7, :], ACT.Sin)
            f(st[:, 10, :], st[:, 7, :], ACT.Sin, scale=0.5).then_inc(N.s5_sin, 1)
            relu(0)
            act.wait_ge(N.s5_b_tr, 1)
            act.wait_ge(N.s5_tables, 1)
            nc.scalar.copy(BT.rearrange("p k r n -> p r k n"), psum[:, 0:4, :].rearrange("p (r k) (l n) -> p r (k l) n", r=2, l=4)
                           ).then_inc(N.s5_b_ev, 1)
            norm(2)
            act.wait_ge(N.fin_tr, 1)
            nc.scalar.copy(finrow[:, 1:5, :].rearrange("p a c -> p (a c)"), bank[7][:, 0:512]).then_inc(N.fin_ev, 1)
            act.wait_ge(N.y_ev, 1)
            f(yT[:, :, TP:T], yT[:, :, TP:T], ACT.Gelu_apprx_tanh).then_inc(N.gelu_ready, 1)
            for g in range(16):
                seg, k = divmod(g, 8)
                act.wait_ge(N.y_ev, g + 2)
                y = yT[:, k, SEG * seg:SEG * seg + SEG]
                f(y, y, ACT.Gelu_apprx_tanh).then_inc(N.gelu_ready, 1)
            act.wait_ge(N.fin_tr, 2)
            nc.scalar.copy(finrow[0:64, 0, :], bank[6][0:64, 0:P]).then_inc(N.fin_ev, 1)
            for n in range(8):
                act.wait_ge(N.mm_done, 4 * SEQ["glu"] + 2 * n + 2)
                if n >= 2:
                    act.wait_ge(N.out_free, 16 + n - 1)
                f(sig[:, n % 2, :], bank[4 * (n // 2 % 2) + 2 * (n % 2) + 1][:, 0:T], ACT.Sigmoid).then_inc(N.sig_ready, 1)
            norm(3)
            relu(1)
            for t in range(3):
                rows = P if t < 2 else TS
                for half in range(2):
                    act.wait_ge(N.y_tr, 2 * t + half + 1)
                    nc.scalar.copy(yrow[0:rows, t, 512 * half:512 * half + 512], bank[2 * t + half][0:rows, 0:512]
                                   ).then_inc(N.y_out_ev, 1)

        @block.vector
        def _(dve):
            step = [0]

            def then(ins):
                step[0] += 1
                ins.then_inc(N.dve_step, 1)
                dve.wait_ge(N.dve_step, step[0])

            tt, ts = nc.vector.tensor_tensor, nc.vector.tensor_scalar
            stt, red, cp = nc.vector.scalar_tensor_tensor, nc.vector.tensor_reduce, nc.vector.tensor_copy
            rcp = nc.vector.reciprocal

            def mods_evac(n):
                dve.wait_ge(N.ada_tr, 6 * (n + 1))
                src = bank[6 if n == 2 else 7]
                then(tt(mods[:, n].rearrange("p c j -> p (c j)").rearrange("p (c j) -> p c j", j=9),
                        src[:, 0:216].rearrange("p (c j) -> p c j", j=9), at(vT[:, 24 * n:], (1, 24), (0, 9)), ALU.add))
                a = mods[:, n, 8:16, :]
                stt(out=a, in0=a, scalar=1.0, in1=at(vT[:, GAIN_AT[n]:], (1, 8), (0, 9)), op0=ALU.add, op1=ALU.mult
                    ).then_inc(N.mods_ready, 1)
                dve.wait_ge(N.mods_ready, n + 1)

            def norm(n):
                dve.wait_ge(N.ssq_ready, n + 1)
                r = sq[:, 0, :]
                ts(r, bank[6][:, 0:T], 1.0 / D, EPS, ALU.mult, ALU.add).then_inc(N.r_ready, 1)
                dve.wait_ge(N.rt_ready, n + 1)
                rcp(r, r).then_inc(N.r_ready, 1)
                dve.wait_ge(N.r_ready, 2 * n + 2)
                for k in range(KC):
                    stt(out=hT[:, k, 0:TP], in0=xT[:, k, 0:TP], scalar=mods[:, n, 8 + k, 0:1], in1=r[:, 0:TP],
                        op0=ALU.mult, op1=ALU.mult).then_inc(N.h_mul, 1)
                hs = hT[:, :, TP:T]
                then(tt(hs, xT[:, :, TP:T], mods[:, n, 8:16, 1:9], ALU.mult))
                then(tt(hs, hs, at(r[:, TP:T], (0, 8), (1, 8)), ALU.mult))
                tt(hs, hs, mods[:, n, 0:8, 1:9], ALU.add).then_inc(N.hs_ready, 1)

            def add_out(n, src, k, gate, t8):
                stt(out=xT[:, k, 0:TP], in0=src[:, 0:TP], scalar=gate[:, 0:1],
                    in1=xT[:, k, 0:TP], op0=ALU.mult, op1=ALU.add)
                tt(t8, src[:, TP:T], gate[:, 1:9], ALU.mult).then_inc(N.out_free, 1)

            def add_samples(n, count):
                dve.wait_ge(N.out_free, count)
                tt(xT[:, :, TP:T], xT[:, :, TP:T], tmp8x, ALU.add).then_inc(N.x_ready, 1)
                dve.wait_ge(N.x_ready, n + 1)

            tmp8x = cT[:, :, 0:8]

            for u in range(KVS):
                dve.sem_inc(kv_free[u], 1)
            dve.sem_inc(N.scored, 1)
            dve.wait_ge(N.small_tr, 1)
            cp(vT[:], bank[1][:, 0:136])
            cp(posT, bank[1][:, 136:168]).then_inc(N.small_ev, 1)
            dve.wait_ge(N.c_tr, 1)
            cp(cT[:].rearrange("p k j -> p (k j)"), bank[0][:, 0:72]).then_inc(N.c_ev, 1)
            dve.wait_ge(N.small_ev, 1)
            mods_evac(0)
            norm(0)
            dve.wait_ge(N.bias_mm, 1)
            cp(tz, bank[4][0:16, 0:384])
            cp(at(biasP, (64, 2), (8, 8), (1, 8)), at(bank[5][:, 0:128], (8, 2), (16, 8), (1, 8)))
            cp(biasC, bank[5][:, 128:136])
            cp(biasO, bank[5][0:8, 136:152])
            for par in range(2):
                last = cp(at(biasCP[:, 64 * par:], (32, 2), (8, 4), (1, 8)), at(bank[5][:, 152 + par:], (64, 2), (2, 4), (8, 8)))
            last.then_inc(N.bias_ev, 1)
            cp(s4.rearrange("p (b i) -> p b i", b=8), at(ident[0:8, 0:8], (1, 8), (0, 32)))

            def head_norms(zv, ssv, rows, tiles, ss_sem, std_sem, out_sem, sq_cols):
                for t in range(tiles):
                    off = 0
                    for c0, nh, _ in GROUPS:
                        zc = zv(c0, nh * 64, t)
                        last = tt(sqf[0:rows, off:off + nh * 64], zc, zc, ALU.mult)
                        off += nh * 64
                    then(last)
                    then(red(ssv[:, 28 * t:28 * t + 28], sqf[0:rows, 0:1792].rearrange("p (h d) -> p h d", d=64), AX, ALU.add))
                ts(ssv, ssv, 1.0 / HD, EPS, ALU.mult, ALU.add).then_inc(ss_sem, 1)
                dve.wait_ge(std_sem, 1)
                then(rcp(ssv, ssv))

            zf = lambda c0, w, t: z[:, t, c0:c0 + w]
            zsf = lambda c0, w, t: zs[:, c0:c0 + w]
            dve.wait_ge(N.z_ev, 18)
            head_norms(zsf, sss, TS, 1, N.zs_ss, N.zs_std, None, None)
            for c0, nh, off in GROUPS:
                v = zs[:, c0:c0 + nh * 64].rearrange("p (h d) -> p h d", d=64)
                last = tt(v, v, at(sss[:, off:], (1, nh), (0, 64)), ALU.mult)
            then(last)
            for c0, nh, g in GAINS:
                v = zs[:, c0:c0 + nh * 64].rearrange("p (h d) -> p h d", d=64)
                last = tt(v, v, at(qkg[0:8, g, :], (0, nh), (1, 64)), ALU.mult)
            last.then_inc(N.zs_normed, 1)
            dve.wait_ge(N.zs_normed, 1)
            tt(sqf[0:8, 0:512], zs[:, MQ:MQ + 512], zs[:, MK:MK + 512], ALU.mult)
            for i, c0 in enumerate((KSEL, KWIN)):
                last = tt(sqf[0:8, 512 + 512 * i:1024 + 512 * i].rearrange("p (k g d) -> p k g d", k=2, g=4),
                          zs[:, NQ:NQ + 512].rearrange("p (k g d) -> p k g d", k=2, g=4),
                          at(zs[:, c0:], (64, 2), (0, 4), (1, 64)), ALU.mult)
            then(last)
            then(red(sss[:, 0:24], sqf[0:8, 0:1536].rearrange("p (h d) -> p h d", d=64), AX, ALU.add))
            stt(out=sss[:, 0:8], in0=sss[:, 0:8], scalar=SCALE, in1=biasO[:, 0:8], op0=ALU.mult, op1=ALU.add)
            then(stt(out=at(sss[:, 8:], (8, 2), (1, 8)), in0=at(sss[:, 8:], (8, 2), (1, 8)), scalar=SCALE,
                     in1=at(biasO[:, 8:], (0, 2), (1, 8)), op0=ALU.mult, op1=ALU.add))
            for br in range(3):
                last = tt(own[:, 64 * br:64 * br + 64].rearrange("p (b h) -> p b h", b=8), at(sss[:, 8 * br:], (0, 8), (1, 8)),
                          cst[0:8, C_OM:C_OM + 64].rearrange("p (b h) -> p b h", b=8), ALU.add)
            then(last)
            head_norms(zf, ss, P, 2, N.z_ss, N.z_std, None, None)
            for c0, nh, off in GROUPS:
                v = z[:, :, c0:c0 + nh * 64].rearrange("p t (h d) -> p t h d", d=64)
                last = tt(v, v, at(ss[:, off:], (28, 2), (1, nh), (0, 64)), ALU.mult)
            then(last)
            for c0, nh, g in GAINS:
                v = z[:, :, c0:c0 + nh * 64].rearrange("p t (h d) -> p t h d", d=64)
                last = tt(v, v, at(qkg[:, g, :], (0, 2), (0, nh), (1, 64)), ALU.mult)
            last.then_inc(N.z_normed, 1)
            dve.wait_ge(N.small_tr, 2)
            then(tt(gtmp.rearrange("p (h j) -> p h j", j=3), bank[6][0:64, 0:24].rearrange("p (h j) -> p h j", j=3),
                    at(cst[0:64, C_DM:], (1, 8), (0, 3)), ALU.mult))
            red(gcol, at(gtmp, (1, 3), (3, 8)), AX, ALU.add).then_inc(N.small_ev, 1)

            dve.wait_ge(N.z_normed, 1)
            dve.wait_ge(N.q_bc_ev, 8)
            sraw_b = s_raw.rearrange("p (b c) -> p b c", b=8)
            with dve.Fori(0, TS) as b:
                for pg in range(PAGES):
                    dve.wait_ge(kv_full[pg], b * 16 + kv_full_value(KV_MK + pg))
                    if pg % 2 == 0:
                        dve.wait_ge(N.scored, b * 4 + pg // 2 + 1)
                    tt(prod[:, 512 * (pg % 2):512 * (pg % 2) + 512], kv[:, pg, :], qb[:, DS(b, 1), :].rearrange("p b c -> p (b c)"),
                       ALU.mult).then_inc(kv_free[pg], 1)
                    if pg % 2:
                        dve.wait_ge(kv_free[pg], b + KV_MK // KVS + 2)
                        last = red(sraw_b[:, DS(b, 1), 8 * (pg - 1):8 * (pg + 1)].rearrange("p b c -> p (b c)"),
                                   prod.rearrange("p (h d) -> p h d", d=64), AX, ALU.add)
                        last.then_inc(N.scored, 1)
            dve.wait_ge(N.scored, 33)
            cp(m1[:, 0:1], s_raw[:, 0:1]).then_inc(N.moba_scored, 1)

            dve.wait_ge(N.cmp2_mm, 1)
            cp(kvp, bank[4][0:8, 64:320])
            then(cp(kvc, bank[5][:, 0:512]))
            tt(sqf[:, 0:256], kvc[:, 0:256], kvc[:, 0:256], ALU.mult)
            then(tt(sqf[0:8, 256:384], kvp[:, 0:P], kvp[:, 0:P], ALU.mult))
            red(ssc[:, 0:4], sqf[:, 0:256].rearrange("p (h d) -> p h d", d=64), AX, ALU.add)
            then(red(ssc[0:8, 4:6], sqf[0:8, 256:384].rearrange("p (h d) -> p h d", d=64), AX, ALU.add))
            ts(ssc[:, 0:4], ssc[:, 0:4], 1.0 / HD, EPS, ALU.mult, ALU.add)
            ts(ssc[0:8, 4:6], ssc[0:8, 4:6], 1.0 / HD, EPS, ALU.mult, ALU.add).then_inc(N.kc_ss, 1)
            dve.wait_ge(N.kc_std, 1)
            rcp(ssc[:, 0:4], ssc[:, 0:4])
            then(rcp(ssc[0:8, 4:6], ssc[0:8, 4:6]))
            kc4, kp2 = kvc[:, 0:256].rearrange("p (h d) -> p h d", d=64), kvp[:, 0:P].rearrange("p (h d) -> p h d", d=64)
            tt(kc4, kc4, at(ssc, (1, 4), (0, 64)), ALU.mult)
            then(tt(kp2, kp2, at(ssc[0:8, 4:], (1, 2), (0, 64)), ALU.mult))
            tt(kc4, kc4, at(qkg[:, 3, :], (0, 4), (1, 64)), ALU.mult)
            then(tt(kp2, kp2, at(qkg[0:8, 3, :], (0, 2), (1, 64)), ALU.mult))
            cp(kpd.rearrange("p (h r d) -> p h r d", h=2, r=2), at(kvp, (64, 2), (0, 2), (1, 64))).then_inc(N.kdup_ready, 1)
            dve.wait_ge(N.kcp_tr, 1)
            cp(kcTp, bank[4][:, 384:400]).then_inc(N.kcp_ev, 1)
            mods_evac(1)
            mods_evac(2)

            def logits(raw, tiles, first_page, heads):
                return stt(out=s_log[:, 0:64 * tiles].rearrange("p (b c) -> p b c", b=8), in0=raw.rearrange("p (b c) -> p b c", b=8),
                           scalar=SCALE, in1=at(biasP[:, 64 * heads + 8 * first_page:], (0, 8), (1, 8 * tiles)),
                           op0=ALU.mult, op1=ALU.add)

            g4, e4, w4 = spt[:, 0:256], spt[:, 256:512], spt[:, 512:768]
            dve.wait_ge(N.gate_sum, 1)
            then(red(g4, at(bank[0], (16, 32), (1, 8), (8, 2)), AX, ALU.add))
            then(red(m1, at(g4, (32, 8), (1, 8), (8, 4)), AX, ALU.min))
            then(tt(e4.rearrange("p (b n h) -> p b n h", b=8, n=4), g4.rearrange("p (b n h) -> p b n h", b=8, n=4),
                    at(m1, (8, 8), (0, 4), (1, 8)), ALU.is_equal))
            nidx = at(cst[:, C_NI:], (0, 8), (1, 4), (0, 8))
            then(tt(w4.rearrange("p (b n h) -> p b n h", b=8, n=4), e4.rearrange("p (b n h) -> p b n h", b=8, n=4), nidx, ALU.mult))
            then(red(m1, at(w4, (32, 8), (1, 8), (8, 4)), AX, ALU.max))
            then(tt(e4.rearrange("p (b n h) -> p b n h", b=8, n=4), at(m1, (8, 8), (0, 4), (1, 8)), nidx, ALU.is_equal))
            ts(e4, e4, NEG, None, ALU.mult)
            then(logits(s_raw, 8, 0, 0))
            then(tt(at(s_log, (16, 32), (8, 2), (1, 8)), at(s_log, (16, 32), (8, 2), (1, 8)), at(e4, (8, 32), (0, 2), (1, 8)), ALU.add))

            def soft(br, src, tiles, mine):
                if tiles:
                    red(m1, at(src, (8 * tiles, 8), (1, 8), (8, tiles)), AX, ALU.max).then_inc(N.mx_in, 1)
                dve.wait_ge(N.mx_tr, br + 1)
                then(red(mx, bank[2][0:64, 0:P + (8 if mine is not None else 0)], AX, ALU.max))
                ts(diag, ident[0:64, 0:64], mx[:, 0:1], None, ALU.mult).then_inc(N.mx_diag, 1)
                dve.wait_ge(N.mx_bc, br + 1)
                if tiles:
                    v = at(src, (8 * tiles, 8), (8, tiles), (1, 8))
                    tt(v, v, at(bank[3], (8, 8), (0, tiles), (1, 8)), ALU.subtract)
                    tt(mine, mine, bank[3][0:8, 0:64], ALU.subtract).then_inc(N.log_ready, 1)
                else:
                    tt(src, src, bank[3][:, 0:64], ALU.subtract).then_inc(N.log_ready, 1)
                dve.wait_ge(N.p_exp, br + 1)
                if tiles:
                    for half in range(2):
                        last = red(lsum[:, 32 * half:32 * half + 32].rearrange("p (b h) -> p b h", b=4),
                                   at(pbuf[:, 1024 * half:], (264, 4), (1, 8), (32, tiles)), AX, ALU.add)
                    last.then_inc(N.p_ready, 1)
                else:
                    ts(m1[:, 0:1], m1[:, 0:1], 0.0, None, ALU.mult).then_inc(N.p_ready, 1)

            dve.wait_ge(N.mm_done, 4 * (SEQ["cmp_p"] + 2))
            then(nc.vector.memset(pbuf[:, 0:2048], 0.0))
            soft(0, s_log, 8, own[:, 0:64])

            dve.wait_ge(N.q_bc, 18)
            k4 = lambda ap: ap.rearrange("p (k d) -> p k d", k=2)
            for half in range(2):
                last = tt(prod[:, 512 * half:512 * half + 512].rearrange("p (k g d) -> p k g d", k=2, g=4),
                          at(kvc[:, P * half:], (64, 2), (0, 4), (1, 64)),
                          bank[half][:, 0:512].rearrange("p (k g d) -> p k g d", k=2, g=4), ALU.mult)
            last.then_inc(N.cw_made, 1)
            dve.wait_ge(N.cw_made, 1)
            then(red(cw, prod.rearrange("p (h d) -> p h d", d=64), AX, ALU.add))
            then(stt(out=cw.rearrange("p (a h) -> p a h", a=2), in0=cw.rearrange("p (a h) -> p a h", a=2), scalar=SCALE,
                     in1=at(biasC, (0, 2), (1, 8)), op0=ALU.mult, op1=ALU.add))
            then(tt(s_cs.rearrange("p (a b h) -> p a b h", a=2, b=4), at(cw, (8, 2), (0, 4), (1, 8)),
                    at(cst[:, C_AM:], (0, 2), (1, 4), (0, 8)), ALU.add))

            def pair_log(i):
                dve.wait_ge(N.pr_s, i + 1)
                if i >= 2:
                    dve.wait_ge(N.pr_tr, i - 1)
                buf = sps[i % 2].rearrange("p (a c) -> p a c", a=2)
                head, per_row = (2 * i, 256) if i < 4 else (i - 4, 0)
                b2 = lambda n: at(bias[:, head, n - 1:], (per_row, 2), (-1, n))
                stt(out=buf[:, :, P:384], in0=psum[:, 0:2, P:384], scalar=-SCALE, in1=b2(256), op0=ALU.mult, op1=ALU.subtract)
                then(stt(out=buf[:, :, 0:P], in0=psum[:, 0:2, 0:P], scalar=-SCALE, in1=b2(P), op0=ALU.mult, op1=ALU.subtract))
                nm = nmin[:, 4 * (i % 2):4 * (i % 2) + 4]
                red(at(nm, (2, 2)), buf[:, :, 0:P], AX, ALU.min)
                red(at(nm[:, 1:], (2, 2)), buf[:, :, P:384], AX, ALU.min).then_inc(N.pr_log, 1)

            def pair_scale(i):
                dve.wait_ge(N.pr_exp, i + 1)
                w = wrow[:, 4 * (i % 2):4 * (i % 2) + 4]
                then(rcp(w, lrow[:, 4 * (i % 2):4 * (i % 2) + 4]))
                if i >= 4:
                    then(tt(w.rearrange("p (a t) -> p a t", a=2), w.rearrange("p (a t) -> p a t", a=2),
                            at(gates[:, 3 * (i - 4) + 1:], (1, 2), (24, 2)), ALU.mult))
                buf = sps[i % 2].rearrange("p (a c) -> p a c", a=2)
                tt(buf[:, :, 0:P], buf[:, :, 0:P], at(w, (2, 2), (0, P)), ALU.mult)
                tt(buf[:, :, P:384], buf[:, :, P:384], at(w[:, 1:], (2, 2), (0, 256)), ALU.mult).then_inc(N.pr_p, 1)

            def pair_steps(first, end):
                for i in range(first, end + 1):
                    if i < end:
                        pair_log(i)
                    if i > first:
                        pair_scale(i - 1)

            dve.wait_ge(N.bias_back, 16)
            dve.wait_ge(N.z_stored, 16 * 6)
            pair_steps(0, 4)

            def weights(br):
                dve.wait_ge(N.l_done, br + 1)
                dve.wait_ge(N.pv_done, br + 1)
                then(ts(lrec, bank[4][0:64, 0:1], 1e-30, None, ALU.max))
                then(rcp(lrec, lrec))
                if br:
                    then(tt(lrec, lrec, gcol[:, br - 1:br], ALU.mult))

            def turned(n):
                dve.wait_ge(N.osum_mm, n + 1)
                cp(hT[:, 4 * n:4 * n + 4, TP:T], bank[2][:, 0:32].rearrange("p (c b) -> p c b", c=4)).then_inc(N.oTs_ready, 1)

            weights(0)
            stt(out=oacc.rearrange("p (h d) -> p h d", d=64), in0=bank[5][0:64, 0:512].rearrange("p (h d) -> p h d", d=64),
                scalar=lrec[:, 0:1], in1=at(cst[0:64, C_DM:], (1, 8), (0, 64)), op0=ALU.mult, op1=ALU.mult).then_inc(N.osum_ready, 1)
            turned(0)

            for src, c0 in enumerate((KSEL, KWIN)):
                for t in range(2):
                    last = cp(zdup[:, t, src].rearrange("p h (r d) -> p h r d", r=2), at(z[:, t, c0:], (64, 2), (0, 2), (1, 64)))
            last.then_inc(N.zdup_ready, 1)
            dve.wait_ge(N.cp_mm, 1)
            then(stt(out=s_cp.rearrange("p (a c) -> p a c", a=2), in0=psum[:, 0:2, 0:64], scalar=SCALE,
                     in1=biasCP.rearrange("p (a c) -> p a c", a=2), op0=ALU.mult, op1=ALU.add))
            s3 = s_cp.rearrange("p (i n) -> p i n", n=8)
            then(red(m16, s3, AX, ALU.max))
            then(ts(m16, m16, -1e20, None, ALU.max))
            tt(s3, s3, at(m16, (1, 16), (0, 8)), ALU.subtract).then_inc(N.cp_log, 1)
            dve.wait_ge(N.cp_exp, 1)
            then(red(l16, s3, AX, ALU.add))
            then(ts(l16, l16, 1e-30, None, ALU.max))
            then(rcp(l16, l16))
            then(tt(l16.rearrange("p (a t h) -> p a t h", a=2, t=2), l16.rearrange("p (a t h) -> p a t h", a=2, t=2),
                    at(gates, (3, 2), (24, 2), (6, 4)), ALU.mult))
            tt(s3, s3, at(l16, (1, 16), (0, 8)), ALU.mult).then_inc(N.cp_ready, 1)
            dve.wait_ge(N.q_bc_ev, 16)

            def grouped(dst, slot, g, q):
                return tt(dst.rearrange("p (k g d) -> p k g d", k=2, g=4), at(kv[:, slot, P * g:], (64, 2), (0, 4), (1, 64)),
                          q.rearrange("p (k g d) -> p k g d", k=2, g=4), ALU.mult)

            with dve.Fori(0, 2) as r:
                for u in range(KVS):
                    dve.wait_ge(kv_full[u], r * 64 + kv_full_value(KV_SK + u))
                    q = qb[:, DS(r * 4 + u // 2, 1), :].rearrange("p b c -> p (b c)")
                    for g in range(4):
                        if g % 2 == 0:
                            dve.wait_ge(N.scored, r * 24 + 33 + 3 * u + g)
                        ins = grouped(prod[:, 512 * (g % 2):512 * (g % 2) + 512], u, g, q)
                        if g == 3:
                            ins.then_inc(kv_free[u], 1)
                            dve.wait_ge(kv_free[u], r + (KV_SK + u) // KVS + 2)
                        elif g == 1:
                            ins.then_inc(N.scored, 1)
                            dve.wait_ge(N.scored, r * 24 + 33 + 3 * u + 1)
                        if g % 2:
                            c = 32 * (u % 2) + 8 * (g - 1)
                            red(sraw_b[:, DS(r * 4 + u // 2, 1), c:c + 16].rearrange("p b c -> p (b c)"),
                                prod.rearrange("p (h d) -> p h d", d=64), AX, ALU.add).then_inc(N.scored, 1)
            dve.wait_ge(N.scored, 81)
            for b in range(TS):
                dve.wait_ge(kv_full[b], kv_full_value(KV_WK + b))
                for g in range(4):
                    ins = grouped(prod[:, 512 * (g % 2):512 * (g % 2) + 512], b, g, qb[:, b, :])
                    if g == 3:
                        ins.then_inc(kv_free[b], 1)
                        dve.wait_ge(kv_free[b], (KV_WK + b) // KVS + 2)
                    elif g == 1:
                        then(ins)
                    if g % 2:
                        then(red(s_win[:, 32 * b + 8 * (g - 1):32 * b + 8 * (g + 1)], prod.rearrange("p (h d) -> p h d", d=64), AX, ALU.add))

            def nsa_out(br):
                weights(br)
                head = otmp[:, 0:P]
                then(ts(head, bank[5][0:64, 0:P], lrec[:, 0:1], None, ALU.mult))
                o3 = (oacc if br == 1 else obr).rearrange("p (k g d) -> p k g d", k=2, g=4)
                then(tt(o3, at(head, (64, 2), (0, 4), (1, 64)), at(cst[0:64, C_DM:], (4, 2), (1, 4), (0, 64)), ALU.mult))
                if br > 1:
                    ins = tt(oacc, oacc, obr, ALU.add)
                    if br == 3:
                        ins.then_inc(N.osum_ready, 1)
                    else:
                        then(ins)

            mods_evac(3)
            ts(m1[:, 0:1], m1[:, 0:1], 0.0, None, ALU.mult).then_inc(N.mx_in, 1)
            soft(1, s_cs, 0, None)
            nsa_out(1)
            then(logits(s_raw, 8, 0, 1))
            soft(2, s_log, 8, own[:, 64:128])
            dve.wait_ge(N.bias_back, 32)
            pair_steps(4, 12)
            nsa_out(2)
            then(logits(s_win, 4, 4, 1))
            soft(3, s_log, 4, own[:, 128:192])
            nsa_out(3)
            turned(1)
            def static_out(n, k, mm_value, src):
                dve.wait_ge(N.mm_done, mm_value)
                add_out(n, src, k, mods[:, n, 16 + k], tmp8x[:, k, :])

            for k in range(KC):
                static_out(0, k, 4 * SEQ["w_out"] + k + 1, bank[k % 4])
            add_samples(0, 8)
            norm(1)

            def squares(layer):
                with dve.Fori(0, 2) as it:
                    for j in range(4):
                        dve.wait_ge(N.relu_ev, it * 16 + 36 * layer + 4 * j + 8)
                        v = actT[:, DS(it * 16 + 4 * j, 4), :]
                        tt(v, v, v, ALU.mult).then_inc(N.act_ready, 1)

            def mlp_out(n, layer):
                with dve.Fori(0, 2) as it:
                    for m in range(4):
                        dve.wait_ge(N.mm_done, it * 16 + 4 * SEQ["w2_%d" % layer] + 8 * (m // 2) + 6 + 2 * (m % 2))
                        src, k = psum[:, m, :], DS(it * 4 + m, 1)
                        stt(out=xT[:, k, 0:TP].rearrange("p k t -> p (k t)"), in0=src[:, 0:TP],
                            scalar=mods[:, n, DS(it * 4 + 16 + m, 1), 0:1].rearrange("p k t -> p (k t)"),
                            in1=xT[:, k, 0:TP].rearrange("p k t -> p (k t)"), op0=ALU.mult, op1=ALU.add)
                        tt(tmp8x[:, k, :].rearrange("p k t -> p (k t)"), src[:, TP:T],
                           mods[:, n, DS(it * 4 + 16 + m, 1), 1:9].rearrange("p k t -> p (k t)"), ALU.mult).then_inc(N.out_free, 1)

            sv = lambda i: st[:, i, :]
            dve.wait_ge(N.s5_rows_loaded, 64)
            cp(s5row[:, 2, :].rearrange("p (j n) -> p j n", j=2), at(s5dt, (1, 2), (0, 64))).then_inc(N.s5_rows_made, 1)
            dve.wait_ge(N.s5_rows_tr, 1)
            cp(st[:, 0:3, :].rearrange("p i q -> p (i q)"), bank[0][:, 0:96])
            cp(h0.rearrange("p b r q -> p (b r q)"), bank[1][:, 0:512]).then_inc(N.s5_rows_ev, 1)
            dve.wait_ge(N.s5_dt, 1)
            tt(sv(4), sv(3), sv(0), ALU.mult)
            then(tt(sv(5), sv(3), sv(1), ALU.mult))
            then(ts(sv(6), sv(5), 0.15915494309189535, ROUND, ALU.mult, ALU.add))
            then(ts(sv(6), sv(6), ROUND, None, ALU.subtract))
            then(stt(out=sv(7), in0=sv(6), scalar=-TWO_PI_A, in1=sv(5), op0=ALU.mult, op1=ALU.add))
            then(stt(out=sv(7), in0=sv(6), scalar=-TWO_PI_B, in1=sv(7), op0=ALU.mult, op1=ALU.add))
            then(stt(out=sv(7), in0=sv(6), scalar=-TWO_PI_C, in1=sv(7), op0=ALU.mult, op1=ALU.add))
            ts(sv(7), sv(7), 3.1415925, -3.1415925, ALU.min, ALU.max).then_inc(N.s5_ang, 1)
            dve.wait_ge(N.s5_sin, 1)
            then(tt(sv(11), sv(10), sv(10), ALU.mult))
            then(ts(sv(11), sv(11), -2.0, 1.0, ALU.mult, ALU.add))
            tt(sv(12), sv(8), sv(11), ALU.mult)
            then(tt(sv(13), sv(8), sv(9), ALU.mult))
            tt(sv(14), sv(0), sv(0), ALU.mult)
            then(tt(sv(17), sv(1), sv(1), ALU.mult))
            then(tt(sv(14), sv(14), sv(17), ALU.add))
            rcp(sv(14), sv(14))
            then(ts(sv(18), sv(12), -1.0, None, ALU.add))
            tt(sv(15), sv(18), sv(0), ALU.mult)
            tt(sv(17), sv(13), sv(1), ALU.mult)
            tt(sv(16), sv(13), sv(0), ALU.mult)
            then(tt(sv(18), sv(18), sv(1), ALU.mult))
            tt(sv(15), sv(15), sv(17), ALU.add)
            then(tt(sv(16), sv(16), sv(18), ALU.subtract))
            tt(sv(15), sv(15), sv(14), ALU.mult)
            then(tt(sv(16), sv(16), sv(14), ALU.mult))
            dve.wait_ge(N.s5_loaded, 16 * (S5_LOADS - 4))
            fre, fim = at(sv(15), (1, 32), (0, 16)), at(sv(16), (1, 32), (0, 16))
            scr = bdia[:, 0].rearrange("p q j c -> p (q j c)")[:, 0:512].rearrange("p (q c) -> p q c", c=16)
            tt(bbar[:, 0], braw[:, 0], fre, ALU.mult)
            tt(bbar[:, 1], braw[:, 1], fre, ALU.mult)
            then(tt(scr, braw[:, 1], fim, ALU.mult))
            then(tt(bbar[:, 0], bbar[:, 0], scr, ALU.subtract))
            then(tt(scr, braw[:, 0], fim, ALU.mult))
            then(tt(bbar[:, 1], bbar[:, 1], scr, ALU.add))
            for r in range(2):
                for j in range(2):
                    last = ts(bdia[:, r, :, j, :], bbar[:, r], cst[:, C_MB + j:C_MB + j + 1], None, ALU.mult)
            last.then_inc(N.s5_bd, 1)
            then(nc.vector.memset(cosT[:, :, 0:1], 1.0))
            then(nc.vector.memset(sinT[:, :, 0:1], 0.0))
            cp(sv(19), sv(11))
            then(cp(sv(20), sv(9)))
            tmpa = BT.rearrange("p k r n -> p (k r n)")
            s, a = 1, 19
            while s <= SEG // 2:
                cs, sn = at(sv(a), (1, NT), (0, s)), at(sv(a + 1), (1, NT), (0, s))
                for q0, qn in (((0, NT),) if s < 64 else ((0, 16), (16, 16))):
                    qs = slice(q0, q0 + qn)
                    x1 = at(tmpa, (s, qn), (1, s))
                    x2 = at(tmpa[:, 1024:], (s, qn), (1, s))
                    csq, snq = at(st[:, a, q0:], (1, qn), (0, s)), at(st[:, a + 1, q0:], (1, qn), (0, s))
                    tt(cosT[:, qs, s:2 * s], cosT[:, qs, 0:s], csq, ALU.mult)
                    tt(sinT[:, qs, s:2 * s], sinT[:, qs, 0:s], csq, ALU.mult)
                    tt(x1, sinT[:, qs, 0:s], snq, ALU.mult)
                    then(tt(x2, cosT[:, qs, 0:s], snq, ALU.mult))
                    tt(cosT[:, qs, s:2 * s], cosT[:, qs, s:2 * s], x1, ALU.subtract)
                    then(tt(sinT[:, qs, s:2 * s], sinT[:, qs, s:2 * s], x2, ALU.add))
                b = 40 - a
                tt(sv(b), sv(a), sv(a), ALU.mult)
                tt(sv(17), sv(a + 1), sv(a + 1), ALU.mult)
                then(tt(sv(b + 1), sv(a), sv(a + 1), ALU.mult))
                tt(sv(b), sv(b), sv(17), ALU.subtract)
                then(ts(sv(b + 1), sv(b + 1), 2.0, None, ALU.mult))
                s, a = 2 * s, b
            jump = a
            cp(sv(18)[:, 0:1], sv(17)[:, 0:1]).then_inc(N.s5_tables, 1)
            squares(0)
            dve.wait_ge(N.s5_c_tr, 1)
            for r in range(2):
                for hb in range(2):
                    src = bank[4 + 2 * r + hb][:, 0:512].rearrange("p (a c) -> p a c", c=16)
                    mask = at(cst[:, C_MC:], (0, 4), (1, 8), (0, 16))
                    dst = CT[:, 0 if r == 0 else 2, 4 * hb:4 * hb + 4, :]
                    last = tt(dst.rearrange("p k (g c) -> p k g c", c=16), bank[4 + 2 * r + hb][:, 0:512].rearrange("p (k g c) -> p k g c", k=4, g=8), mask, ALU.mult)
            then(last)
            ts(CT[:, 1], CT[:, 0], -1.0, None, ALU.mult)
            ts(CT[:, 2], CT[:, 2], -1.0, None, ALU.mult).then_inc(N.s5_c_ev, 1)
            mlp_out(1, 0)
            add_samples(1, 16)
            norm(2)

            dve.wait_ge(N.us_mm, 1)
            bq = lambda i: at(sv(i), (0, 8), (1, NT))
            hre, him = h0[:, :, 0, :], h0[:, :, 1, :]
            xre, xim = xs5[:, :, 0, :], xs5[:, :, 1, :]
            ta = t1.rearrange("p (i b q) -> p i b q", i=2, b=8)
            tt(xre, hre, bq(12), ALU.mult)
            tt(xim, him, bq(12), ALU.mult)
            tt(ta[:, 0], him, bq(13), ALU.mult)
            then(tt(ta[:, 1], hre, bq(13), ALU.mult))
            tt(xre, xre, ta[:, 0], ALU.subtract)
            then(tt(xim, xim, ta[:, 1], ALU.add))
            for r, x in ((0, xre), (1, xim)):
                v = x.rearrange("p b (k e) -> p b k e", e=4)
                last = tt(v, v, at(bank[4][:, 8 * r:], (1, 8), (16, 8), (512, 4)), ALU.add)
            last.then_inc(N.xs_ready, 1)

            def y_evac(g):
                seg, k = divmod(g, 8)
                dve.wait_ge(N.y_mm, 2 * (g + 1))
                stt(out=yT[:, k, SEG * seg:SEG * seg + SEG], in0=hT[:, k, SEG * seg:SEG * seg + SEG], scalar=vT[:, 112 + k:113 + k],
                    in1=bank[4 + g % 2][:, 0:SEG], op0=ALU.mult, op1=ALU.add).then_inc(N.y_ev, 1)

            def cmul(dst, src, i):
                re, im, c, s_ = src[:, 0:32], src[:, 32:64], sv(i), sv(i + 1)
                tt(t5s[:, 0:32], re, c, ALU.mult)
                tt(t5s[:, 32:64], im, s_, ALU.mult)
                tt(t5s[:, 64:96], re, s_, ALU.mult)
                then(tt(t5s[:, 96:128], im, c, ALU.mult))
                tt(dst[:, 0:32], t5s[:, 0:32], t5s[:, 32:64], ALU.subtract)
                return tt(dst[:, 32:64], t5s[:, 64:96], t5s[:, 96:128], ALU.add)

            for n in range(32):
                seg, i = divmod(n, 16)
                dve.wait_ge(N.u_mm, n + 1)
                u3 = psum[:, 2 * (n % 2):2 * (n % 2) + 2, 0:256].rearrange("p q (r t) -> p q r t", r=2)
                c2 = at(cosT[:, 2 * i:2 * i + 2, :], (SEG, 2), (0, 2), (1, SEG))
                s2 = at(sinT[:, 2 * i:2 * i + 2, :], (SEG, 2), (0, 2), (1, SEG))
                q4 = lambda ap: ap.rearrange("p (q r t) -> p q r t", q=2, r=2)
                tt(q4(t1), u3, c2, ALU.mult)
                tt(q4(t2), u3, s2, ALU.mult).then_inc(N.u_free, 1)
                dve.wait_ge(N.u_free, n + 1)
                tt(q4(zin)[:, :, 0], q4(t1)[:, :, 0], q4(t2)[:, :, 1], ALU.add)
                then(tt(q4(zin)[:, :, 1], q4(t1)[:, :, 1], q4(t2)[:, :, 0], ALU.subtract))
                if n >= 2:
                    dve.wait_ge(N.zp_done, 2 * (n - 1))
                for e in range(2):
                    for r in range(2):
                        q = 2 * i + e
                        c = 256 * e + SEG * r
                        last = nc.vector.tensor_tensor_scan(
                            out=zcur[:, n % 2, c:c + SEG], data0=st[:, 8, q:q + 1].to_broadcast([P, SEG]), data1=zin[:, c:c + SEG],
                            initial=0.0 if seg == 0 else zinit[:, 32 * r + q:32 * r + q + 1], op0=ALU.mult, op1=ALU.add)
                last.then_inc(N.zc_ready, 1)
                dve.wait_ge(N.zc_ready, n + 1)
                then(cp(at(zlast[:, 2 * i:], (1, 2), (32, 2)), at(zcur[:, n % 2, SEG - 1:], (256, 2), (SEG, 2))))
                if n == 15:
                    then(cmul(zinit, zlast, jump))
                if n == 0:
                    dve.wait_ge(N.ys_mm, 1)
                    ys = yT[:, :, TP:T]
                    then(tt(ys, hT[:, :, TP:T], at(vT[:, 112:], (1, 8), (0, 8)), ALU.mult))
                    tt(ys, ys, bank[6][:, 0:64].rearrange("p (k b) -> p k b", k=8), ALU.add).then_inc(N.y_ev, 1)
                if n >= 3 and n % 2:
                    y_evac((n - 3) // 2)
            cp(sv(19), cosT[:, :, SEG - 1:SEG].rearrange("p q t -> p (q t)"))
            then(cp(sv(20), sinT[:, :, SEG - 1:SEG].rearrange("p q t -> p (q t)")))
            cmul(xlast, zlast, 19).then_inc(N.fin_ready, 1)
            y_evac(15)

            for n in range(8):
                dve.wait_ge(N.sig_ready, n + 1)
                b = 4 * (n // 2 % 2) + 2 * (n % 2)
                then(tt(glu[:, n % 2, :], bank[b][:, 0:T], sig[:, n % 2, :], ALU.mult))
                add_out(2, glu[:, n % 2, :], n, mods[:, 2, 16 + n], tmp8x[:, n, :])
            add_samples(2, 24)
            norm(3)
            squares(1)
            mlp_out(3, 1)
            add_samples(3, 32)


_INS = ["x_prompt", "x_sample", "cache_moba_kv", "cache_nsa_kv", "state_nsa_win", "state_s5", "page_table",
        "c_prompt", "c_sample", "rel_bias", "attn_norm_g", "attn_ada_w", "attn_ada_b", "attn_w_in", "attn_qk_g",
        "nsa_cmp_pos", "nsa_cmp_w1", "nsa_cmp_w2", "attn_w_out", "ssm_norm_g", "ssm_ada_w", "ssm_ada_b",
        "s5_a_re", "s5_a_im", "s5_log_dt", "s5_b_re", "s5_b_im", "s5_c_re", "s5_c_im", "s5_d", "s5_w_glu",
        "mlp_norm_g", "mlp_ada_w", "mlp_ada_b", "mlp_w1", "mlp_w2"]
_OUTS = [("y_prompt", (1, 256, 1024)), ("y_sample", (8, 1, 1024)), ("moba_prompt", (256, 1024)), ("moba_sample", (8, 1024)),
         ("nsa_prompt", (256, 512)), ("nsa_sample", (8, 512)), ("win_prompt", (256, 256)), ("win_sample", (1, 8, 512, 2, 2, 64)),
         ("s5_prompt", (1, 1, 2, 64, 64)), ("s5_sample", (1, 8, 2, 64, 64))]
_SHAPES = [(1, 256, 1024), (8, 1, 1024), (1, 1, 2, 128, 2, 8, 64), (1, 8, 1, 2, 8, 64), (1, 1, 2, 128, 4, 2, 64),
           (1, 8, 1, 4, 2, 64), (1, 1, 256, 2, 2, 64), (1, 8, 512, 2, 2, 64), (1, 1, 2, 64, 64), (1, 8, 2, 64, 64)]


def _bucket(np, dist):
    n = np.maximum(dist, 0)
    large = 16 + (np.log(np.maximum(n, 1) / 16.0) / np.log(8.0) * 16).astype(np.int64)
    return np.where(n < 16, n, np.minimum(large, 31))


def _constants():
    import numpy as np

    def hot(dist, masked):
        out = np.zeros((33, dist.size), np.float32)
        out[_bucket(np, dist), np.arange(dist.size)] = 1.0
        if masked:
            out[:, dist < 0] = 0.0
            out[32, dist < 0] = NEG
        return out

    onehot = np.concatenate([
        hot(np.arange(384) - 127, True),
        hot(PAST - np.arange(PAST), False),
        hot(PAST - (CMP * (np.arange(P) % CMP + 1) - 1), False),
        hot(np.zeros(8, np.int64), False),
        np.concatenate([hot(P * t + np.arange(P) - (CMP * (n + 1) - 1), True) for t in range(2) for n in range(8)], axis=1),
    ], axis=1)
    c = np.zeros((P, C_ALL), np.float32)
    p = np.arange(P)
    c[:, C_ID:C_ID + P] = np.eye(P)
    c[:, C_MB:C_MB + 2] = p[:, None] // 64 == np.arange(2)
    c[:64, C_G:C_G + 8] = p[:64, None] // 8 == np.arange(8)
    c[:64, C_DM:C_DM + 8] = p[:64, None] % 8 == np.arange(8)
    c[:, C_AM:C_AM + 4] = np.where(p[:, None] // 32 == np.arange(4), 0.0, NEG)
    c[:, C_NI:C_NI + 4] = np.arange(4) + 1
    c[:, C_MC:C_MC + 8] = p[:, None] // 64 == np.arange(8) % 2
    c[:8, C_OM:C_OM + 64] = np.where(p[:8, None] == np.arange(64) // 8, 0.0, NEG)
    c[:8, C_GT:C_GT + 64] = p[:8, None] == np.arange(64) // 8
    return {"c_cst": c, "c_onehot": onehot, "c_one": np.ones((1, 16), np.float32)}


def kernel(**inputs):
    import numpy as np
    import concourse.bacc as bacc
    from concourse.bass_utils import run_bass_kernel_spmd

    nc = bacc.Bacc("TRN2", target_bir_lowering=False, num_devices=1)
    arrays = {"in_" + n: np.ascontiguousarray(inputs[n]) for n in _INS}
    arrays.update({"in_" + n: a for n, a in _constants().items()})
    ins = {n[3:]: nc.dram_tensor(n, a.shape, mybir.dt.from_np(a.dtype), kind="ExternalInput").ap() for n, a in arrays.items()}
    outs = {n: nc.dram_tensor("out_" + n, shape, F32, kind="ExternalOutput").ap() for n, shape in _OUTS}
    program(nc, ins, outs)
    r = run_bass_kernel_spmd(nc, [arrays], core_ids=[0]).results[0]
    return tuple(r["out_" + n].reshape(shape) for (n, _), shape in zip(_OUTS, _SHAPES))
```

```python
from contextlib import ExitStack

import concourse.bass as bass
from concourse import mybir

F32 = mybir.dt.float32
I32 = mybir.dt.int32
ALU = mybir.AluOpType
ACT = mybir.ActivationFunctionType
AX = mybir.AxisListType.X
DS = bass.DynSlice

P = 128
D = 1024
KC = D // P
TP, TS = 256, 8
T = TP + TS
PAST, PAGE = 1024, 128
PAGES = PAST // PAGE
POOL = 80
HD = 64
MOBA_H, NSA_H, KVH, GRP = 8, 8, 2, 4
IN_COLS = 2840
MQ, MK, MV, NQ, KCMP, VCMP, KSEL, VSEL, KWIN, VWIN, GATE = 0, 512, 1024, 1536, 2048, 2176, 2304, 2432, 2560, 2688, 2816
SCALE = HD ** -0.5
EPS = 1e-6
NEG = -1e30
CMP = 32
SEG = 128
NT = 32
ARENA = 28670
EARLY = 12
SMALL, S5_LOADS = 15, 12
OH_TZ, OH_PG, OH_CS, OH_OWN, OH_CP, OH_ALL = 0, 384, 1408, 1536, 1544, 3592
C_ID, C_MB, C_G, C_DM, C_AM, C_NI, C_MC, C_OM, C_GT, C_JM, C_SL, C_ALL = 0, 128, 130, 138, 146, 150, 154, 162, 226, 290, 294, 303
TWO_PI_A, TWO_PI_B, TWO_PI_C = 6.28125, 0.0019350051879882812, 3.019916050561733e-07
ROUND = 12582912.0


def at(ap, *dims):
    return bass.AP(tensor=ap.tensor, offset=ap.offset, ap=[list(ap.ap[0])] + [list(d) for d in dims])


SLOTS = 4
SEQ = dict(ada0=0, cmp=6, w_in=8, ada1=14, ada2=20, cmp_p=26, ada3=28, w_out=34, w1_0=36, w2_0=44, glu=52, w1_1=56, w2_1=64)


def panel_full(seq):
    return sum(32 if SEQ["glu"] <= n < SEQ["glu"] + 4 else 16 for n in range(seq % SLOTS, seq + 1, SLOTS))


KVS = 8
KV_CMP, KV_MK, KV_MV, KV_SK, KV_WK, KV_SV, KV_WV, KV_END = 0, 32, 96, 160, 176, 184, 200, 208


def kv_full_value(seq):
    total = 0
    for n in range(seq % KVS, seq + 1, KVS):
        total += 32 if n < KV_MK else 64 if KV_SK <= n < KV_WK or KV_SV <= n < KV_WV else 16
    return total


class Signals:

    def __init__(self, sem):
        self.small_loaded = sem("small_loaded")
        self.x_loaded = sem("x_loaded")
        self.pt_loaded = sem("pt_loaded")
        self.s5_rows_loaded = sem("s5_rows_loaded")
        self.s5_loaded = sem("s5_loaded")
        self.ones_made = sem("ones_made")
        self.tz_stored = sem("tz_stored")
        self.bias_back = sem("bias_back")
        self.mm_done = sem("mm_done")
        self.small_tr = sem("small_tr")
        self.small_ev = sem("small_ev")
        self.bias_mm = sem("bias_mm")
        self.bias_ev = sem("bias_ev")
        self.csil_ready = sem("csil_ready")
        self.c_tr = sem("c_tr")
        self.c_ev = sem("c_ev")
        self.x_tr = sem("x_tr")
        self.x_ev = sem("x_ev")
        self.sq_ready = sem("sq_ready")
        self.ssq_ready = sem("ssq_ready")
        self.rt_ready = sem("rt_ready")
        self.h_mul = sem("h_mul")
        self.h_ready = sem("h_ready")
        self.hs_ready = sem("hs_ready")
        self.mods_ready = sem("mods_ready")
        self.x_ready = sem("x_ready")
        self.z_ev = sem("z_ev")
        self.zs_normed = sem("zs_normed")
        self.z_normed = sem("z_normed")
        self.gates_ready = sem("gates_ready")
        self.z_stored = sem("z_stored")
        self.q_bc = sem("q_bc")
        self.q_bc_ev = sem("q_bc_ev")
        self.qk_tr = sem("qk_tr")
        self.qk_ev = sem("qk_ev")
        self.scored = sem("scored")
        self.moba_scored = sem("moba_scored")
        self.zdup_ready = sem("zdup_ready")
        self.cmp_tr = sem("cmp_tr")
        self.cmp_ev = sem("cmp_ev")
        self.gelu_ev = sem("gelu_ev")
        self.pb_mm = sem("pb_mm")
        self.pb_ev = sem("pb_ev")
        self.cmp2_mm = sem("cmp2_mm")
        self.kc_ss = sem("kc_ss")
        self.kc_std = sem("kc_std")
        self.kdup_ready = sem("kdup_ready")
        self.kcp_tr = sem("kcp_tr")
        self.kcp_ev = sem("kcp_ev")
        self.gate_sum = sem("gate_sum")
        self.mx_in = sem("mx_in")
        self.mx_tr = sem("mx_tr")
        self.mx_diag = sem("mx_diag")
        self.mx_bc = sem("mx_bc")
        self.log_ready = sem("log_ready")
        self.p_exp = sem("p_exp")
        self.p_ready = sem("p_ready")
        self.l_done = sem("l_done")
        self.pv_done = sem("pv_done")
        self.osum_ready = sem("osum_ready")
        self.osum_mm = sem("osum_mm")
        self.oTs_ready = sem("oTs_ready")
        self.cp_mm = sem("cp_mm")
        self.cp_log = sem("cp_log")
        self.cp_exp = sem("cp_exp")
        self.cp_ready = sem("cp_ready")
        self.cp_tr = sem("cp_tr")
        self.cp_tev = sem("cp_tev")
        self.pr_s = sem("pr_s")
        self.pr_log = sem("pr_log")
        self.pr_exp = sem("pr_exp")
        self.pr_p = sem("pr_p")
        self.pr_tr = sem("pr_tr")
        self.pr_tev = sem("pr_tev")
        self.pr_pv = sem("pr_pv")
        self.pr_oev = sem("pr_oev")
        self.relu_ev = sem("relu_ev")
        self.act_ready = sem("act_ready")
        self.out_free = sem("out_free")
        self.sig_ready = sem("sig_ready")
        self.dve_step = sem("dve_step")
        self.act_step = sem("act_step")
        self.s5_rows_made = sem("s5_rows_made")
        self.s5_rows_tr = sem("s5_rows_tr")
        self.s5_rows_ev = sem("s5_rows_ev")
        self.s5_dt = sem("s5_dt")
        self.s5_ang = sem("s5_ang")
        self.s5_sin = sem("s5_sin")
        self.s5_bd = sem("s5_bd")
        self.s5_b_tr = sem("s5_b_tr")
        self.s5_b_ev = sem("s5_b_ev")
        self.s5_c_tr = sem("s5_c_tr")
        self.s5_c_ev = sem("s5_c_ev")
        self.s5_tables = sem("s5_tables")
        self.u_mm = sem("u_mm")
        self.u_free = sem("u_free")
        self.zc_ready = sem("zc_ready")
        self.zp_done = sem("zp_done")
        self.y_mm = sem("y_mm")
        self.y_ev = sem("y_ev")
        self.gelu_ready = sem("gelu_ready")
        self.us_mm = sem("us_mm")
        self.xs_ready = sem("xs_ready")
        self.ys_mm = sem("ys_mm")
        self.fin_ready = sem("fin_ready")
        self.fin_tr = sem("fin_tr")
        self.fin_ev = sem("fin_ev")
        self.y_tr = sem("y_tr")
        self.y_out_ev = sem("y_out_ev")
        self.y_stored = sem("y_stored")
        self.r_ready = sem("r_ready")
        self.ada_row = sem("ada_row")
        self.ada_tr = sem("ada_tr")
        self.c_loaded = sem("c_loaded")
        self.win_stored = sem("win_stored")
        self.cmp_mm = sem("cmp_mm")
        self.cw_made = sem("cw_made")
        self.qs_normed = sem("qs_normed")
        self.pprod_ready = sem("pprod_ready")
        self.pprod_used = sem("pprod_used")
        self.pool_step = sem("pool_step")
        self.zs_mm = sem("zs_mm")
        self.zs_rows = sem("zs_rows")
        self.zs_sum = sem("zs_sum")
        self.head_roots = sem("head_roots")
        self.head_sums = sem("head_sums")
        self.padded_ready = sem("padded_ready")


def program(nc, I, O):
    scratch = nc.dram_tensor("toeplitz_rows", [16, 384], F32).ap()
    with ExitStack() as ctx:
        def sb(name, shape, dt=F32):
            return ctx.enter_context(nc.sbuf_tensor("sb_" + name, shape, dt))

        def sem(name):
            return ctx.enter_context(nc.semaphore(name))

        xT = sb("xT", [P, KC, T])
        hT = sb("hT", [P, KC, T])
        sq = sb("sq", [P, KC, T])
        ring = sb("ring", [P, SLOTS, 4096])
        ones = sb("ones", [P, P])
        cst = sb("cst", [P, C_ALL])
        mods = sb("mods", [P, 4, 24, 9])
        vT = sb("vT", [P, 136])
        cT = sb("cT", [P, KC, 32])
        ident = cst[:, C_ID:C_ID + 128]
        arena = sb("arena", [P, ARENA])
        pt = sb("pt", [1, 64], I32)

        used = [0]

        def take(n, rows=P):
            a = arena[0:rows, used[0]:used[0] + n]
            used[0] += n
            return a

        z = take(2 * IN_COLS).rearrange("p (t c) -> p t c", t=2)
        zs = take(IN_COLS, TS)
        kv = take(KVS * 512).rearrange("p (s c) -> p s c", s=KVS)
        pbuf = take(2304)
        qb = take(8 * 512).rearrange("p (b c) -> p b c", b=8)
        bias = take(8 * 256).rearrange("p (h k) -> p h k", h=8)
        kvc = take(512)
        qkT = take(2048)
        qkg = take(384).rearrange("p (i d) -> p i d", i=6)
        spt = take(1536)
        biasP, biasC, biasO, biasCP = take(128), take(8), take(16, 8), take(128)
        s_win, own = take(256), take(192, 8)
        m1, mx, diag, lsum, lrec = take(64), take(1, 64), take(64, 64), take(64), take(1, 64)
        gcol, gtmp = take(3, 64), take(24, 64)
        ss, sss, gates, gates_s = take(56), take(28, 8), take(48), take(24, 8)
        posT, pbias, w2c = take(32), take(2), take(128)
        kvp, kpd, kcTp, s_cs, s_cp = take(256, 8), take(256, 8), take(16), take(64), take(128)
        nmin, lrow, wrow = take(8), take(8), take(8)
        ssc, cw, m16, l16, s4 = take(8), take(16), take(16), take(16), take(256, 8)
        pcT = take(512, 8)
        assert used[0] <= ARENA, used[0]
        onehot = arena[0:33, 0:OH_ALL]
        xrow = [qb[:, 0:2, :].rearrange("p b c -> p (b c)"), qb[:, 2:4, :].rearrange("p b c -> p (b c)"),
                qb[0:TS, 4:6, :].rearrange("p b c -> p (b c)")]
        rel = qb[0:33, 6, 0:16]
        crow, csil = pbuf[0:9, 0:1024], pbuf[0:9, 1024:2048]
        vecA, vecB = pbuf[0:120, 2048:2176], pbuf[0:16, 2176:2304]
        posrow, tz = qkT[0:32, 0:128], qkT[0:16, 128:512]
        sqf = sq[:, :, :].rearrange("p k t -> p (k t)")
        prod, s_raw, s_log = sqf[:, 0:1024], sqf[:, 1024:1536], sqf[:, 1536:2048]
        hg = spt[:, 0:1056]
        pprod = spt[:, 0:1024]
        zs_part = qkT[:, 0:1024].rearrange("p (i c) -> p i c", i=2)
        hs32 = pbuf[:, 2048:2304].rearrange("p (k b) -> p k b", k=KC)
        pairs = arena[:, 0:8192]
        p_pairs = kvc
        sp_, pT = spt[:, 0:768], spt[:, 768:1536]
        sps, pTs = (sp_, z[:, 0, 0:768]), (pT, z[:, 1, 0:768])
        otmp, oacc, obr = z[0:64, 1, 768:896], z[0:64, 0, MV:MV + 512], z[0:64, 1, MV:MV + 512]
        zdup = spt[:, 0:1024].rearrange("p (t s h c) -> p t s h c", t=2, s=2, h=2)
        used[0] = 0
        actT = take(32 * T).rearrange("p (f t) -> p f t", f=32)
        cosT = take(NT * SEG).rearrange("p (q t) -> p q t", q=NT)
        sinT = take(NT * SEG).rearrange("p (q t) -> p q t", q=NT)
        BT = take(2048).rearrange("p (k r n) -> p k r n", k=8, r=2)
        CT = take(3072).rearrange("p (i k c) -> p i k c", i=3, k=8)
        h0 = take(512).rearrange("p (b r q) -> p b r q", b=8, r=2)
        xs5 = take(512).rearrange("p (b r q) -> p b r q", b=8, r=2)
        st = take(24 * 32).rearrange("p (i q) -> p i q", i=24)
        tail5 = take(ARENA - used[0])
        yT = actT[:, 0:8, :]
        braw = tail5[:, 0:1024].rearrange("p (r q c) -> p r q c", r=2, q=NT)
        bbar = tail5[:, 1024:2048].rearrange("p (r q c) -> p r q c", r=2, q=NT)
        bdia = tail5[:, 2048:4096].rearrange("p (r q j c) -> p r q j c", r=2, q=NT, j=2)
        s5row = tail5[0:32, 4096:4480].rearrange("p (i c) -> p i c", i=3)
        hrow = tail5[:, 4480:4992].rearrange("p (a c) -> p a c", a=4)
        s5dt = tail5[0:32, 4992:4994]
        craw = CT.rearrange("p i k c -> p (i k c)")[:, 0:2048].rearrange("p (r k j n) -> p r k j n", r=2, k=8, j=2)
        dbl = tail5[:, 0:4096].rearrange("p (i q t) -> p i q t", i=2, q=NT)
        t1, t2 = tail5[:, 0:512], tail5[:, 512:1024]
        zin = arena[:, 4096:5120].rearrange("p (i c) -> p i c", i=2)
        zcur = tail5[:, 1536:2560].rearrange("p (i c) -> p i c", i=2)
        pc5 = tail5[:, 2560:3584].rearrange("p (i c) -> p i c", i=2)
        ps5 = tail5[:, 3584:4608].rearrange("p (i c) -> p i c", i=2)
        hm = arena[:, 5120:5376]
        zlast, zinit, xlast = tail5[:, 4608:4672], tail5[:, 4672:4736], tail5[:, 4736:4800]
        t5s = tail5[:, 4800:5056]
        finrow = arena[:, 3200:3840].rearrange("p (i c) -> p i c", i=5)
        yrow = arena[:, 8448:8448 + 3072].rearrange("p (t c) -> p t c", t=3)
        sig = arena[:, 2112:2112 + 2 * T].rearrange("p (i t) -> p i t", i=2)
        glu = arena[:, 2640:2640 + 2 * T].rearrange("p (i t) -> p i t", i=2)

        psum = ctx.enter_context(nc.psum_tensor("psum", [P, 8, 512], F32))
        bank = [psum[:, i, :] for i in range(8)]

        N = Signals(sem)
        ring_full = [sem(f"ring_full{i}") for i in range(SLOTS)]
        kv_full = [sem(f"kv_full{i}") for i in range(KVS)]
        kv_odd = [sem(f"kv_odd{i}") for i in range(KVS)]
        kv_free = [sem(f"kv_free{i}") for i in range(KVS)]

        block = ctx.enter_context(nc.Block())

        def cmp_piece(page, u, g, e):
            return (kv[64 * g:64 * g + 64, u, :].rearrange("p (x e d) -> p x e d", x=4, e=2)[:, :, e],
                    I["cache_nsa_kv"][0].rearrange("n (q e) a h d -> n q e (a h d)", e=2)[page, :, e, 0:256].rearrange(
                        "n q (x d) -> (n q) x d", d=HD))

        @block.sync
        def _(sp):
            sp.dma_start(pt[:], I["page_table"].rearrange("b (o p) -> o (b p)", o=1)).then_inc(N.pt_loaded, 16)
            sp.dma_start(crow[0:1, :], I["c_prompt"]).then_inc(N.c_loaded, 16)
            sp.dma_start(crow[1:9, :], I["c_sample"]).then_inc(N.c_loaded, 16)
            small = [
                (cst[:], I["c_cst"]), (onehot, I["c_onehot"]), (rel[0:32, :], I["rel_bias"]), (rel[32:33, :], I["c_one"]),
                (vecA[0:24, :], I["attn_ada_b"].rearrange("a (r c) -> (a r) c", c=P)),
                (vecA[24:48, :], I["mlp_ada_b"][0].rearrange("(r c) -> r c", c=P)),
                (vecA[48:72, :], I["ssm_ada_b"].rearrange("a (r c) -> (a r) c", c=P)),
                (vecA[72:96, :], I["mlp_ada_b"][1].rearrange("(r c) -> r c", c=P)),
                (vecA[96:104, :], I["attn_norm_g"].rearrange("a (r c) -> (a r) c", c=P)),
                (vecA[104:112, :], I["ssm_norm_g"].rearrange("a (r c) -> (a r) c", c=P)),
                (vecA[112:120, :], I["s5_d"].rearrange("a (r c) -> (a r) c", c=P)),
                (vecB, I["mlp_norm_g"].rearrange("a (r c) -> (a r) c", c=P)),
                (posrow, I["nsa_cmp_pos"][0].rearrange("a (i e) d -> (a i) (e d)", e=2)),
                (w2c.rearrange("p (a d) -> p a d", a=2), I["nsa_cmp_w2"][0].rearrange("a h d -> h a d")),
                (qkg, I["attn_qk_g"][0].partition_broadcast(P)),
            ]
            assert len(small) == SMALL
            for dst, src in small:
                sp.dma_start(dst, src).then_inc(N.small_loaded, 16)
            for t in range(2):
                sp.dma_start(xrow[t], I["x_prompt"][0, t * P:(t + 1) * P, :]).then_inc(N.x_loaded, 16)
            sp.dma_start(xrow[2], I["x_sample"].rearrange("b t d -> (b t) d")).then_inc(N.x_loaded, 16)
            sp.wait_ge(N.bias_ev, 1)
            sp.dma_start(scratch, tz).then_inc(N.tz_stored, 16)
            sp.wait_ge(N.tz_stored, 16)
            toeplitz = [bass.AP(tensor=scratch.tensor, offset=h0_ * 384, ap=[[1, P], [384, 8], [1, 256]])
                        for h0_ in (0, 8)]
            sp.dma_start(bias, toeplitz[0]).then_inc(N.bias_back, 16)
            sp.wait_ge(N.pt_loaded, 16)
            moba = I["cache_moba_kv"][0].rearrange("n p a h d -> n p (a h d)")
            nsa = I["cache_nsa_kv"][0].rearrange("n p a h d -> n p (a h d)")

            def page(i):
                return DS(sp.value_load(pt[0:1, DS(i, 1)], min_val=0, max_val=POOL - 1), 1)

            def moba_units(first, col):
                with sp.Fori(0, TS) as b:
                    for pg in range(PAGES):
                        sp.wait_ge(kv_free[pg], b + first // KVS + 1)
                        sp.dma_start(kv[:, pg, :], moba[page(b * 8 + pg), :, col:col + 512].rearrange("n p c -> (n p) c")
                                     ).then_inc(kv_full[pg], 16)

            def nsa_units(first, col):
                with sp.Fori(0, 2) as r:
                    for u in range(KVS):
                        sp.wait_ge(kv_free[u], r + first // KVS + 1)
                        for g in range(4):
                            sp.dma_start(kv[:, u, g * P:(g + 1) * P],
                                         nsa[page(r * 32 + u * 4 + g), :, col:col + P].rearrange("n p c -> (n p) c")
                                         ).then_inc(kv_full[u], 16)

            def window_units(first, which):
                for b in range(TS):
                    sp.wait_ge(kv_free[b], first // KVS + 1)
                    sp.dma_start(kv[:, b, :].rearrange("p (t c) -> p t c", t=4),
                                 I["state_nsa_win"][0, b, :, which].rearrange("(t p) k d -> p t (k d)", p=P)
                                 ).then_inc(kv_full[b], 16)

            with sp.Fori(0, 4) as r:
                for u in range(KVS):
                    sp.wait_ge(kv_free[u], r + 1)
                    for g in range(2):
                        sp.dma_start(*cmp_piece(page(r * 16 + u * 2 + g), u, g, 0)).then_inc(kv_full[u], 16)
            moba_units(KV_MK, 0)
            moba_units(KV_MV, 512)
            sp.wait_ge(N.pr_log, 4)
            sp.dma_start(bias, toeplitz[1]).then_inc(N.bias_back, 16)
            nsa_units(KV_SK, 256)
            window_units(KV_WK, 0)
            nsa_units(KV_SV, 384)
            window_units(KV_WV, 1)
            sp.wait_ge(N.x_ready, 1)
            sp.wait_ge(N.z_stored, 16 * 6)
            loads = [
                (s5row[:, 0, :], I["s5_a_re"][0].rearrange("(q j) n -> q (j n)", j=2)),
                (s5row[:, 1, :], I["s5_a_im"][0].rearrange("(q j) n -> q (j n)", j=2)),
                (s5dt, I["s5_log_dt"][0].rearrange("(q j) -> q j", j=2)),
                (hrow, I["state_s5"][0].rearrange("(a b) r (q j) n -> (b r q) a (j n)", b=2, j=2)),
            ]
            for i, name in enumerate(("s5_b_re", "s5_b_im")):
                for j in range(2):
                    loads.append((braw[64 * j:64 * j + 64, i], I[name][0].rearrange("(q j) n c -> j n q c", j=2)[j]))
            for i, name in enumerate(("s5_c_re", "s5_c_im")):
                for j in range(2):
                    loads.append((craw[:, i, :, j], I[name][0].rearrange("(k g) c n -> (g c) k n", g=8)))
            assert len(loads) == S5_LOADS
            for n, (dst, src) in enumerate(loads):
                sp.dma_start(dst, src).then_inc(N.s5_rows_loaded if n < 4 else N.s5_loaded, 16)
            sp.dma_start(O["win_sample"][0, :, 0:511].rearrange("b t a k d -> b (t a k d)"),
                         I["state_nsa_win"][0, :, 1:512].rearrange("b t a k d -> b (t a k d)")).then_inc(N.win_stored, 16)
            sp.wait_ge(N.fin_ev, 2)
            sp.dma_start(O["s5_prompt"][0, 0].rearrange("r (q j) n -> (r q) (j n)", j=2), finrow[0:64, 0, :]).then_inc(N.y_stored, 16)
            sp.dma_start(O["s5_sample"][0].rearrange("(a b) r (q j) n -> (b r q) a (j n)", b=2, j=2), finrow[:, 1:5, :]).then_inc(N.y_stored, 16)
            for t in range(3):
                sp.wait_ge(N.y_out_ev, 2 * (t + 1))
                dst = O["y_prompt"][0, t * P:(t + 1) * P, :] if t < 2 else O["y_sample"].rearrange("b t d -> (b t) d")
                sp.dma_start(dst, yrow[0:P if t < 2 else TS, t, :]).then_inc(N.y_stored, 16)
            sp.wait_ge(N.win_stored, 16)
            sp.wait_ge(N.y_stored, 16 * 5)

        @block.gpsimd
        def _(pool):
            nc.gpsimd.memset(ones[:], 1.0).then_inc(N.ones_made, 1)
            nc.gpsimd.memset(cT[:], 0.0).then_inc(N.ones_made, 1)

            def room(seq):
                if seq >= SLOTS:
                    pool.wait_ge(N.mm_done, 4 * (seq - SLOTS + 1))

            def load(seq, src, dst=None):
                room(seq)
                s = seq % SLOTS
                pool.dma_start(ring[:, s, :].rearrange("p (k c) -> p k c", k=KC) if dst is None else dst, src
                               ).then_inc(ring_full[s], 16)

            def by_rows(w):
                return w.rearrange("(k p) c -> p k c", p=P)

            def load_ada(seq, w, first=0, end=6):
                for i in range(first, end):
                    load(seq + i, by_rows(w)[:, :, 512 * i:512 * i + 512])

            pool.wait_ge(N.x_loaded, 48)
            def load_cmp(seq):
                for kind in range(2):
                    load(seq + kind, I["nsa_cmp_w1"][0, kind].rearrange("(i p) h -> p i h", p=P),
                         ring[:, (seq + kind) % SLOTS, 0:2048].rearrange("p (i h) -> p i h", i=CMP // 2))

            def cmp_pages(r):
                for u in range(KVS):
                    pool.wait_ge(kv_free[u], r + 1)
                    for g in range(2):
                        n = pool.value_load(pt[0:1, DS(r * 16 + u * 2 + g, 1)], min_val=0, max_val=POOL - 1)
                        pool.dma_start(*cmp_piece(DS(n, 1), u, g, 1)).then_inc(kv_odd[u], 16)

            load_ada(SEQ["ada0"], I["attn_ada_w"][0], 0, 4)
            pool.wait_ge(N.pt_loaded, 16)
            cmp_pages(0)
            load_ada(SEQ["ada0"], I["attn_ada_w"][0], 4, 6)
            load_cmp(SEQ["cmp"])
            with pool.Fori(1, 4) as r:
                cmp_pages(r)
            for i in range(6):
                w = min(512, IN_COLS - 512 * i)
                s = (SEQ["w_in"] + i) % SLOTS
                load(SEQ["w_in"] + i, by_rows(I["attn_w_in"][0])[:, :, 512 * i:512 * i + w],
                     ring[:, s, 0:KC * w].rearrange("p (k c) -> p k c", k=KC))
            load_ada(SEQ["ada1"], I["mlp_ada_w"][0])
            load_ada(SEQ["ada2"], I["ssm_ada_w"][0])
            load_cmp(SEQ["cmp_p"])
            load_ada(SEQ["ada3"], I["mlp_ada_w"][1], 0, 4)

            def products(slot, q):
                for g in range(2):
                    last = nc.gpsimd.tensor_tensor(
                        pprod[:, 512 * g:512 * g + 512].rearrange("p (k g d) -> p k g d", k=2, g=4),
                        at(kv[:, slot, P * g:], (64, 2), (0, 4), (1, 64)), q.rearrange("p (k g d) -> p k g d", k=2, g=4), ALU.mult)
                last.then_inc(N.pprod_ready, 1)

            pool.wait_ge(N.qk_ev, 8)
            pool.wait_ge(N.q_bc_ev, 16)
            with pool.Fori(0, 2) as r:
                for u in range(KVS):
                    pool.wait_ge(kv_full[u], r * 64 + kv_full_value(KV_SK + u))
                    pool.wait_ge(N.pprod_used, r * 8 + u + 1)
                    pool.sem_inc(N.pool_step, 1)
                    products(u, qb[:, DS(r * 4 + u // 2, 1), :].rearrange("p b c -> p (b c)"))
            load_ada(SEQ["ada3"], I["mlp_ada_w"][1], 4, 6)
            for b in range(TS):
                pool.wait_ge(kv_full[b], kv_full_value(KV_WK + b))
                pool.wait_ge(N.pprod_used, 17 + b)
                products(b, qb[:, b, :])
            for i in range(2):
                load(SEQ["w_out"] + i, by_rows(I["attn_w_out"][0])[:, :, 512 * i:512 * i + 512])

            def load_mlp(layer):
                base = SEQ["w1_%d" % layer]
                w1 = by_rows(I["mlp_w1"][layer])
                with pool.Fori(0, 2) as it:
                    for j in range(4):
                        pool.wait_ge(N.mm_done, it * 16 + 4 * (base + j - SLOTS + 1))
                        pool.dma_start(ring[:, (base + j) % SLOTS, :].rearrange("p (k c) -> p k c", k=KC),
                                       w1[:, :, DS(it * 2048 + j * 512, 512)]).then_inc(ring_full[(base + j) % SLOTS], 16)
                base = SEQ["w2_%d" % layer]
                w2 = I["mlp_w2"][layer].rearrange("(f p) c -> p f c", p=P)
                with pool.Fori(0, 2) as it:
                    for j in range(4):
                        pool.wait_ge(N.mm_done, it * 16 + 4 * (base + j - SLOTS + 1))
                        pool.dma_start(ring[:, (base + j) % SLOTS, :].rearrange("p (f c) -> p f c", f=16),
                                       w2[:, 16 * (j % 2):16 * (j % 2) + 16, DS(it * 512 + (j // 2) * 256, 256)]
                                       ).then_inc(ring_full[(base + j) % SLOTS], 16)

            load_mlp(0)
            for i in range(4):
                seq = SEQ["glu"] + i
                room(seq)
                for half in range(2):
                    pool.dma_start(ring[:, seq % SLOTS, :].rearrange("p (k z c) -> p k z c", k=KC, z=2)[:, :, half, :],
                                   by_rows(I["s5_w_glu"][0])[:, :, half * D + 256 * i:half * D + 256 * i + 256]
                                   ).then_inc(ring_full[seq % SLOTS], 16)
            for n in range(NT):
                pool.wait_ge(N.zc_ready, n + 1)
                if n >= 2:
                    pool.wait_ge(N.y_mm, n - 1)
                zc = zcur[:, n % 2].rearrange("p (s t) -> p s t", t=SEG)
                for table, dst in ((cosT, pc5), (sinT, ps5)):
                    nc.gpsimd.tensor_tensor(dst[:, n % 2].rearrange("p (s t) -> p s t", t=SEG), zc, at(table[:, n, :], (0, 4), (1, SEG)),
                                            ALU.mult).then_inc(N.zp_done, 1)
            load_mlp(1)

        def l_of(br):
            c = 0 if br else 400
            return bank[4][0:64, c:c + 1]

        def ada_row(i):
            return hT[:, 4 + 2 * (i % 2):6 + 2 * (i % 2), 0:TP]

        GROUPS = ((0, 16, 0), (NQ, 8, 16), (KSEL, 2, 24), (KWIN, 2, 26))
        S_GROUPS = ((MK, 8, 8),) + GROUPS[1:]
        GAINS = ((MQ, 8, 0), (MK, 8, 1), (NQ, 8, 2), (KSEL, 2, 4), (KWIN, 2, 5))
        ADA_SEQ = (SEQ["ada0"], SEQ["ada1"], SEQ["ada2"], SEQ["ada3"])
        GAIN_AT = (96, 120, 104, 128)

        @block.tensor
        def _(pe):
            mm = nc.tensor.matmul

            def tr(out, in_, rows=P):
                return nc.tensor.transpose(out, in_, ident[0:rows, 0:rows])

            pe.wait_ge(N.small_loaded, 16 * SMALL)
            tr(bank[1][:, 0:120], vecA, 120)
            tr(bank[1][:, 120:136], vecB, 16)
            tr(bank[1][:, 136:168], posrow, 32).then_inc(N.small_tr, 1)
            pe.wait_ge(N.csil_ready, 1)
            for k in range(KC):
                last = tr(bank[0][:, 9 * k:9 * k + 9], csil[:, P * k:P * k + P], 9)
            last.then_inc(N.c_tr, 1)
            pe.wait_ge(N.x_loaded, 48)
            for k in range(KC):
                if k >= 2:
                    pe.wait_ge(N.x_ev, k - 1)
                for t in range(3):
                    rows = P if t < 2 else TS
                    last = tr(bank[2 + k % 2][:, P * t:P * t + rows], xrow[t][:, P * k:P * k + P], rows)
                last.then_inc(N.x_tr, 1)

            def group(k):
                return slice(32 * (k % 4), 32 * (k % 4) + 32)

            def ada(n, mm_banks, dst, between=lambda i: None, first=0, end=6):
                def turn_back(i):
                    pe.wait_ge(N.ada_row, 6 * n + i + 1)
                    for ch in range(4):
                        last = mm(dst[:, (4 * i + ch) * 9:(4 * i + ch) * 9 + 9], ada_row(i)[:, ch // 2, P * (ch % 2):P * (ch % 2) + P],
                                  cst[:, C_SL:C_SL + 9], start=True, stop=True)
                    last.then_inc(N.ada_tr, 1)

                for i in range(first, end):
                    seq = ADA_SEQ[n] + i
                    pe.wait_ge(ring_full[seq % SLOTS], panel_full(seq))
                    if i >= 2:
                        pe.wait_ge(N.ada_row, 6 * n + i - 1)
                    for k in range(KC):
                        last = mm(mm_banks[i % 2][group(k), 0:512], cT[:, k, :], ring[:, seq % SLOTS, 512 * k:512 * k + 512],
                                  start=(k < 4), stop=(k >= 4))
                    last.then_inc(N.mm_done, 4)
                    if i:
                        turn_back(i - 1)
                    between(i)
                if end == 6:
                    turn_back(5)

            def sum_squares(n):
                for half in range(2):
                    pe.wait_ge(N.sq_ready, 2 * n + half + 1)
                    for k in range(4 * half, 4 * half + 4):
                        last = mm(bank[6][:, 0:T], ones[:], sq[:, k, :], start=(k == 0), stop=(k == KC - 1))
                last.then_inc(N.ssq_ready, 1)

            def normed(n):
                pe.wait_ge(N.h_ready, 8 * (n + 1))
                pe.wait_ge(N.hs_ready, n + 1)

            def turn_unit(seq):
                pe.wait_ge(kv_full[seq % KVS], kv_full_value(seq))
                pe.wait_ge(kv_odd[seq % KVS], 32 * (seq // KVS + 1))
                if seq >= 2:
                    pe.wait_ge(N.cmp_ev, seq - 1)
                for x in range(4):
                    last = tr(bank[2 + seq % 2][:, P * x:P * x + P], kv[:, seq % KVS, P * x:P * x + P])
                    if x == 0 and seq % (2 * KVS):
                        last.then_inc(kv_free[(seq - 1) % KVS], 1)
                last.then_inc(N.cmp_tr, 1)

            def turn_early(i):
                if i < EARLY // 2:
                    if i == 0:
                        pe.wait_ge(N.x_ev, 8)
                    turn_unit(2 * i)
                    turn_unit(2 * i + 1)

            pe.wait_ge(N.small_ev, 1)
            mm(bank[4][0:16, 0:384], rel, onehot[:, OH_TZ:OH_TZ + 384], start=True, stop=True)
            for pg in range(PAGES):
                mm(bank[5][:, 16 * pg:16 * pg + 16], onehot[:, OH_PG + P * pg:OH_PG + P * pg + P], rel, start=True, stop=True)
            mm(bank[5][:, 128:136], onehot[:, OH_CS:OH_CS + P], rel[:, 8:16], start=True, stop=True)
            mm(bank[5][0:8, 136:152], onehot[:, OH_OWN:OH_OWN + 8], rel, start=True, stop=True)
            for tn in range(16):
                last = mm(bank[5][:, 152 + 8 * tn:160 + 8 * tn], onehot[:, OH_CP + P * tn:OH_CP + P * tn + P], rel[:, 8:16],
                          start=True, stop=True)
            last.then_inc(N.bias_mm, 1)
            pe.wait_ge(N.c_ev, 1)
            ada(0, bank[0:2], bank[7], turn_early)
            pe.wait_ge(N.ones_made, 1)
            sum_squares(0)

            pe.wait_ge(N.bias_ev, 1)
            w1k = []
            for kind in range(2):
                seq = SEQ["cmp"] + kind
                pe.wait_ge(ring_full[seq % SLOTS], panel_full(seq))
                w1k.append(ring[:, seq % SLOTS, 0:2048].rearrange("p (i h) -> p i h", i=CMP // 2))
                for i in range(CMP // 2):
                    last = mm(bank[4][:, kind:kind + 1], w1k[kind][:, i, :], posT[:, 16 * kind + i:16 * kind + i + 1],
                              start=(i == 0), stop=(i == CMP // 2 - 1))
            last.then_inc(N.pb_mm, 1)
            for half in range(2):
                for seq in range(2 * KVS * half + (EARLY if half == 0 else 0), 2 * KVS * (half + 1)):
                    turn_unit(seq)
                pe.wait_ge(N.cmp_ev, 2 * KVS * (half + 1))
                if half:
                    pe.wait_ge(N.gelu_ev, 1)
                for kind in range(2):
                    for i in range(CMP // 2):
                        last = mm(bank[kind][:, 0:256], w1k[kind][:, i, :], at(pairs[:, 4096 * kind + i:], (2048, 2), (16, 128)),
                                  start=(i == 0), stop=(i == CMP // 2 - 1))
                        if kind == 0 and i == 0:
                            last.then_inc(kv_free[seq % KVS], 1)
                if half:
                    last.then_inc(N.mm_done, 8)
                else:
                    last.then_inc(N.cmp_mm, 1)

            def spread_q(col, n0, banks):
                for b in range(TS):
                    if b >= 2 or n0:
                        pe.wait_ge(N.q_bc_ev, n0 + b - 1)
                    mm(banks[b % 2][:, 0:512], ident[0:TS, b:b + 1].to_broadcast([TS, P]), zs[:, col:col + 512],
                       start=True, stop=True).then_inc(N.q_bc, 1)

            normed(0)
            pe.wait_ge(N.gelu_ev, 2)
            pe.wait_ge(N.small_ev, 1)
            pe.wait_ge(N.padded_ready, 1)
            for p in range(6):
                seq = SEQ["w_in"] + p
                w = min(512, IN_COLS - 512 * p)
                pe.wait_ge(ring_full[seq % SLOTS], panel_full(seq))
                samples, total = bank[3 * (p % 2) + 2], bank[6 + p % 2]
                if p >= 2:
                    pe.wait_ge(N.zs_rows, p - 1)
                for k in range(KC):
                    last = mm(samples[group(k), 0:w], hs32[:, k, :], ring[:, seq % SLOTS, w * k:w * k + w], start=(k < 4), stop=(k >= 4))
                last.then_inc(N.zs_mm, 1)
                for t in range(2):
                    if p >= 2:
                        pe.wait_ge(N.z_ev, 3 * (p - 2) + 2 * t + 1)
                    for k in range(KC):
                        last = mm(bank[3 * (p % 2) + t][:, 0:w], hT[:, k, P * t:P * t + P],
                                  ring[:, seq % SLOTS, w * k:w * k + w], start=(k == 0), stop=(k == KC - 1))
                    last.then_inc(N.mm_done, 3 if t else 1)
                    if t == 0:
                        pe.wait_ge(N.zs_rows, p + 1)
                        if p >= 2:
                            pe.wait_ge(N.q_bc_ev, 8)
                            pe.wait_ge(N.z_ev, 3 * (p - 2) + 2)
                        mm(total[0:TS, 0:w], cst[:, C_SL:C_SL + TS], zs_part[:, p % 2, 0:w], start=True, stop=True).then_inc(N.zs_sum, 1)
                if p == 1:
                    pe.wait_ge(N.qs_normed, 1)
                    pe.wait_ge(N.z_ev, 5)
                    spread_q(MQ, 0, bank[6:8])

            pe.wait_ge(N.z_ev, 18)
            ada(1, bank[0:2], bank[7])
            ada(2, bank[2:4], bank[6], end=SLOTS)

            pe.wait_ge(N.zs_normed, 1)
            spread_q(NQ, 8, bank[0:2])

            pe.wait_ge(N.moba_scored, 1)
            pe.wait_ge(N.q_bc_ev, 16)
            mm(bank[0][:, 0:512], ones[:], s_raw, start=True, stop=True).then_inc(N.gate_sum, 1)

            pe.wait_ge(N.gates_ready, 1)
            mm(bank[5][0:64, 0:24], cst[0:8, C_GT:C_GT + 64], gates_s, start=True, stop=True).then_inc(N.small_tr, 1)

            def turn(groups, n0):
                for g, pieces in enumerate(groups):
                    if n0 + g >= 2:
                        pe.wait_ge(N.qk_ev, n0 + g - 1)
                    for i, piece in enumerate(pieces):
                        last = tr(bank[2 + g % 2][:, P * i:P * i + P], piece)
                    last.then_inc(N.qk_tr, 1)

            def chunks_of(col, pair):
                return [z[:, t, col + P * c:col + P * c + P] for c in (2 * pair, 2 * pair + 1) for t in range(2)]

            pe.wait_ge(N.z_normed, 1)
            pe.wait_ge(N.ada_row, 6 * 2 + SLOTS)
            turn([chunks_of(MQ, 0), chunks_of(MQ, 1), chunks_of(MK, 0), chunks_of(MK, 1)], 0)
            pe.wait_ge(N.mods_ready, 1)
            pe.wait_ge(N.qk_ev, 4)
            for kind in range(2):
                for h in range(KVH):
                    for t in range(2):
                        for e in range(2):
                            c = 256 * kind + P * h + 64 * t
                            last = mm(bank[2][64 * e:64 * e + 64, c:c + 64],
                                      z[:, t, KCMP + P * kind + 64 * h:KCMP + P * kind + 64 * h + 64], at(ident[:, e:], (2, 64)),
                                      start=True, stop=True)
            last.then_inc(N.cmp_tr, 1)
            pe.wait_ge(N.cmp_ev, 4 * KVS + 1)

            own_m, own_s, own_w = own[:, 0:64], own[:, 64:128], own[:, 128:192]

            def softmax_sums(br, last_dim, mine):
                pe.wait_ge(N.mx_in, br + 1)
                last = tr(bank[2][0:64, 0:P], last_dim)
                if mine is not None:
                    last = tr(bank[2][0:64, P:P + 8], mine, 8)
                last.then_inc(N.mx_tr, 1)
                pe.wait_ge(N.mx_diag, br + 1)
                mm(bank[3][:, 0:64], ones[0:64, :], diag, start=True, stop=True).then_inc(N.mx_bc, 1)
                pe.wait_ge(N.p_ready, br + 1)
                l = l_of(br)
                last = mm(l, s_cs if br == 1 else lsum, ones[:, 0:1], start=True, stop=mine is None)
                if mine is not None:
                    last = mm(l, mine, ones[0:8, 0:1], start=False, stop=True)
                last.then_inc(N.l_done, 1)

            softmax_sums(0, m1, own_m)

            def p_of(half, b4, pg):
                return pbuf[:, 1024 * half + 256 * b4 + 32 * pg:1024 * half + 256 * b4 + 32 * pg + 32]

            def moba_pv(b):
                for pg in range(PAGES):
                    seq = KV_MV + 8 * b + pg
                    pe.wait_ge(kv_full[seq % KVS], kv_full_value(seq))
                    mm(bank[5][32 * (b // 4):32 * (b // 4) + 32, 0:512], p_of(b // 4, b % 4, pg), kv[:, seq % KVS, :],
                       start=(b % 4 == 0 and pg == 0), stop=False).then_inc(kv_free[seq % KVS], 1)

            pe.wait_ge(N.small_ev, 2)
            moba_pv(0)
            ada(2, bank[2:4], bank[6], first=SLOTS)
            for kind in range(2):
                seq = SEQ["cmp_p"] + kind
                pe.wait_ge(ring_full[seq % SLOTS], panel_full(seq))
                w1 = ring[:, seq % SLOTS, 0:2048].rearrange("p (i h) -> p i h", i=CMP // 2)
                for i in range(CMP // 2):
                    last = mm(bank[4][:, 16 * kind:16 * kind + 16], w1[:, i, :], at(p_pairs[:, 256 * kind + i:], (P, 2), (16, 8)),
                              start=(i == 0), stop=(i == CMP // 2 - 1))
                last.then_inc(N.mm_done, 4)
            pe.wait_ge(N.mods_ready, 2)
            pe.wait_ge(N.gelu_ev, 3)
            for kind in range(2):
                for half in range(2):
                    for h in range(KVH):
                        c = ((kind * 2 + half) * 2 + h) * 64
                        last = mm(bank[7][:, c:c + 64], hg[:, (kind * 2 + h) * 256 + P * half:(kind * 2 + h) * 256 + P * half + P],
                                  w2c[:, 64 * kind:64 * kind + 64], start=True, stop=True)
            for kind in range(2):
                for h in range(KVH):
                    c = 64 + (kind * 2 + h) * 64
                    last = mm(bank[4][0:8, c:c + 64], hg[:, 1024 + (kind * 2 + h) * 8:1032 + (kind * 2 + h) * 8],
                              w2c[:, 64 * kind:64 * kind + 64], start=True, stop=True)
            last.then_inc(N.cmp2_mm, 1)

            pe.wait_ge(N.kdup_ready, 1)
            for h in range(KVH):
                last = tr(bank[4][:, 384 + 8 * h:392 + 8 * h], kpd[:, P * h:P * h + P], 8)
            last.then_inc(N.kcp_tr, 1)

            def pair_scores(i):
                if i:
                    pe.wait_ge(N.pr_log, i)
                for pr in range(2):
                    if i < 4:
                        r = slice(64 * pr, 64 * pr + 64)
                        q = qkT[r, TP * i:TP * i + TP]
                        k = qkT[r, 1024 + TP * i:1024 + TP * i + TP]
                    else:
                        h = i - 4
                        r = slice(64 * (h % 2), 64 * (h % 2) + 64)
                        q = qkT[r, TP * (h // 2):TP * (h // 2) + TP]
                        k = qkT[r, 1024 + 512 * pr + TP * (h // 4):1024 + 512 * pr + TP * (h // 4) + TP]
                    mm(bank[pr][:, 0:P], q[:, 0:P], k[:, 0:P], start=True, stop=True)
                    last = mm(bank[pr][:, P:P + TP], q[:, P:TP], k, start=True, stop=True)
                last.then_inc(N.pr_s, 1)

            def pair_rest(i):
                pe.wait_ge(N.pr_p, i + 1)
                if i:
                    pe.wait_ge(N.pr_tev, i)
                for pr in range(2):
                    for j in range(3):
                        last = tr(bank[2 + pr][:, P * j:P * j + P], sps[i % 2][:, 384 * pr + P * j:384 * pr + P * j + P])
                last.then_inc(N.pr_tr, 1)
                chunk = i if i < 4 else 4 + (i - 4) // 2
                ob = bank[6 + chunk % 2]
                if chunk >= 2 and (i < 4 or i % 2 == 0):
                    pe.wait_ge(N.pr_oev, chunk - 1)
                h = i - 4
                if i >= 4:
                    if i > 4:
                        pe.wait_ge(N.cp_tev, h)
                    for t in range(2):
                        c = (((h % 2) * 2 + t) * 4 + h // 2) * 8
                        last = tr(bank[4][0:8, TP + P * t:TP + P * t + P], s_cp[:, c:c + 8])
                    last.then_inc(N.cp_tr, 1)
                    rows = slice(64 * (h % 2), 64 * (h % 2) + 64)
                    pe.wait_ge(N.cp_tev, h + 1)
                    mm(ob[rows, 0:TP], kvp[:, P + 64 * (h // 4):P + 64 * (h // 4) + 64], pcT[:, TP * (h % 2):TP * (h % 2) + TP],
                       start=True, stop=False)
                pe.wait_ge(N.pr_tev, i + 1)
                for pr in range(2):
                    if i < 4:
                        rows, v = slice(64 * pr, 64 * pr + 64), MV + 64 * (2 * i + pr)
                        first, final = True, True
                    else:
                        v = (VSEL, VWIN)[pr] + 64 * (h // 4)
                        first, final = False, pr == 1
                    pTp = pTs[i % 2][:, 384 * pr:384 * pr + 384]
                    mm(ob[rows, 0:TP], z[:, 0, v:v + 64], pTp[:, 0:TP], start=first, stop=False)
                    last = mm(ob[rows, P:TP], z[:, 1, v:v + 64], pTp[:, TP:384], start=False, stop=final)
                last.then_inc(N.pr_pv, 1)

            def pair_step(i, first, end):
                if i < end:
                    pair_scores(i)
                if i > first:
                    pair_rest(i - 1)

            pe.wait_ge(N.kcp_ev, 1)
            for half in range(2):
                mm(bank[half][:, 0:512], s4[:, P * half:P * half + P], zs[:, NQ:NQ + 512], start=True, stop=True).then_inc(N.q_bc, 1)
            for b in range(TS):
                if b:
                    moba_pv(b)
                if b == 0:
                    pe.wait_ge(N.cw_made, 1)
                    pe.wait_ge(N.mods_ready, 3)
                    pe.wait_ge(N.bias_back, 16)
                if b < 5:
                    pair_step(b, 0, 4)
            for half in range(2):
                last = mm(bank[5][32 * half:32 * half + 32, 0:512], own_m[:, 32 * half:32 * half + 32], zs[:, MV:MV + 512],
                          start=False, stop=True)
            last.then_inc(N.pv_done, 1)
            pe.wait_ge(N.osum_ready, 1)
            for c in range(4):
                last = mm(bank[2][:, 8 * c:8 * c + 8], oacc[:, P * c:P * c + P], cst[0:64, C_G:C_G + 8], start=True, stop=True)
            last.then_inc(N.osum_mm, 1)
            pe.wait_ge(N.zdup_ready, 1)
            pe.wait_ge(N.oTs_ready, 1)
            turn([chunks_of(NQ, 0), chunks_of(NQ, 1)] +
                 [[zdup[:, t, src, h] for h in range(KVH) for t in range(2)] for src in range(2)], 4)
            pe.wait_ge(N.qk_ev, 8)
            for h in range(NSA_H):
                r = slice(64 * (h % 2), 64 * (h % 2) + 64)
                for t in range(2):
                    last = mm(bank[h % 2][:, (t * 4 + h // 2) * 8:(t * 4 + h // 2) * 8 + 8],
                              qkT[r, TP * (h // 2) + P * t:TP * (h // 2) + P * t + P], kcTp[r, 8 * (h // 4):8 * (h // 4) + 8],
                              start=True, stop=True)
            last.then_inc(N.cp_mm, 1)
            pe.wait_ge(N.pr_oev, 4)
            ada(3, bank[2:4], bank[7])

            softmax_sums(1, s_cs, None)
            for half in range(2):
                last = mm(bank[5][32 * half:32 * half + 32, 0:P], s_cs[:, 32 * half:32 * half + 32],
                          kvc[:, 256 + P * half:256 + P * half + P], start=True, stop=True)
            last.then_inc(N.pv_done, 1)

            def pages_pv(br, mine, vcol, units, tiles):
                softmax_sums(br, m1, mine)
                for u in range(units[1] - units[0]):
                    seq = units[0] + u
                    pe.wait_ge(kv_full[seq % KVS], kv_full_value(seq))
                    for g in range(4):
                        b, pg = divmod(4 * u + g, tiles)
                        last = mm(bank[5][32 * (b // 4):32 * (b // 4) + 32, 0:P], p_of(b // 4, b % 4, pg),
                                  kv[:, seq % KVS, P * g:P * g + P], start=(b % 4 == 0 and pg == 0), stop=False)
                    last.then_inc(kv_free[seq % KVS], 1)
                    if br == 2 and u % 2:
                        if u == 1:
                            pe.wait_ge(N.cp_ready, 1)
                            pe.wait_ge(N.mods_ready, 4)
                            pe.wait_ge(N.bias_back, 32)
                        pair_step(4 + u // 2, 4, 12)
                if br == 2:
                    pair_step(12, 4, 12)
                for half in range(2):
                    last = mm(bank[5][32 * half:32 * half + 32, 0:P], mine[:, 32 * half:32 * half + 32],
                              zs[:, vcol:vcol + P], start=False, stop=True)
                last.then_inc(N.pv_done, 1)

            pages_pv(2, own_s, VSEL, (KV_SV, KV_WV), 8)
            pages_pv(3, own_w, VWIN, (KV_WV, KV_END), 4)
            pe.wait_ge(N.osum_ready, 2)
            for c in range(4):
                last = mm(bank[2][:, 8 * c:8 * c + 8], oacc[:, P * c:P * c + P], cst[0:64, C_G:C_G + 8], start=True, stop=True)
            last.then_inc(N.osum_mm, 1)

            pe.wait_ge(N.pr_oev, 8)
            pe.wait_ge(N.oTs_ready, 2)
            for i in range(2):
                seq = SEQ["w_out"] + i
                pe.wait_ge(ring_full[seq % SLOTS], panel_full(seq))
                for ch in range(4):
                    if i:
                        pe.wait_ge(N.out_free, ch + 1)
                    for k in range(KC):
                        last = mm(bank[ch][:, 0:T], ring[:, seq % SLOTS, 512 * k + P * ch:512 * k + P * ch + P], hT[:, k, :],
                                  start=(k == 0), stop=(k == KC - 1))
                    last.then_inc(N.mm_done, 1)

            def mlp(layer, outs_before, between):
                base = SEQ["w1_%d" % layer]
                normed(1 + 2 * layer)
                pe.wait_ge(N.out_free, outs_before)
                with pe.Fori(0, 2) as it:
                    for j in range(4):
                        s = (base + j) % SLOTS
                        pe.wait_ge(ring_full[s], it * 16 + panel_full(base + j))
                        for ch in range(4):
                            pe.wait_ge(N.relu_ev, it * 16 + 36 * layer + 4 * j + ch + 1)
                            for k in range(KC):
                                last = mm(bank[ch][:, 0:T], ring[:, s, 512 * k + P * ch:512 * k + P * ch + P], hT[:, k, :],
                                          start=(k == 0), stop=(k == KC - 1))
                            last.then_inc(N.mm_done, 1)
                pe.wait_ge(N.relu_ev, 36 * (layer + 1))
                between()
                base = SEQ["w2_%d" % layer]
                pe.wait_ge(N.act_ready, 8 * (layer + 1))
                with pe.Fori(0, 2) as it:
                    for j in range(4):
                        s = (base + j) % SLOTS
                        pe.wait_ge(ring_full[s], it * 16 + panel_full(base + j))
                        if j % 2 == 0:
                            pe.wait_ge(N.out_free, it * 4 + outs_before)
                        for c in range(2):
                            for f in range(16):
                                last = mm(bank[j // 2 * 2 + c][:, 0:T], ring[:, s, 256 * f + P * c:256 * f + P * c + P],
                                          actT[:, 16 * (j % 2) + f, :], start=(j % 2 == 0 and f == 0), stop=(j % 2 == 1 and f == 15))
                            last.then_inc(N.mm_done, 2)

            sum_squares(1)
            pe.wait_ge(N.s5_rows_made, 1)
            pe.wait_ge(N.s5_rows_loaded, 64)
            pe.wait_ge(N.out_free, 8)
            for i in range(3):
                tr(bank[0][:, 32 * i:32 * i + 32], s5row[:, i, :], 32)
            for a in range(4):
                last = tr(bank[1][:, P * a:P * a + P], hrow[:, a, :])
            last.then_inc(N.s5_rows_tr, 1)
            pe.wait_ge(N.s5_rows_ev, 1)

            def s5_turns():
                pe.wait_ge(N.s5_bd, 1)
                for r in range(2):
                    for k in range(8):
                        last = tr(bank[2 * r + k // 4][:, P * (k % 4):P * (k % 4) + P],
                                  bdia[:, r].rearrange("p q j c -> p (q j c)")[:, P * k:P * k + P])
                last.then_inc(N.s5_b_tr, 1)
                for r in range(2):
                    for k in range(8):
                        last = tr(bank[4 + 2 * r + k // 4][:, P * (k % 4):P * (k % 4) + P],
                                  craw[:, r, k].rearrange("p j n -> p (j n)"))
                last.then_inc(N.s5_c_tr, 1)
                pe.wait_ge(N.s5_b_ev, 1)
                pe.wait_ge(N.s5_c_ev, 1)

            mlp(0, 8, s5_turns)
            sum_squares(2)

            normed(2)
            pe.wait_ge(N.out_free, 16)

            def rows_of(q):
                return slice(32 * (q % 4), 32 * (q % 4) + 32)

            def c_of(i, q):
                return CT[:, i, q // 4, 32 * (q % 4):32 * (q % 4) + 32]

            def tile_out(q):
                k = q // 4
                pe.wait_ge(N.zp_done, 2 * (q + 1))
                if k >= 2 and q % 4 == 0:
                    pe.wait_ge(N.y_ev, k)
                out = bank[4 + k % 2][rows_of(q), 0:TP]
                c3 = pc5[:, q % 2].rearrange("p (r t) -> p r t", r=2)
                s3 = ps5[:, q % 2].rearrange("p (r t) -> p r t", r=2)
                mm(out, c_of(0, q), c3[:, 0], start=True, stop=False)
                mm(out, c_of(1, q), s3[:, 1], start=False, stop=False)
                mm(out, c_of(2, q), s3[:, 0], start=False, stop=False)
                mm(out, c_of(2, q), c3[:, 1], start=False, stop=True).then_inc(N.y_mm, 1)

            def tile_in(q):
                if q >= 4:
                    pe.wait_ge(N.u_free, q - 3)
                for r in range(2):
                    last = mm(bank[q % 4][:, TP * r:TP * r + TP], BT[rows_of(q), q // 4, r, :], hT[rows_of(q), q // 4, 0:TP],
                              start=True, stop=True)
                last.then_inc(N.u_mm, 1)

            for q in range(3):
                tile_in(q)
            pe.wait_ge(N.padded_ready, 2)
            for k in range(KC):
                for r in range(2):
                    last = mm(bank[4][:, 64 * k + 32 * r:64 * k + 32 * r + 32], BT[:, k, r, :], hm[:, 32 * k:32 * k + 32],
                              start=True, stop=True)
            last.then_inc(N.us_mm, 1)
            def samples_out():
                pe.wait_ge(N.xs_ready, 1)
                for q in range(NT):
                    out = bank[6][rows_of(q), 8 * (q // 4):8 * (q // 4) + 8]
                    mm(out, c_of(0, q), xs5[:, :, 0, q], start=True, stop=False)
                    last = mm(out, c_of(2, q), xs5[:, :, 1, q], start=False, stop=True)
                last.then_inc(N.ys_mm, 1)
                for a in range(4):
                    last = tr(bank[7][:, P * a:P * a + P], xs5[:, 2 * a:2 * a + 2].rearrange("p b r q -> p (b r q)"))
                last.then_inc(N.fin_tr, 1)

            for q in range(NT):
                if q + 3 < NT:
                    tile_in(q + 3)
                if q == 0:
                    samples_out()
                tile_out(q)
            pe.wait_ge(N.fin_ready, 1)
            pe.wait_ge(N.gelu_ready, 9)
            tr(bank[6][0:64, 0:P], xlast).then_inc(N.fin_tr, 1)

            pe.wait_ge(N.fin_ev, 2)
            pe.wait_ge(N.u_free, 32)
            for j in range(4):
                seq = SEQ["glu"] + j
                pe.wait_ge(ring_full[seq % SLOTS], panel_full(seq))
                for c in range(2):
                    if 2 * j + c >= 4:
                        pe.wait_ge(N.out_free, 16 + 2 * j + c - 3)
                    for zi in range(2):
                        b = 4 * (j % 2) + 2 * c + zi
                        for k in range(KC):
                            last = mm(bank[b][:, 0:T], ring[:, seq % SLOTS, 512 * k + 256 * zi + P * c:512 * k + 256 * zi + P * c + P],
                                      yT[:, k, :], start=(k == 0), stop=(k == KC - 1))
                        last.then_inc(N.mm_done, 1)
            pe.wait_ge(N.out_free, 24)
            sum_squares(3)
            mlp(1, 24, lambda: None)

            pe.wait_ge(N.x_ready, 4)
            for t in range(3):
                rows = P if t < 2 else TS
                for half in range(2):
                    for k in range(4):
                        last = tr(bank[2 * t + half][0:rows, P * k:P * k + P], xT[:, 4 * half + k, P * t:P * t + rows])
                    last.then_inc(N.y_tr, 1)

        @block.scalar
        def _(act):
            step = [0]

            def then(ins):
                step[0] += 1
                ins.then_inc(N.act_step, 1)
                act.wait_ge(N.act_step, step[0])

            f = nc.scalar.activation
            act.wait_ge(N.c_loaded, 32)
            f(csil, crow, ACT.Silu).then_inc(N.csil_ready, 1)
            for k in range(KC):
                act.wait_ge(N.x_tr, k + 1)
                nc.scalar.copy(xT[:, k, :], bank[2 + k % 2][:, 0:T]).then_inc(N.x_ev, 1)

            def norm(n):
                act.wait_ge(N.x_ev, 8)
                if n:
                    act.wait_ge(N.x_ready, n)
                for half in range(2):
                    k = slice(4 * half, 4 * half + 4)
                    f(sq[:, k, :], xT[:, k, :], ACT.Square).then_inc(N.sq_ready, 1)
                act.wait_ge(N.r_ready, 2 * n + 1)
                f(sq[:, 0, :], sq[:, 0, :], ACT.Sqrt).then_inc(N.rt_ready, 1)
                for k in range(KC):
                    act.wait_ge(N.h_mul, 8 * n + k + 1)
                    f(hT[:, k, 0:TP], hT[:, k, 0:TP], ACT.Identity, bias=mods[:, n, k, 0:1]).then_inc(N.h_ready, 1)

            def ada_evac(n, banks, between=lambda i: None, first=0, end=6):
                for i in range(first, end):
                    act.wait_ge(N.mm_done, 4 * (ADA_SEQ[n] + i + 1))
                    if 6 * n + i >= 2:
                        act.wait_ge(N.ada_tr, 6 * n + i - 1)
                    nc.scalar.copy(ada_row(i), banks[i % 2][:, 0:512].rearrange("p (k c) -> p k c", k=2)).then_inc(N.ada_row, 1)
                    between(i)

            def cmp_evac(n):
                act.wait_ge(N.cmp_tr, n + 1)
                nc.scalar.copy(at(pairs[:, P * (n % (2 * KVS)):], (2048, 4), (1, P)),
                               bank[2 + n % 2][:, 0:512].rearrange("p (x c) -> p x c", x=4)).then_inc(N.cmp_ev, 1)

            def evac_early(i):
                if i < EARLY // 2:
                    cmp_evac(2 * i)
                    cmp_evac(2 * i + 1)

            ada_evac(0, bank[0:2], evac_early)
            norm(0)
            act.wait_ge(N.pb_mm, 1)
            nc.scalar.copy(pbias, bank[4][:, 0:2]).then_inc(N.pb_ev, 1)
            for half in range(2):
                for n in range(2 * KVS * half + (EARLY if half == 0 else 0), 2 * KVS * (half + 1)):
                    cmp_evac(n)
                if half:
                    act.wait_ge(N.mm_done, 4 * (SEQ["cmp"] + 2))
                else:
                    act.wait_ge(N.cmp_mm, 1)
                act.wait_ge(N.pb_ev, 1)
                for kind in range(2):
                    last = f(at(hg[:, 512 * kind + P * half:], (256, 2), (1, P)), bank[kind][:, 0:256].rearrange("p (h c) -> p h c", h=2),
                             ACT.Gelu_apprx_tanh, bias=pbias[:, kind:kind + 1])
                last.then_inc(N.gelu_ev, 1)
            def spread_evac(n0, banks):
                for b in range(TS):
                    act.wait_ge(N.q_bc, n0 + b + 1)
                    nc.scalar.copy(qb[:, b, :], banks[b % 2][:, 0:512]).then_inc(N.q_bc_ev, 1)

            act.wait_ge(N.tz_stored, 16)
            for p in range(6):
                w = min(512, IN_COLS - 512 * p)
                act.wait_ge(N.zs_mm, p + 1)
                nc.scalar.copy(zs_part[:, p % 2, 0:w], bank[3 * (p % 2) + 2][:, 0:w]).then_inc(N.zs_rows, 1)
                for t in range(2):
                    act.wait_ge(N.mm_done, 4 * (SEQ["w_in"] + p) + (4 if t else 1))
                    nc.scalar.copy(z[:, t, 512 * p:512 * p + w], bank[3 * (p % 2) + t][:, 0:w]).then_inc(N.z_ev, 1)
                    if t == 0:
                        act.wait_ge(N.zs_sum, p + 1)
                        nc.scalar.copy(zs[:, 512 * p:512 * p + w], bank[6 + p % 2][0:TS, 0:w]).then_inc(N.z_ev, 1)
                if p == 0:
                    act.wait_ge(N.head_sums, 1)
                    f(sss[:, 0:8], sss[:, 0:8], ACT.Sqrt).then_inc(N.head_roots, 1)
                elif p == 1:
                    spread_evac(0, bank[6:8])

            def zs_root(i):
                if i == 3:
                    act.wait_ge(N.head_sums, 2)
                    f(sss[:, 8:28], sss[:, 8:28], ACT.Sqrt).then_inc(N.head_roots, 1)

            ada_evac(1, bank[0:2], zs_root)
            ada_evac(2, bank[2:4], end=SLOTS)
            act.wait_ge(N.head_sums, 3)
            f(ss, ss, ACT.Sqrt).then_inc(N.head_roots, 1)
            f(gates_s, zs[:, GATE:GATE + 24], ACT.Sigmoid).then_inc(N.gates_ready, 1)
            f(gates.rearrange("p (t c) -> p t c", t=2), z[:, :, GATE:GATE + 24], ACT.Sigmoid).then_inc(N.gates_ready, 1)
            act.wait_ge(N.moba_scored, 1)
            spread_evac(8, bank[0:2])

            def turn_evac(n0):
                for g in range(4):
                    act.wait_ge(N.qk_tr, n0 + g + 1)
                    nc.scalar.copy(qkT[:, 512 * g:512 * g + 512], bank[2 + g % 2][:, 0:512]).then_inc(N.qk_ev, 1)

            turn_evac(0)
            act.wait_ge(N.zs_normed, 1)
            act.dma_start(O["moba_sample"], zs[:, MK:MK + 1024]).then_inc(N.z_stored, 16)
            act.dma_start(O["nsa_sample"], zs[:, KCMP:KCMP + 512]).then_inc(N.z_stored, 16)
            act.dma_start(O["win_sample"][0, :, 511].rearrange("b a k d -> b (a k d)"), zs[:, KWIN:KWIN + 256]).then_inc(N.z_stored, 16)
            act.wait_ge(N.z_normed, 1)
            act.dma_start(O["moba_prompt"].rearrange("(t p) c -> p t c", p=P), z[:, :, MK:MK + 1024]).then_inc(N.z_stored, 16)
            act.dma_start(O["nsa_prompt"].rearrange("(t p) c -> p t c", p=P), z[:, :, KCMP:KCMP + 512]).then_inc(N.z_stored, 16)
            act.dma_start(O["win_prompt"].rearrange("(t p) c -> p t c", p=P), z[:, :, KWIN:KWIN + 256]).then_inc(N.z_stored, 16)

            act.wait_ge(N.cmp_tr, 4 * KVS + 1)
            nc.scalar.copy(p_pairs, bank[2][:, 0:512]).then_inc(N.cmp_ev, 1)
            def exp_pages(br, tiles, mine):
                act.wait_ge(N.log_ready, br + 1)
                for half in range(2):
                    f(at(pbuf[:, 1024 * half:], (264, 4), (32, tiles), (1, 8)),
                      at(s_log[:, 32 * tiles * half:], (8 * tiles, 4), (8, tiles), (1, 8)), ACT.Exp)
                f(mine, mine, ACT.Exp).then_inc(N.p_exp, 1)

            exp_pages(0, 8, own[:, 0:64])
            ada_evac(2, bank[2:4], first=SLOTS)
            act.wait_ge(N.mm_done, 4 * (SEQ["cmp_p"] + 2))
            for kind in range(2):
                last = f(hg[:, 1024 + 16 * kind:1040 + 16 * kind], bank[4][:, 16 * kind:16 * kind + 16], ACT.Gelu_apprx_tanh,
                         bias=pbias[:, kind:kind + 1])
            last.then_inc(N.gelu_ev, 1)
            act.wait_ge(N.kc_ss, 1)
            f(ssc[:, 0:4], ssc[:, 0:4], ACT.Sqrt)
            f(ssc[0:8, 4:6], ssc[0:8, 4:6], ACT.Sqrt).then_inc(N.kc_std, 1)

            def pair_exp(i):
                act.wait_ge(N.pr_log, i + 1)
                buf = sps[i % 2]
                for pr in range(2):
                    for t, (a, b) in enumerate(((0, P), (P, 384))):
                        j = 4 * (i % 2) + 2 * pr + t
                        last = f(buf[:, 384 * pr + a:384 * pr + b], buf[:, 384 * pr + a:384 * pr + b], ACT.Exp,
                                 bias=nmin[:, j:j + 1], scale=-1.0, accum_out=lrow[:, j:j + 1])
                last.then_inc(N.pr_exp, 1)

            def pair_evac(i):
                act.wait_ge(N.pr_tr, i + 1)
                if i >= 2:
                    act.wait_ge(N.pr_pv, i - 1)
                nc.scalar.copy(pTs[i % 2].rearrange("p (a c) -> p a c", a=2), psum[:, 2:4, 0:384]).then_inc(N.pr_tev, 1)
                if i >= 4:
                    act.wait_ge(N.cp_tr, i - 3)
                    c = TP * (i % 2)
                    nc.scalar.copy(pcT[:, c:c + TP], bank[4][0:8, TP:2 * TP]).then_inc(N.cp_tev, 1)

            def pair_out(i):
                chunk = i if i < 4 else 4 + (i - 4) // 2
                if i < 4 or i % 2:
                    act.wait_ge(N.pr_pv, i + 1)
                    nc.scalar.copy(hT[:, chunk, 0:TP], bank[6 + chunk % 2][:, 0:TP]).then_inc(N.pr_oev, 1)

            def pair_steps(first, end):
                for i in range(first, end + 1):
                    if i > first:
                        pair_evac(i - 1)
                    if i < end:
                        pair_exp(i)
                    if i > first:
                        pair_out(i - 1)

            act.wait_ge(N.z_stored, 16 * 6)
            pair_steps(0, 4)
            turn_evac(4)
            act.wait_ge(N.cp_log, 1)
            f(s_cp, s_cp, ACT.Exp).then_inc(N.cp_exp, 1)
            ada_evac(3, bank[2:4])
            act.wait_ge(N.log_ready, 2)
            f(s_cs, s_cs, ACT.Exp).then_inc(N.p_exp, 1)
            exp_pages(2, 8, own[:, 64:128])
            pair_steps(4, 12)
            exp_pages(3, 4, own[:, 128:192])

            def relu(layer):
                act.wait_ge(N.x_ready, 1 + 2 * layer)
                if layer:
                    act.wait_ge(N.y_stored, 32)
                act.sem_inc(N.relu_ev, 4)
                act.wait_ge(N.z_stored, 16 * 6)
                base = SEQ["w1_%d" % layer]
                with act.Fori(0, 2) as it:
                    for m in range(16):
                        act.wait_ge(N.mm_done, it * 16 + 4 * base + m + 1)
                        f(actT[:, DS(it * 16 + m, 1), :], psum[:, m % 4:m % 4 + 1, 0:T], ACT.Relu).then_inc(N.relu_ev, 1)

            norm(1)
            act.wait_ge(N.s5_rows_ev, 1)
            f(st[:, 3, :], st[:, 2, :], ACT.Exp).then_inc(N.s5_dt, 1)
            act.wait_ge(N.s5_ang, 1)
            f(st[:, 8, :], st[:, 4, :], ACT.Exp)
            f(st[:, 9, :], st[:, 7, :], ACT.Sin)
            f(st[:, 10, :], st[:, 7, :], ACT.Sin, scale=0.5).then_inc(N.s5_sin, 1)
            relu(0)
            act.wait_ge(N.s5_b_tr, 1)
            act.wait_ge(N.s5_tables, 1)
            nc.scalar.copy(BT.rearrange("p k r n -> p r k n"), psum[:, 0:4, :].rearrange("p (r k) (l n) -> p r (k l) n", r=2, l=4)
                           ).then_inc(N.s5_b_ev, 1)
            norm(2)
            act.wait_ge(N.fin_tr, 1)
            nc.scalar.copy(finrow[:, 1:5, :].rearrange("p a c -> p (a c)"), bank[7][:, 0:512]).then_inc(N.fin_ev, 1)
            act.wait_ge(N.y_ev, 1)
            f(yT[:, :, TP:T], yT[:, :, TP:T], ACT.Gelu_apprx_tanh).then_inc(N.gelu_ready, 1)
            for k in range(KC):
                act.wait_ge(N.y_ev, k + 2)
                f(yT[:, k, 0:TP], yT[:, k, 0:TP], ACT.Gelu_apprx_tanh).then_inc(N.gelu_ready, 1)
            act.wait_ge(N.fin_tr, 2)
            nc.scalar.copy(finrow[0:64, 0, :], bank[6][0:64, 0:P]).then_inc(N.fin_ev, 1)
            for n in range(8):
                act.wait_ge(N.mm_done, 4 * SEQ["glu"] + 2 * n + 2)
                if n >= 2:
                    act.wait_ge(N.out_free, 16 + n - 1)
                f(sig[:, n % 2, :], bank[4 * (n // 2 % 2) + 2 * (n % 2) + 1][:, 0:T], ACT.Sigmoid).then_inc(N.sig_ready, 1)
            norm(3)
            relu(1)
            for t in range(3):
                rows = P if t < 2 else TS
                for half in range(2):
                    act.wait_ge(N.y_tr, 2 * t + half + 1)
                    nc.scalar.copy(yrow[0:rows, t, 512 * half:512 * half + 512], bank[2 * t + half][0:rows, 0:512]
                                   ).then_inc(N.y_out_ev, 1)

        @block.vector
        def _(dve):
            step = [0]

            def then(ins):
                step[0] += 1
                ins.then_inc(N.dve_step, 1)
                dve.wait_ge(N.dve_step, step[0])

            tt, ts = nc.vector.tensor_tensor, nc.vector.tensor_scalar
            stt, red, cp = nc.vector.scalar_tensor_tensor, nc.vector.tensor_reduce, nc.vector.tensor_copy
            rcp = nc.vector.reciprocal

            def mods_evac(n):
                dve.wait_ge(N.ada_tr, 6 * (n + 1))
                src = bank[6 if n == 2 else 7]
                then(tt(mods[:, n].rearrange("p c j -> p (c j)").rearrange("p (c j) -> p c j", j=9),
                        src[:, 0:216].rearrange("p (c j) -> p c j", j=9), at(vT[:, 24 * n:], (1, 24), (0, 9)), ALU.add))
                a = mods[:, n, 8:16, :]
                stt(out=a, in0=a, scalar=1.0, in1=at(vT[:, GAIN_AT[n]:], (1, 8), (0, 9)), op0=ALU.add, op1=ALU.mult
                    ).then_inc(N.mods_ready, 1)
                dve.wait_ge(N.mods_ready, n + 1)

            def norm(n):
                dve.wait_ge(N.ssq_ready, n + 1)
                r = sq[:, 0, :]
                ts(r, bank[6][:, 0:T], 1.0 / D, EPS, ALU.mult, ALU.add).then_inc(N.r_ready, 1)
                dve.wait_ge(N.rt_ready, n + 1)
                rcp(r, r).then_inc(N.r_ready, 1)
                dve.wait_ge(N.r_ready, 2 * n + 2)
                for k in range(KC):
                    stt(out=hT[:, k, 0:TP], in0=xT[:, k, 0:TP], scalar=mods[:, n, 8 + k, 0:1], in1=r[:, 0:TP],
                        op0=ALU.mult, op1=ALU.mult).then_inc(N.h_mul, 1)
                hs = hT[:, :, TP:T]
                then(tt(hs, xT[:, :, TP:T], mods[:, n, 8:16, 1:9], ALU.mult))
                then(tt(hs, hs, at(r[:, TP:T], (0, 8), (1, 8)), ALU.mult))
                tt(hs, hs, mods[:, n, 0:8, 1:9], ALU.add).then_inc(N.hs_ready, 1)

            def add_out(n, src, k, gate, t8):
                stt(out=xT[:, k, 0:TP], in0=src[:, 0:TP], scalar=gate[:, 0:1],
                    in1=xT[:, k, 0:TP], op0=ALU.mult, op1=ALU.add)
                tt(t8, src[:, TP:T], gate[:, 1:9], ALU.mult).then_inc(N.out_free, 1)

            def add_samples(n, count):
                dve.wait_ge(N.out_free, count)
                tt(xT[:, :, TP:T], xT[:, :, TP:T], tmp8x, ALU.add).then_inc(N.x_ready, 1)
                dve.wait_ge(N.x_ready, n + 1)

            tmp8x = cT[:, :, 0:8]

            for u in range(KVS):
                dve.sem_inc(kv_free[u], 1)
            dve.sem_inc(N.scored, 1)
            dve.sem_inc(N.pprod_used, 1)
            dve.wait_ge(N.small_tr, 1)
            cp(vT[:], bank[1][:, 0:136])
            cp(posT, bank[1][:, 136:168]).then_inc(N.small_ev, 1)
            dve.wait_ge(N.c_tr, 1)
            dve.wait_ge(N.ones_made, 2)
            cp(cT[:, :, 0:9], bank[0][:, 0:72].rearrange("p (k j) -> p k j", k=KC)).then_inc(N.c_ev, 1)
            dve.wait_ge(N.small_ev, 1)
            dve.wait_ge(N.bias_mm, 1)
            cp(tz, bank[4][0:16, 0:384])
            cp(at(biasP, (64, 2), (8, 8), (1, 8)), at(bank[5][:, 0:128], (8, 2), (16, 8), (1, 8)))
            cp(biasC, bank[5][:, 128:136])
            cp(biasO, bank[5][0:8, 136:152])
            for par in range(2):
                last = cp(at(biasCP[:, 64 * par:], (32, 2), (8, 4), (1, 8)), at(bank[5][:, 152 + par:], (64, 2), (2, 4), (8, 8)))
            last.then_inc(N.bias_ev, 1)
            cp(s4.rearrange("p (b i) -> p b i", b=8), at(ident[0:8, 0:8], (1, 8), (0, 32)))
            mods_evac(0)
            norm(0)

            def head_norms(zv, ssv, groups, first, rows, tiles, n):
                for t in range(tiles):
                    off = 0
                    for c0, nh, _ in groups:
                        zc = zv(c0, nh * 64, t)
                        last = tt(pbuf[0:rows, off:off + nh * 64], zc, zc, ALU.mult)
                        off += nh * 64
                    then(last)
                    last = red(ssv[:, 28 * t + first:28 * t + 28], pbuf[0:rows, 0:off].rearrange("p (h d) -> p h d", d=64), AX, ALU.add)
                    then(last)
                ssv = ssv if not first else ssv[:, first:]
                ts(ssv, ssv, 1.0 / HD, EPS, ALU.mult, ALU.add).then_inc(N.head_sums, 1)
                dve.wait_ge(N.head_roots, n)
                then(rcp(ssv, ssv))

            zf = lambda c0, w, t: z[:, t, c0:c0 + w]
            zsf = lambda c0, w, t: zs[:, c0:c0 + w]
            then(nc.vector.memset(hs32, 0.0))
            dve.wait_ge(N.hs_ready, 1)
            cp(hs32[:, :, 0:TS], hT[:, :, TP:T]).then_inc(N.padded_ready, 1)
            dve.wait_ge(N.z_ev, 2)
            then(tt(pbuf[0:8, 0:512], zs[:, 0:512], zs[:, 0:512], ALU.mult))
            then(red(sss[:, 0:8], pbuf[0:8, 0:512].rearrange("p (h d) -> p h d", d=64), AX, ALU.add))
            ts(sss[:, 0:8], sss[:, 0:8], 1.0 / HD, EPS, ALU.mult, ALU.add).then_inc(N.head_sums, 1)
            dve.wait_ge(N.head_roots, 1)
            then(rcp(sss[:, 0:8], sss[:, 0:8]))
            v = zs[:, MQ:MQ + 512].rearrange("p (h d) -> p h d", d=64)
            then(tt(v, v, at(sss, (1, 8), (0, 64)), ALU.mult))
            tt(v, v, at(qkg[0:8, 0, :], (0, 8), (1, 64)), ALU.mult).then_inc(N.qs_normed, 1)

            dve.wait_ge(N.q_bc_ev, 8)
            sraw_b = s_raw.rearrange("p (b c) -> p b c", b=8)
            with dve.Fori(0, TS) as b:
                for pg in range(PAGES):
                    dve.wait_ge(kv_full[pg], b * 16 + kv_full_value(KV_MK + pg))
                    if pg % 2 == 0:
                        dve.wait_ge(N.scored, b * 4 + pg // 2 + 1)
                    tt(prod[:, 512 * (pg % 2):512 * (pg % 2) + 512], kv[:, pg, :], qb[:, DS(b, 1), :].rearrange("p b c -> p (b c)"),
                       ALU.mult).then_inc(kv_free[pg], 1)
                    if pg % 2:
                        dve.wait_ge(kv_free[pg], b + KV_MK // KVS + 2)
                        last = red(sraw_b[:, DS(b, 1), 8 * (pg - 1):8 * (pg + 1)].rearrange("p b c -> p (b c)"),
                                   prod.rearrange("p (h d) -> p h d", d=64), AX, ALU.add)
                        last.then_inc(N.scored, 1)
            dve.wait_ge(N.scored, 33)
            cp(m1[:, 0:1], s_raw[:, 0:1]).then_inc(N.moba_scored, 1)
            dve.wait_ge(N.z_ev, 18)
            head_norms(zsf, sss, S_GROUPS, 8, TS, 1, 2)
            for c0, nh, off in S_GROUPS:
                v = zs[:, c0:c0 + nh * 64].rearrange("p (h d) -> p h d", d=64)
                last = tt(v, v, at(sss[:, off:], (1, nh), (0, 64)), ALU.mult)
            then(last)
            for c0, nh, g in GAINS[1:]:
                v = zs[:, c0:c0 + nh * 64].rearrange("p (h d) -> p h d", d=64)
                last = tt(v, v, at(qkg[0:8, g, :], (0, nh), (1, 64)), ALU.mult)
            last.then_inc(N.zs_normed, 1)
            dve.wait_ge(N.zs_normed, 1)
            tt(pbuf[0:8, 0:512], zs[:, MQ:MQ + 512], zs[:, MK:MK + 512], ALU.mult)
            for i, c0 in enumerate((KSEL, KWIN)):
                last = tt(pbuf[0:8, 512 + 512 * i:1024 + 512 * i].rearrange("p (k g d) -> p k g d", k=2, g=4),
                          zs[:, NQ:NQ + 512].rearrange("p (k g d) -> p k g d", k=2, g=4),
                          at(zs[:, c0:], (64, 2), (0, 4), (1, 64)), ALU.mult)
            then(last)
            then(red(sss[:, 0:24], pbuf[0:8, 0:1536].rearrange("p (h d) -> p h d", d=64), AX, ALU.add))
            stt(out=sss[:, 0:8], in0=sss[:, 0:8], scalar=SCALE, in1=biasO[:, 0:8], op0=ALU.mult, op1=ALU.add)
            then(stt(out=at(sss[:, 8:], (8, 2), (1, 8)), in0=at(sss[:, 8:], (8, 2), (1, 8)), scalar=SCALE,
                     in1=at(biasO[:, 8:], (0, 2), (1, 8)), op0=ALU.mult, op1=ALU.add))
            for br in range(3):
                last = tt(own[:, 64 * br:64 * br + 64].rearrange("p (b h) -> p b h", b=8), at(sss[:, 8 * br:], (0, 8), (1, 8)),
                          cst[0:8, C_OM:C_OM + 64].rearrange("p (b h) -> p b h", b=8), ALU.add)
            then(last)
            head_norms(zf, ss, GROUPS, 0, P, 2, 3)
            for c0, nh, off in GROUPS:
                v = z[:, :, c0:c0 + nh * 64].rearrange("p t (h d) -> p t h d", d=64)
                last = tt(v, v, at(ss[:, off:], (28, 2), (1, nh), (0, 64)), ALU.mult)
            then(last)
            for c0, nh, g in GAINS:
                v = z[:, :, c0:c0 + nh * 64].rearrange("p t (h d) -> p t h d", d=64)
                last = tt(v, v, at(qkg[:, g, :], (0, 2), (0, nh), (1, 64)), ALU.mult)
            last.then_inc(N.z_normed, 1)
            dve.wait_ge(N.small_tr, 2)
            then(tt(gtmp.rearrange("p (h j) -> p h j", j=3), bank[5][0:64, 0:24].rearrange("p (h j) -> p h j", j=3),
                    at(cst[0:64, C_DM:], (1, 8), (0, 3)), ALU.mult))
            red(gcol, at(gtmp, (1, 3), (3, 8)), AX, ALU.add).then_inc(N.small_ev, 1)


            def logits(raw, tiles, first_page, heads):
                return stt(out=s_log[:, 0:64 * tiles].rearrange("p (b c) -> p b c", b=8), in0=raw.rearrange("p (b c) -> p b c", b=8),
                           scalar=SCALE, in1=at(biasP[:, 64 * heads + 8 * first_page:], (0, 8), (1, 8 * tiles)),
                           op0=ALU.mult, op1=ALU.add)

            g4, e4, w4 = prod[:, 0:256], prod[:, 256:512], prod[:, 512:768]
            dve.wait_ge(N.gate_sum, 1)
            then(red(g4, at(bank[0], (16, 32), (1, 8), (8, 2)), AX, ALU.add))
            then(red(m1, at(g4, (32, 8), (1, 8), (8, 4)), AX, ALU.min))
            then(tt(e4.rearrange("p (b n h) -> p b n h", b=8, n=4), g4.rearrange("p (b n h) -> p b n h", b=8, n=4),
                    at(m1, (8, 8), (0, 4), (1, 8)), ALU.is_equal))
            nidx = at(cst[:, C_NI:], (0, 8), (1, 4), (0, 8))
            then(tt(w4.rearrange("p (b n h) -> p b n h", b=8, n=4), e4.rearrange("p (b n h) -> p b n h", b=8, n=4), nidx, ALU.mult))
            then(red(m1, at(w4, (32, 8), (1, 8), (8, 4)), AX, ALU.max))
            then(tt(e4.rearrange("p (b n h) -> p b n h", b=8, n=4), at(m1, (8, 8), (0, 4), (1, 8)), nidx, ALU.is_equal))
            ts(e4, e4, NEG, None, ALU.mult)
            then(logits(s_raw, 8, 0, 0))
            then(tt(at(s_log, (16, 32), (8, 2), (1, 8)), at(s_log, (16, 32), (8, 2), (1, 8)), at(e4, (8, 32), (0, 2), (1, 8)), ALU.add))

            def soft(br, src, tiles, mine):
                if tiles:
                    red(m1, at(src, (8 * tiles, 8), (1, 8), (8, tiles)), AX, ALU.max).then_inc(N.mx_in, 1)
                dve.wait_ge(N.mx_tr, br + 1)
                then(red(mx, bank[2][0:64, 0:P + (8 if mine is not None else 0)], AX, ALU.max))
                ts(diag, ident[0:64, 0:64], mx[:, 0:1], None, ALU.mult).then_inc(N.mx_diag, 1)
                dve.wait_ge(N.mx_bc, br + 1)
                if tiles:
                    v = at(src, (8 * tiles, 8), (8, tiles), (1, 8))
                    tt(v, v, at(bank[3], (8, 8), (0, tiles), (1, 8)), ALU.subtract)
                    tt(mine, mine, bank[3][0:8, 0:64], ALU.subtract).then_inc(N.log_ready, 1)
                else:
                    tt(src, src, bank[3][:, 0:64], ALU.subtract).then_inc(N.log_ready, 1)
                dve.wait_ge(N.p_exp, br + 1)
                if tiles:
                    for half in range(2):
                        last = red(lsum[:, 32 * half:32 * half + 32].rearrange("p (b h) -> p b h", b=4),
                                   at(pbuf[:, 1024 * half:], (264, 4), (1, 8), (32, tiles)), AX, ALU.add)
                    last.then_inc(N.p_ready, 1)
                else:
                    ts(m1[:, 0:1], m1[:, 0:1], 0.0, None, ALU.mult).then_inc(N.p_ready, 1)

            then(nc.vector.memset(pbuf[:, 0:2048], 0.0))
            soft(0, s_log, 8, own[:, 0:64])
            mods_evac(1)
            dve.wait_ge(N.cmp2_mm, 1)
            cp(kvp, bank[4][0:8, 64:320])
            then(cp(kvc, bank[7][:, 0:512]))
            tt(sqf[:, 0:256], kvc[:, 0:256], kvc[:, 0:256], ALU.mult)
            then(tt(sqf[0:8, 256:384], kvp[:, 0:P], kvp[:, 0:P], ALU.mult))
            red(ssc[:, 0:4], sqf[:, 0:256].rearrange("p (h d) -> p h d", d=64), AX, ALU.add)
            then(red(ssc[0:8, 4:6], sqf[0:8, 256:384].rearrange("p (h d) -> p h d", d=64), AX, ALU.add))
            ts(ssc[:, 0:4], ssc[:, 0:4], 1.0 / HD, EPS, ALU.mult, ALU.add)
            ts(ssc[0:8, 4:6], ssc[0:8, 4:6], 1.0 / HD, EPS, ALU.mult, ALU.add).then_inc(N.kc_ss, 1)
            dve.wait_ge(N.kc_std, 1)
            rcp(ssc[:, 0:4], ssc[:, 0:4])
            then(rcp(ssc[0:8, 4:6], ssc[0:8, 4:6]))
            kc4, kp2 = kvc[:, 0:256].rearrange("p (h d) -> p h d", d=64), kvp[:, 0:P].rearrange("p (h d) -> p h d", d=64)
            tt(kc4, kc4, at(ssc, (1, 4), (0, 64)), ALU.mult)
            then(tt(kp2, kp2, at(ssc[0:8, 4:], (1, 2), (0, 64)), ALU.mult))
            tt(kc4, kc4, at(qkg[:, 3, :], (0, 4), (1, 64)), ALU.mult)
            then(tt(kp2, kp2, at(qkg[0:8, 3, :], (0, 2), (1, 64)), ALU.mult))
            cp(kpd.rearrange("p (h r d) -> p h r d", h=2, r=2), at(kvp, (64, 2), (0, 2), (1, 64))).then_inc(N.kdup_ready, 1)
            dve.wait_ge(N.kcp_tr, 1)
            cp(kcTp, bank[4][:, 384:400]).then_inc(N.kcp_ev, 1)
            mods_evac(2)

            dve.wait_ge(N.q_bc, 18)
            for half in range(2):
                last = tt(prod[:, 512 * half:512 * half + 512].rearrange("p (k g d) -> p k g d", k=2, g=4),
                          at(kvc[:, P * half:], (64, 2), (0, 4), (1, 64)),
                          bank[half][:, 0:512].rearrange("p (k g d) -> p k g d", k=2, g=4), ALU.mult)
            last.then_inc(N.cw_made, 1)
            dve.wait_ge(N.cw_made, 1)
            then(red(cw, prod.rearrange("p (h d) -> p h d", d=64), AX, ALU.add))
            then(stt(out=cw.rearrange("p (a h) -> p a h", a=2), in0=cw.rearrange("p (a h) -> p a h", a=2), scalar=SCALE,
                     in1=at(biasC, (0, 2), (1, 8)), op0=ALU.mult, op1=ALU.add))
            then(tt(s_cs.rearrange("p (a b h) -> p a b h", a=2, b=4), at(cw, (8, 2), (0, 4), (1, 8)),
                    at(cst[:, C_AM:], (0, 2), (1, 4), (0, 8)), ALU.add))

            def pair_log(i):
                dve.wait_ge(N.pr_s, i + 1)
                if i >= 2:
                    dve.wait_ge(N.pr_tr, i - 1)
                buf = sps[i % 2].rearrange("p (a c) -> p a c", a=2)
                head, per_row = (2 * i, 256) if i < 4 else (i - 4, 0)
                b2 = lambda n: at(bias[:, head, n - 1:], (per_row, 2), (-1, n))
                stt(out=buf[:, :, P:384], in0=psum[:, 0:2, P:384], scalar=-SCALE, in1=b2(256), op0=ALU.mult, op1=ALU.subtract)
                then(stt(out=buf[:, :, 0:P], in0=psum[:, 0:2, 0:P], scalar=-SCALE, in1=b2(P), op0=ALU.mult, op1=ALU.subtract))
                nm = nmin[:, 4 * (i % 2):4 * (i % 2) + 4]
                red(at(nm, (2, 2)), buf[:, :, 0:P], AX, ALU.min)
                red(at(nm[:, 1:], (2, 2)), buf[:, :, P:384], AX, ALU.min).then_inc(N.pr_log, 1)

            def pair_scale(i):
                dve.wait_ge(N.pr_exp, i + 1)
                w = wrow[:, 4 * (i % 2):4 * (i % 2) + 4]
                then(rcp(w, lrow[:, 4 * (i % 2):4 * (i % 2) + 4]))
                if i >= 4:
                    then(tt(w.rearrange("p (a t) -> p a t", a=2), w.rearrange("p (a t) -> p a t", a=2),
                            at(gates[:, 3 * (i - 4) + 1:], (1, 2), (24, 2)), ALU.mult))
                buf = sps[i % 2].rearrange("p (a c) -> p a c", a=2)
                tt(buf[:, :, 0:P], buf[:, :, 0:P], at(w, (2, 2), (0, P)), ALU.mult)
                tt(buf[:, :, P:384], buf[:, :, P:384], at(w[:, 1:], (2, 2), (0, 256)), ALU.mult).then_inc(N.pr_p, 1)

            def pair_steps(first, end):
                for i in range(first, end + 1):
                    if i > first:
                        pair_scale(i - 1)
                    if i < end:
                        pair_log(i)

            dve.wait_ge(N.bias_back, 16)
            dve.wait_ge(N.z_stored, 16 * 6)
            pair_steps(0, 4)

            def weights(br):
                dve.wait_ge(N.l_done, br + 1)
                dve.wait_ge(N.pv_done, br + 1)
                then(ts(lrec, l_of(br), 1e-30, None, ALU.max))
                then(rcp(lrec, lrec))
                if br:
                    then(tt(lrec, lrec, gcol[:, br - 1:br], ALU.mult))

            def turned(n):
                dve.wait_ge(N.osum_mm, n + 1)
                cp(hT[:, 4 * n:4 * n + 4, TP:T], bank[2][:, 0:32].rearrange("p (c b) -> p c b", c=4)).then_inc(N.oTs_ready, 1)

            weights(0)
            stt(out=oacc.rearrange("p (h d) -> p h d", d=64), in0=bank[5][0:64, 0:512].rearrange("p (h d) -> p h d", d=64),
                scalar=lrec[:, 0:1], in1=at(cst[0:64, C_DM:], (1, 8), (0, 64)), op0=ALU.mult, op1=ALU.mult).then_inc(N.osum_ready, 1)
            turned(0)

            for src, c0 in enumerate((KSEL, KWIN)):
                for t in range(2):
                    last = cp(zdup[:, t, src].rearrange("p h (r d) -> p h r d", r=2), at(z[:, t, c0:], (64, 2), (0, 2), (1, 64)))
            last.then_inc(N.zdup_ready, 1)
            dve.wait_ge(N.cp_mm, 1)
            then(stt(out=s_cp.rearrange("p (a c) -> p a c", a=2), in0=psum[:, 0:2, 0:64], scalar=SCALE,
                     in1=biasCP.rearrange("p (a c) -> p a c", a=2), op0=ALU.mult, op1=ALU.add))
            s3 = s_cp.rearrange("p (i n) -> p i n", n=8)
            then(red(m16, s3, AX, ALU.max))
            then(ts(m16, m16, -1e20, None, ALU.max))
            tt(s3, s3, at(m16, (1, 16), (0, 8)), ALU.subtract).then_inc(N.cp_log, 1)
            dve.wait_ge(N.cp_exp, 1)
            then(red(l16, s3, AX, ALU.add))
            then(ts(l16, l16, 1e-30, None, ALU.max))
            then(rcp(l16, l16))
            then(tt(l16.rearrange("p (a t h) -> p a t h", a=2, t=2), l16.rearrange("p (a t h) -> p a t h", a=2, t=2),
                    at(gates, (3, 2), (24, 2), (6, 4)), ALU.mult))
            tt(s3, s3, at(l16, (1, 16), (0, 8)), ALU.mult).then_inc(N.cp_ready, 1)
            dve.wait_ge(N.q_bc_ev, 16)

            def grouped(dst, slot, g, q):
                return tt(dst.rearrange("p (k g d) -> p k g d", k=2, g=4), at(kv[:, slot, P * g:], (64, 2), (0, 4), (1, 64)),
                          q.rearrange("p (k g d) -> p k g d", k=2, g=4), ALU.mult)

            with dve.Fori(0, 2) as r:
                for u in range(KVS):
                    dve.wait_ge(kv_full[u], r * 64 + kv_full_value(KV_SK + u))
                    q = qb[:, DS(r * 4 + u // 2, 1), :].rearrange("p b c -> p (b c)")
                    dve.wait_ge(N.scored, r * 16 + 2 * u + 33)
                    grouped(prod[:, 0:512], u, 2, q)
                    grouped(prod[:, 512:1024], u, 3, q).then_inc(N.scored, 1)
                    dve.wait_ge(N.scored, r * 16 + 2 * u + 34)
                    c = 32 * (u % 2)
                    into = lambda c: sraw_b[:, DS(r * 4 + u // 2, 1), c:c + 16].rearrange("p b c -> p (b c)")
                    red(into(c + 16), prod.rearrange("p (h d) -> p h d", d=64), AX, ALU.add).then_inc(N.scored, 1)
                    dve.wait_ge(N.pprod_ready, r * 8 + u + 1)
                    red(into(c), pprod.rearrange("p (h d) -> p h d", d=64), AX, ALU.add).then_inc(N.pprod_used, 1)
                    dve.wait_ge(N.pprod_used, r * 8 + u + 2)
                    dve.sem_inc(kv_free[u], 1)
            for b in range(TS):
                dve.wait_ge(kv_full[b], kv_full_value(KV_WK + b))
                dve.wait_ge(N.scored, 2 * b + 65)
                grouped(prod[:, 0:512], b, 2, qb[:, b, :])
                grouped(prod[:, 512:1024], b, 3, qb[:, b, :]).then_inc(N.scored, 1)
                dve.wait_ge(N.scored, 2 * b + 66)
                red(s_win[:, 32 * b + 16:32 * b + 32], prod.rearrange("p (h d) -> p h d", d=64), AX, ALU.add).then_inc(N.scored, 1)
                dve.wait_ge(N.pprod_ready, 17 + b)
                red(s_win[:, 32 * b:32 * b + 16], pprod.rearrange("p (h d) -> p h d", d=64), AX, ALU.add).then_inc(N.pprod_used, 1)
                dve.wait_ge(N.pprod_used, 18 + b)
                dve.sem_inc(kv_free[b], 1)
            dve.wait_ge(N.scored, 81)

            def nsa_out(br):
                weights(br)
                head = otmp[:, 0:P]
                then(ts(head, bank[5][0:64, 0:P], lrec[:, 0:1], None, ALU.mult))
                o3 = (oacc if br == 1 else obr).rearrange("p (k g d) -> p k g d", k=2, g=4)
                then(tt(o3, at(head, (64, 2), (0, 4), (1, 64)), at(cst[0:64, C_DM:], (4, 2), (1, 4), (0, 64)), ALU.mult))
                if br > 1:
                    ins = tt(oacc, oacc, obr, ALU.add)
                    if br == 3:
                        ins.then_inc(N.osum_ready, 1)
                    else:
                        then(ins)

            mods_evac(3)
            ts(m1[:, 0:1], m1[:, 0:1], 0.0, None, ALU.mult).then_inc(N.mx_in, 1)
            soft(1, s_cs, 0, None)
            nsa_out(1)
            then(logits(s_raw, 8, 0, 1))
            soft(2, s_log, 8, own[:, 64:128])
            dve.wait_ge(N.bias_back, 32)
            pair_steps(4, 12)
            nsa_out(2)
            then(logits(s_win, 4, 4, 1))
            soft(3, s_log, 4, own[:, 128:192])
            nsa_out(3)
            turned(1)
            def static_out(n, k, mm_value, src):
                dve.wait_ge(N.mm_done, mm_value)
                add_out(n, src, k, mods[:, n, 16 + k], tmp8x[:, k, :])

            for k in range(KC):
                static_out(0, k, 4 * SEQ["w_out"] + k + 1, bank[k % 4])
            add_samples(0, 8)
            norm(1)

            def squares(layer):
                with dve.Fori(0, 2) as it:
                    for j in range(4):
                        dve.wait_ge(N.relu_ev, it * 16 + 36 * layer + 4 * j + 8)
                        v = actT[:, DS(it * 16 + 4 * j, 4), :]
                        tt(v, v, v, ALU.mult).then_inc(N.act_ready, 1)

            def mlp_out(n, layer):
                with dve.Fori(0, 2) as it:
                    for m in range(4):
                        dve.wait_ge(N.mm_done, it * 16 + 4 * SEQ["w2_%d" % layer] + 8 * (m // 2) + 6 + 2 * (m % 2))
                        src, k = psum[:, m, :], DS(it * 4 + m, 1)
                        stt(out=xT[:, k, 0:TP].rearrange("p k t -> p (k t)"), in0=src[:, 0:TP],
                            scalar=mods[:, n, DS(it * 4 + 16 + m, 1), 0:1].rearrange("p k t -> p (k t)"),
                            in1=xT[:, k, 0:TP].rearrange("p k t -> p (k t)"), op0=ALU.mult, op1=ALU.add)
                        tt(tmp8x[:, k, :].rearrange("p k t -> p (k t)"), src[:, TP:T],
                           mods[:, n, DS(it * 4 + 16 + m, 1), 1:9].rearrange("p k t -> p (k t)"), ALU.mult).then_inc(N.out_free, 1)

            sv = lambda i: st[:, i, :]
            dve.wait_ge(N.s5_rows_loaded, 64)
            cp(s5row[:, 2, :].rearrange("p (j n) -> p j n", j=2), at(s5dt, (1, 2), (0, 64))).then_inc(N.s5_rows_made, 1)
            dve.wait_ge(N.s5_rows_tr, 1)
            cp(st[:, 0:3, :].rearrange("p i q -> p (i q)"), bank[0][:, 0:96])
            cp(h0.rearrange("p b r q -> p (b r q)"), bank[1][:, 0:512]).then_inc(N.s5_rows_ev, 1)
            dve.wait_ge(N.s5_dt, 1)
            tt(sv(4), sv(3), sv(0), ALU.mult)
            then(tt(sv(5), sv(3), sv(1), ALU.mult))
            then(ts(sv(6), sv(5), 0.15915494309189535, ROUND, ALU.mult, ALU.add))
            then(ts(sv(6), sv(6), ROUND, None, ALU.subtract))
            then(stt(out=sv(7), in0=sv(6), scalar=-TWO_PI_A, in1=sv(5), op0=ALU.mult, op1=ALU.add))
            then(stt(out=sv(7), in0=sv(6), scalar=-TWO_PI_B, in1=sv(7), op0=ALU.mult, op1=ALU.add))
            then(stt(out=sv(7), in0=sv(6), scalar=-TWO_PI_C, in1=sv(7), op0=ALU.mult, op1=ALU.add))
            ts(sv(7), sv(7), 3.1415925, -3.1415925, ALU.min, ALU.max).then_inc(N.s5_ang, 1)
            dve.wait_ge(N.s5_sin, 1)
            then(tt(sv(11), sv(10), sv(10), ALU.mult))
            then(ts(sv(11), sv(11), -2.0, 1.0, ALU.mult, ALU.add))
            tt(sv(12), sv(8), sv(11), ALU.mult)
            then(tt(sv(13), sv(8), sv(9), ALU.mult))
            tt(sv(14), sv(0), sv(0), ALU.mult)
            then(tt(sv(17), sv(1), sv(1), ALU.mult))
            then(tt(sv(14), sv(14), sv(17), ALU.add))
            rcp(sv(14), sv(14))
            then(ts(sv(18), sv(12), -1.0, None, ALU.add))
            tt(sv(15), sv(18), sv(0), ALU.mult)
            tt(sv(17), sv(13), sv(1), ALU.mult)
            tt(sv(16), sv(13), sv(0), ALU.mult)
            then(tt(sv(18), sv(18), sv(1), ALU.mult))
            tt(sv(15), sv(15), sv(17), ALU.add)
            then(tt(sv(16), sv(16), sv(18), ALU.subtract))
            tt(sv(15), sv(15), sv(14), ALU.mult)
            then(tt(sv(16), sv(16), sv(14), ALU.mult))
            dve.wait_ge(N.s5_loaded, 16 * (S5_LOADS - 4))
            fre, fim = at(sv(15), (1, 32), (0, 16)), at(sv(16), (1, 32), (0, 16))
            scr = bdia[:, 0].rearrange("p q j c -> p (q j c)")[:, 0:512].rearrange("p (q c) -> p q c", c=16)
            tt(bbar[:, 0], braw[:, 0], fre, ALU.mult)
            tt(bbar[:, 1], braw[:, 1], fre, ALU.mult)
            then(tt(scr, braw[:, 1], fim, ALU.mult))
            then(tt(bbar[:, 0], bbar[:, 0], scr, ALU.subtract))
            then(tt(scr, braw[:, 0], fim, ALU.mult))
            then(tt(bbar[:, 1], bbar[:, 1], scr, ALU.add))
            for r in range(2):
                for j in range(2):
                    last = ts(bdia[:, r, :, j, :], bbar[:, r], cst[:, C_MB + j:C_MB + j + 1], None, ALU.mult)
            last.then_inc(N.s5_bd, 1)
            then(nc.vector.memset(cosT[:, :, 0:1], 1.0))
            then(nc.vector.memset(sinT[:, :, 0:1], 0.0))
            cp(sv(19), sv(11))
            then(cp(sv(20), sv(9)))
            tmpa = BT.rearrange("p k r n -> p (k r n)")
            s, a = 1, 19
            while s <= SEG // 2:
                cs, sn = at(sv(a), (1, NT), (0, s)), at(sv(a + 1), (1, NT), (0, s))
                for q0, qn in (((0, NT),) if s < 64 else ((0, 16), (16, 16))):
                    qs = slice(q0, q0 + qn)
                    x1 = at(tmpa, (s, qn), (1, s))
                    x2 = at(tmpa[:, 1024:], (s, qn), (1, s))
                    csq, snq = at(st[:, a, q0:], (1, qn), (0, s)), at(st[:, a + 1, q0:], (1, qn), (0, s))
                    tt(cosT[:, qs, s:2 * s], cosT[:, qs, 0:s], csq, ALU.mult)
                    tt(sinT[:, qs, s:2 * s], sinT[:, qs, 0:s], csq, ALU.mult)
                    tt(x1, sinT[:, qs, 0:s], snq, ALU.mult)
                    then(tt(x2, cosT[:, qs, 0:s], snq, ALU.mult))
                    tt(cosT[:, qs, s:2 * s], cosT[:, qs, s:2 * s], x1, ALU.subtract)
                    then(tt(sinT[:, qs, s:2 * s], sinT[:, qs, s:2 * s], x2, ALU.add))
                b = 40 - a
                tt(sv(b), sv(a), sv(a), ALU.mult)
                tt(sv(17), sv(a + 1), sv(a + 1), ALU.mult)
                then(tt(sv(b + 1), sv(a), sv(a + 1), ALU.mult))
                tt(sv(b), sv(b), sv(17), ALU.subtract)
                then(ts(sv(b + 1), sv(b + 1), 2.0, None, ALU.mult))
                s, a = 2 * s, b
            jump = a
            ts(sv(23), sv(jump + 1), -1.0, None, ALU.mult).then_inc(N.s5_tables, 1)
            squares(0)
            dve.wait_ge(N.s5_c_tr, 1)
            for r in range(2):
                for hb in range(2):
                    src = bank[4 + 2 * r + hb][:, 0:512].rearrange("p (a c) -> p a c", c=16)
                    mask = at(cst[:, C_MC:], (0, 4), (1, 8), (0, 16))
                    dst = CT[:, 0 if r == 0 else 2, 4 * hb:4 * hb + 4, :]
                    last = tt(dst.rearrange("p k (g c) -> p k g c", c=16), bank[4 + 2 * r + hb][:, 0:512].rearrange("p (k g c) -> p k g c", k=4, g=8), mask, ALU.mult)
            then(last)
            ts(CT[:, 1], CT[:, 0], -1.0, None, ALU.mult)
            ts(CT[:, 2], CT[:, 2], -1.0, None, ALU.mult).then_inc(N.s5_c_ev, 1)
            mlp_out(1, 0)
            add_samples(1, 16)
            norm(2)

            dve.wait_ge(N.hs_ready, 3)
            tt(hm.rearrange("p (k j b) -> p k j b", k=8, j=4), at(hT[:, 0, TP:], (T, 8), (0, 4), (1, 8)),
               at(cst[:, C_JM:], (0, 8), (1, 4), (0, 8)), ALU.mult).then_inc(N.padded_ready, 1)

            def sample_step():
                dve.wait_ge(N.us_mm, 1)
                bq = lambda i: at(sv(i), (0, 8), (1, NT))
                hre, him = h0[:, :, 0, :], h0[:, :, 1, :]
                xre, xim = xs5[:, :, 0, :], xs5[:, :, 1, :]
                ta = t1.rearrange("p (i b q) -> p i b q", i=2, b=8)
                tt(xre, hre, bq(12), ALU.mult)
                tt(xim, him, bq(12), ALU.mult)
                tt(ta[:, 0], him, bq(13), ALU.mult)
                then(tt(ta[:, 1], hre, bq(13), ALU.mult))
                tt(xre, xre, ta[:, 0], ALU.subtract)
                then(tt(xim, xim, ta[:, 1], ALU.add))
                for r, x in ((0, xre), (1, xim)):
                    v = x.rearrange("p b (k e) -> p b k e", e=4)
                    last = tt(v, v, at(bank[4][:, 32 * r:], (1, 8), (64, 8), (8, 4)), ALU.add)
                last.then_inc(N.xs_ready, 1)

            def y_evac(k):
                dve.wait_ge(N.y_mm, 4 * (k + 1))
                stt(out=yT[:, k, 0:TP], in0=hT[:, k, 0:TP], scalar=vT[:, 112 + k:113 + k],
                    in1=bank[4 + k % 2][:, 0:TP], op0=ALU.mult, op1=ALU.add).then_inc(N.y_ev, 1)

            def cmul(dst, src, i):
                re, im, c, s_ = src[:, 0:32], src[:, 32:64], sv(i), sv(i + 1)
                tt(t5s[:, 0:32], re, c, ALU.mult)
                tt(t5s[:, 32:64], im, s_, ALU.mult)
                tt(t5s[:, 64:96], re, s_, ALU.mult)
                then(tt(t5s[:, 96:128], im, c, ALU.mult))
                tt(dst[:, 0:32], t5s[:, 0:32], t5s[:, 32:64], ALU.subtract)
                return tt(dst[:, 32:64], t5s[:, 64:96], t5s[:, 96:128], ALU.add)

            def mark(ins):
                step[0] += 1
                ins.then_inc(N.dve_step, 1)
                return step[0]

            def scans(q, seg):
                for r in range(2):
                    c = TP * r + SEG * seg
                    last = nc.vector.tensor_tensor_scan(
                        out=zcur[:, q % 2, c:c + SEG], data0=st[:, 8, q:q + 1].to_broadcast([P, SEG]), data1=zin[:, q % 2, c:c + SEG],
                        initial=0.0 if seg == 0 else zinit[:, 2 + r:3 + r], op0=ALU.mult, op1=ALU.add)
                return last

            half4 = lambda ap: ap.rearrange("p (s t) -> p s t", t=SEG)
            scanned, summed = None, None
            for q in range(NT + 1):
                if q:
                    z2 = zcur[:, (q - 1) % 2]
                    zr, zi = z2[:, SEG - 1:SEG], z2[:, TP + SEG - 1:TP + SEG]
                    dve.wait_ge(N.dve_step, scanned)
                    part = mark(ts(zinit[:, 0:2], at(zr, (TP, 2)), sv(jump)[:, q - 1:q], None, ALU.mult))
                if q < NT:
                    dve.wait_ge(N.u_mm, q + 1)
                    u = half4(bank[q % 4][:, 0:512])
                    first = mark(tt(half4(t1), u, at(cosT[:, q, :], (0, 4), (1, SEG)), ALU.mult))
                if q:
                    dve.wait_ge(N.dve_step, part)
                    stt(out=zinit[:, 2:3], in0=zi, scalar=sv(23)[:, q - 1:q], in1=zinit[:, 0:1], op0=ALU.mult, op1=ALU.add)
                    turned_on = mark(stt(out=zinit[:, 3:4], in0=zr, scalar=sv(jump + 1)[:, q - 1:q], in1=zinit[:, 1:2],
                                         op0=ALU.mult, op1=ALU.add))
                if q < NT:
                    tt(half4(t2), u, at(sinT[:, q, :], (0, 4), (1, SEG)), ALU.mult).then_inc(N.u_free, 1)
                if q:
                    dve.wait_ge(N.dve_step, turned_on)
                    scans(q - 1, 1).then_inc(N.zc_ready, 1)
                if q < NT:
                    dve.wait_ge(N.dve_step, first)
                    dve.wait_ge(N.u_free, q + 1)
                    tt(zin[:, q % 2, 0:TP], t1[:, 0:TP], t2[:, TP:2 * TP], ALU.add)
                    summed = mark(tt(zin[:, q % 2, TP:2 * TP], t1[:, TP:2 * TP], t2[:, 0:TP], ALU.subtract))
                if q:
                    dve.wait_ge(N.zc_ready, q)
                    cp(at(zlast[:, q - 1:], (32, 2)), at(z2[:, TP - 1:], (TP, 2)))
                if q < NT:
                    dve.wait_ge(N.dve_step, summed)
                    if q >= 2:
                        dve.wait_ge(N.zp_done, 2 * (q - 1))
                    scanned = mark(scans(q, 0))
                if q == 2:
                    sample_step()
                if q == 5:
                    dve.wait_ge(N.ys_mm, 1)
                    ys = yT[:, :, TP:T]
                    then(tt(ys, hT[:, :, TP:T], at(vT[:, 112:], (1, 8), (0, 8)), ALU.mult))
                    tt(ys, ys, bank[6][:, 0:64].rearrange("p (k b) -> p k b", k=8), ALU.add).then_inc(N.y_ev, 1)
                if q >= 6 and (q - 6) % 4 == 0:
                    y_evac((q - 6) // 4)
            cp(sv(19), cosT[:, :, SEG - 1:SEG].rearrange("p q t -> p (q t)"))
            then(cp(sv(20), sinT[:, :, SEG - 1:SEG].rearrange("p q t -> p (q t)")))
            cmul(xlast, zlast, 19).then_inc(N.fin_ready, 1)
            y_evac(7)

            for n in range(8):
                dve.wait_ge(N.sig_ready, n + 1)
                b = 4 * (n // 2 % 2) + 2 * (n % 2)
                then(tt(glu[:, n % 2, :], bank[b][:, 0:T], sig[:, n % 2, :], ALU.mult))
                add_out(2, glu[:, n % 2, :], n, mods[:, 2, 16 + n], tmp8x[:, n, :])
            add_samples(2, 24)
            norm(3)
            squares(1)
            mlp_out(3, 1)
            add_samples(3, 32)


_INS = ["x_prompt", "x_sample", "cache_moba_kv", "cache_nsa_kv", "state_nsa_win", "state_s5", "page_table",
        "c_prompt", "c_sample", "rel_bias", "attn_norm_g", "attn_ada_w", "attn_ada_b", "attn_w_in", "attn_qk_g",
        "nsa_cmp_pos", "nsa_cmp_w1", "nsa_cmp_w2", "attn_w_out", "ssm_norm_g", "ssm_ada_w", "ssm_ada_b",
        "s5_a_re", "s5_a_im", "s5_log_dt", "s5_b_re", "s5_b_im", "s5_c_re", "s5_c_im", "s5_d", "s5_w_glu",
        "mlp_norm_g", "mlp_ada_w", "mlp_ada_b", "mlp_w1", "mlp_w2"]
_OUTS = [("y_prompt", (1, 256, 1024)), ("y_sample", (8, 1, 1024)), ("moba_prompt", (256, 1024)), ("moba_sample", (8, 1024)),
         ("nsa_prompt", (256, 512)), ("nsa_sample", (8, 512)), ("win_prompt", (256, 256)), ("win_sample", (1, 8, 512, 2, 2, 64)),
         ("s5_prompt", (1, 1, 2, 64, 64)), ("s5_sample", (1, 8, 2, 64, 64))]
_SHAPES = [(1, 256, 1024), (8, 1, 1024), (1, 1, 2, 128, 2, 8, 64), (1, 8, 1, 2, 8, 64), (1, 1, 2, 128, 4, 2, 64),
           (1, 8, 1, 4, 2, 64), (1, 1, 256, 2, 2, 64), (1, 8, 512, 2, 2, 64), (1, 1, 2, 64, 64), (1, 8, 2, 64, 64)]


def _bucket(np, dist):
    n = np.maximum(dist, 0)
    large = 16 + (np.log(np.maximum(n, 1) / 16.0) / np.log(8.0) * 16).astype(np.int64)
    return np.where(n < 16, n, np.minimum(large, 31))


def _constants():
    import numpy as np

    def hot(dist, masked):
        out = np.zeros((33, dist.size), np.float32)
        out[_bucket(np, dist), np.arange(dist.size)] = 1.0
        if masked:
            out[:, dist < 0] = 0.0
            out[32, dist < 0] = NEG
        return out

    onehot = np.concatenate([
        hot(np.arange(384) - 127, True),
        hot(PAST - np.arange(PAST), False),
        hot(PAST - (CMP * (np.arange(P) % CMP + 1) - 1), False),
        hot(np.zeros(8, np.int64), False),
        np.concatenate([hot(P * t + np.arange(P) - (CMP * (n + 1) - 1), True) for t in range(2) for n in range(8)], axis=1),
    ], axis=1)
    c = np.zeros((P, C_ALL), np.float32)
    p = np.arange(P)
    c[:, C_ID:C_ID + P] = np.eye(P)
    c[:, C_MB:C_MB + 2] = p[:, None] // 64 == np.arange(2)
    c[:64, C_G:C_G + 8] = p[:64, None] // 8 == np.arange(8)
    c[:64, C_DM:C_DM + 8] = p[:64, None] % 8 == np.arange(8)
    c[:, C_AM:C_AM + 4] = np.where(p[:, None] // 32 == np.arange(4), 0.0, NEG)
    c[:, C_NI:C_NI + 4] = np.arange(4) + 1
    c[:, C_MC:C_MC + 8] = p[:, None] // 64 == np.arange(8) % 2
    c[:8, C_OM:C_OM + 64] = np.where(p[:8, None] == np.arange(64) // 8, 0.0, NEG)
    c[:, C_JM:C_JM + 4] = p[:, None] // 32 == np.arange(4)
    c[:, C_SL:C_SL + 9] = p[:, None] % 32 == np.arange(9)
    c[:8, C_GT:C_GT + 64] = p[:8, None] == np.arange(64) // 8
    return {"c_cst": c, "c_onehot": onehot, "c_one": np.ones((1, 16), np.float32)}


def kernel(**inputs):
    import numpy as np
    import concourse.bacc as bacc
    from concourse.bass_utils import run_bass_kernel_spmd

    nc = bacc.Bacc("TRN2", target_bir_lowering=False, num_devices=1)
    arrays = {"in_" + n: np.ascontiguousarray(inputs[n]) for n in _INS}
    arrays.update({"in_" + n: a for n, a in _constants().items()})
    ins = {n[3:]: nc.dram_tensor(n, a.shape, mybir.dt.from_np(a.dtype), kind="ExternalInput").ap() for n, a in arrays.items()}
    outs = {n: nc.dram_tensor("out_" + n, shape, F32, kind="ExternalOutput").ap() for n, shape in _OUTS}
    program(nc, ins, outs)
    r = run_bass_kernel_spmd(nc, [arrays], core_ids=[0]).results[0]
    return tuple(r["out_" + n].reshape(shape) for (n, _), shape in zip(_OUTS, _SHAPES))
```
